# Optimizing a Trainium2 kernel written in Bass

```python
import jax, jax.numpy as jnp
from jax import lax
import numpy as np

D_MODEL = 1024
BATCH = 1
SEQ = 1024
DEPTH = 1
DEC_BATCH = 8
DEC_SEQ = 8
PAST_LEN = 2048
PAGE_SIZE = 128

CHUNK = 128
G_GROUPS = 4
G_HD = 128
G_WIDTH = G_GROUPS * G_HD
SB_HEADS = 8
SB_HD = 128
SB_WIDTH = SB_HEADS * SB_HD
SB_QBLOCK = 128
SB_SCALE = SB_HD ** -0.5
SB_BIAS_HI = -5.0
SB_BIAS_LO = -9.0
MEM_HEADS = 4
MEM_HD = 128
MEM_WIDTH = MEM_HEADS * MEM_HD
N_MEM = 256
N_BRANCH = 3
IN_WIDTH = 2 * G_WIDTH + 3 * SB_WIDTH + MEM_WIDTH + N_BRANCH * D_MODEL
PEER_HEADS = 8
PEER_DQ = 256
PEER_DH = PEER_DQ // 2
N_KEYS = 128
N_EXPERTS = N_KEYS * N_KEYS
PEER_TOPK = 16
PEER_BLOCK = 128
LN_EPS = 1e-5
DEEPNORM_ALPHA = (2 * DEPTH) ** 0.25
DEEPNORM_BETA = (8 * DEPTH) ** -0.25

kernel_name = "hybrid_gmlp_stickbreak_mem_peer_step"

def layer_norm(x, g, b):
    xf = x.astype(jnp.float32)
    mu = jnp.mean(xf, axis=-1, keepdims=True)
    var = jnp.mean(jnp.square(xf - mu), axis=-1, keepdims=True)
    y = (xf - mu) * lax.rsqrt(var + LN_EPS) * g.astype(jnp.float32) + b.astype(jnp.float32)
    return y.astype(x.dtype)

def in_proj(x, w_in, b_gate, gln_g, gln_b):
    B, T = x.shape[0], x.shape[1]
    h = jnp.einsum('btd,de->bte', x, w_in)
    offs = np.cumsum((G_WIDTH, G_WIDTH, SB_WIDTH, SB_WIDTH, SB_WIDTH, MEM_WIDTH)).tolist()
    hu, hv, hq, hk, hvv, hqm, hg = jnp.split(h, offs, axis=-1)
    u = jax.nn.gelu(hu)
    v = layer_norm(jax.nn.gelu(hv), gln_g, gln_b).reshape(B, T, G_GROUPS, G_HD)
    q = hq.reshape(B, T, SB_HEADS, SB_HD)
    k = hk.reshape(B, T, SB_HEADS, SB_HD)
    vv = hvv.reshape(B, T, SB_HEADS, SB_HD)
    qm = hqm.reshape(B, T, MEM_HEADS, MEM_HD)
    gates = jax.nn.sigmoid(hg.reshape(B, T, N_BRANCH, D_MODEL) + b_gate)
    return u, v, q, k, vv, qm, gates

def spatial_gate(u, v, w_s, b_s):
    B, T = v.shape[0], v.shape[1]
    pad = (-T) % CHUNK
    vp = jnp.pad(v, ((0, 0), (0, pad), (0, 0), (0, 0)))
    nc = (T + pad) // CHUNK
    vc = vp.reshape(B, nc, CHUNK, G_GROUPS, G_HD)
    w = jnp.where(jnp.tril(jnp.ones((CHUNK, CHUNK), dtype=bool)), w_s, 0)
    s = jnp.einsum('gij,bcjgd->bcigd', w, vc) + b_s.T[:, :, None]
    s = s.reshape(B, nc * CHUNK, G_WIDTH)[:, :T]
    return u * s

def sb_attend(q, k, v, q_pos, k_pos, bias):
    z = (jnp.einsum('bqhd,bkhd->bhqk', q, k).astype(jnp.float32) * SB_SCALE
         + bias.astype(jnp.float32)[None, :, None, None])
    causal = k_pos[None, :] < q_pos[:, None]
    log_fail = jnp.where(causal, jax.nn.log_sigmoid(-z), 0.0)
    log_a = z + lax.cumsum(log_fail, axis=3, reverse=True)
    a = jnp.exp(jnp.where(causal, log_a, -jnp.inf))
    return jnp.einsum('bhqk,bkhd->bqhd', a.astype(v.dtype), v)

def sb_prompt(q, k, v, bias):
    B, S = q.shape[0], q.shape[1]
    nb = S // SB_QBLOCK
    qb = q.reshape(B, nb, SB_QBLOCK, SB_HEADS, SB_HD).swapaxes(0, 1)
    qpos = jnp.arange(S, dtype=jnp.int32).reshape(nb, SB_QBLOCK)
    kpos = jnp.arange(S, dtype=jnp.int32)
    ob = lax.map(lambda a: sb_attend(a[0], k, v, a[1], kpos, bias), (qb, qpos))
    return ob.swapaxes(0, 1).reshape(B, S, SB_HEADS, SB_HD)

def sb_sample(q, k_new, v_new, k_past, v_past, bias):
    past, T = k_past.shape[1], q.shape[1]
    k_all = jnp.concatenate([k_past, k_new], axis=1)
    v_all = jnp.concatenate([v_past, v_new], axis=1)
    q_pos = past + jnp.arange(T, dtype=jnp.int32)
    k_pos = jnp.arange(past + T, dtype=jnp.int32)
    return sb_attend(q, k_all, v_all, q_pos, k_pos, bias)

def mem_kv(mem, w_mem_kv):
    B, M = mem.shape[0], mem.shape[1]
    mk, mv = jnp.split(jnp.einsum('bmd,de->bme', mem, w_mem_kv), 2, axis=-1)
    return mk.reshape(B, M, MEM_HEADS, MEM_HD), mv.reshape(B, M, MEM_HEADS, MEM_HD)

def mem_attend(qm, mk, mv):
    s = jnp.einsum('bthd,bmhd->bhtm', qm, mk).astype(jnp.float32) * (MEM_HD ** -0.5)
    p = jax.nn.softmax(s, axis=-1)
    return jnp.einsum('bhtm,bmhd->bthd', p.astype(mv.dtype), mv)

def merge(gates, g_out, sb_out, m_out, w_br_g, w_br_sb, w_br_m, w_out):
    B, T = g_out.shape[0], g_out.shape[1]
    z = (gates[:, :, 0] * (g_out @ w_br_g)
         + gates[:, :, 1] * (sb_out.reshape(B, T, SB_WIDTH) @ w_br_sb)
         + gates[:, :, 2] * (m_out.reshape(B, T, MEM_WIDTH) @ w_br_m))
    return z @ w_out

def peer(x, wq, subkeys, u_tab, v_tab):
    B, T, D = x.shape
    n = B * T
    pad = (-n) % PEER_BLOCK
    xt = jnp.pad(x.reshape(n, D), ((0, pad), (0, 0))).reshape(-1, PEER_BLOCK, D)
    ncand = PEER_TOPK * PEER_TOPK

    def block(xb):
        q = jnp.einsum('td,de->te', xb, wq).reshape(PEER_BLOCK, PEER_HEADS, 2, PEER_DH)
        s = jnp.einsum('thpc,hpnc->thpn', q, subkeys).astype(jnp.float32)
        s1, i1 = lax.top_k(s[:, :, 0], PEER_TOPK)
        s2, i2 = lax.top_k(s[:, :, 1], PEER_TOPK)
        cand = (s1[..., :, None] + s2[..., None, :]).reshape(PEER_BLOCK, PEER_HEADS, ncand)
        cidx = (i1[..., :, None] * N_KEYS + i2[..., None, :]).reshape(PEER_BLOCK, PEER_HEADS, ncand)
        top, sel = lax.top_k(cand, PEER_TOPK)
        idx = jnp.take_along_axis(cidx, sel, axis=-1)
        g = jax.nn.softmax(top, axis=-1)
        hid = jnp.einsum('thkd,td->thk', u_tab[idx], xb).astype(jnp.float32)
        act = (g * jax.nn.gelu(hid)).astype(xb.dtype)
        return jnp.einsum('thk,thkd->td', act, v_tab[idx])

    y = lax.map(block, xt).reshape(-1, D)[:n]
    return y.reshape(B, T, D)

def setup_inputs(seed: int = 0) -> dict:
    key = jax.random.key(seed)
    ks = jax.random.split(key, 32)

    def nrm(k, shape, scale):
        return jax.random.normal(k, shape, jnp.float32) * scale

    n_pages = PAST_LEN // PAGE_SIZE
    n_used = DEC_BATCH * n_pages
    n_phys = n_used + n_used // 4
    page_table = jax.random.permutation(ks[5], n_phys)[:n_used].reshape(DEC_BATCH, n_pages).astype(jnp.int32)
    L = DEPTH
    sb_bias0 = jnp.linspace(SB_BIAS_HI, SB_BIAS_LO, SB_HEADS, dtype=jnp.float32)[None, :]
    return {
        "x_prompt": nrm(ks[0], (BATCH, SEQ, D_MODEL), 1.0),
        "x_sample": nrm(ks[1], (DEC_BATCH, DEC_SEQ, D_MODEL), 1.0),
        "mem_prompt": nrm(ks[2], (BATCH, N_MEM, D_MODEL), 1.0),
        "cache_sb_k": nrm(ks[3], (L, n_phys, PAGE_SIZE, SB_HEADS, SB_HD), 1.0),
        "cache_sb_v": nrm(ks[4], (L, n_phys, PAGE_SIZE, SB_HEADS, SB_HD), 1.0),
        "page_table": page_table,
        "cache_mem_k": nrm(ks[6], (L, DEC_BATCH, N_MEM, MEM_HEADS, MEM_HD), 1.0),
        "cache_mem_v": nrm(ks[7], (L, DEC_BATCH, N_MEM, MEM_HEADS, MEM_HD), 1.0),
        "w_in": nrm(ks[8], (L, D_MODEL, IN_WIDTH), D_MODEL ** -0.5),
        "b_gate": nrm(ks[9], (L, N_BRANCH, D_MODEL), 0.01),
        "gmlp_ln_g": 1.0 + nrm(ks[10], (L, G_WIDTH), 0.01),
        "gmlp_ln_b": nrm(ks[11], (L, G_WIDTH), 0.01),
        "w_spatial": nrm(ks[12], (L, G_GROUPS, CHUNK, CHUNK), CHUNK ** -0.5),
        "b_spatial": 1.0 + nrm(ks[13], (L, G_GROUPS, CHUNK), 0.1),
        "sb_bias": sb_bias0 + nrm(ks[27], (L, SB_HEADS), 0.1),
        "w_mem_kv": nrm(ks[14], (L, D_MODEL, 2 * MEM_WIDTH), D_MODEL ** -0.5),
        "w_br_gmlp": nrm(ks[15], (L, G_WIDTH, D_MODEL), DEEPNORM_BETA * G_WIDTH ** -0.5),
        "w_br_sb": nrm(ks[16], (L, SB_WIDTH, D_MODEL), DEEPNORM_BETA * SB_WIDTH ** -0.5),
        "w_br_mem": nrm(ks[17], (L, MEM_WIDTH, D_MODEL), DEEPNORM_BETA * MEM_WIDTH ** -0.5),
        "w_out": nrm(ks[18], (L, D_MODEL, D_MODEL), DEEPNORM_BETA * D_MODEL ** -0.5),
        "ln1_g": 1.0 + nrm(ks[19], (L, D_MODEL), 0.01),
        "ln1_b": nrm(ks[20], (L, D_MODEL), 0.01),
        "peer_wq": nrm(ks[21], (L, D_MODEL, PEER_HEADS * PEER_DQ), D_MODEL ** -0.5),
        "peer_subkeys": nrm(ks[22], (L, PEER_HEADS, 2, N_KEYS, PEER_DH), PEER_DH ** -0.5),
        "peer_u": nrm(ks[23], (L, N_EXPERTS, D_MODEL), D_MODEL ** -0.5),
        "peer_v": nrm(ks[24], (L, N_EXPERTS, D_MODEL), DEEPNORM_BETA * PEER_HEADS ** -0.5),
        "ln2_g": 1.0 + nrm(ks[25], (L, D_MODEL), 0.01),
        "ln2_b": nrm(ks[26], (L, D_MODEL), 0.01),
    }

def reference(x_prompt, x_sample, mem_prompt, cache_sb_k, cache_sb_v, page_table, cache_mem_k, cache_mem_v,
              w_in, b_gate, gmlp_ln_g, gmlp_ln_b, w_spatial, b_spatial, sb_bias, w_mem_kv, w_br_gmlp, w_br_sb,
              w_br_mem, w_out, ln1_g, ln1_b, peer_wq, peer_subkeys, peer_u, peer_v, ln2_g, ln2_b):
    n_seq = page_table.shape[0]
    x_p, x_s = x_prompt, x_sample
    sbk_p, sbv_p, mk_p, mv_p, sbk_s, sbv_s, gv_s = [], [], [], [], [], [], []
    for l in range(DEPTH):
        u, v, q, k, vv, qm, gates = in_proj(x_p, w_in[l], b_gate[l], gmlp_ln_g[l], gmlp_ln_b[l])
        mk, mv = mem_kv(mem_prompt, w_mem_kv[l])
        mix = merge(gates, spatial_gate(u, v, w_spatial[l], b_spatial[l]), sb_prompt(q, k, vv, sb_bias[l]),
                    mem_attend(qm, mk, mv), w_br_gmlp[l], w_br_sb[l], w_br_mem[l], w_out[l])
        x_p = layer_norm(DEEPNORM_ALPHA * x_p + mix, ln1_g[l], ln1_b[l])
        x_p = layer_norm(DEEPNORM_ALPHA * x_p + peer(x_p, peer_wq[l], peer_subkeys[l], peer_u[l], peer_v[l]),
                         ln2_g[l], ln2_b[l])
        sbk_p.append(k)
        sbv_p.append(vv)
        mk_p.append(mk)
        mv_p.append(mv)
        u, v, q, k, vv, qm, gates = in_proj(x_s, w_in[l], b_gate[l], gmlp_ln_g[l], gmlp_ln_b[l])
        k_past = cache_sb_k[l][page_table].reshape(n_seq, -1, SB_HEADS, SB_HD)
        v_past = cache_sb_v[l][page_table].reshape(n_seq, -1, SB_HEADS, SB_HD)
        mix = merge(gates, spatial_gate(u, v, w_spatial[l], b_spatial[l]),
                    sb_sample(q, k, vv, k_past, v_past, sb_bias[l]),
                    mem_attend(qm, cache_mem_k[l], cache_mem_v[l]), w_br_gmlp[l], w_br_sb[l], w_br_mem[l], w_out[l])
        x_s = layer_norm(DEEPNORM_ALPHA * x_s + mix, ln1_g[l], ln1_b[l])
        x_s = layer_norm(DEEPNORM_ALPHA * x_s + peer(x_s, peer_wq[l], peer_subkeys[l], peer_u[l], peer_v[l]),
                         ln2_g[l], ln2_b[l])
        sbk_s.append(k)
        sbv_s.append(vv)
        gv_s.append(v)
    return (x_p, x_s, jnp.stack(sbk_p), jnp.stack(sbv_p), jnp.stack(mk_p), jnp.stack(mv_p),
            jnp.stack(sbk_s), jnp.stack(sbv_s), jnp.stack(gv_s))


_drawn_inputs = setup_inputs


def setup_inputs(seed=0):
    import zlib

    import numpy as np

    out = dict(_drawn_inputs(seed))
    spreads = {}
    factors = {'cache_sb_k': 22.232,
     'cache_sb_v': 18.454,
     'cache_mem_k': 3.283,
     'cache_mem_v': 2.719,
     'b_gate': 21.674,
     'gmlp_ln_g': 93.954,
     'gmlp_ln_b': 103.092,
     'b_spatial': 4.008,
     'sb_bias': 4.685,
     'w_br_sb': 17.531,
     'w_br_mem': 2.7,
     'ln1_g': 54.524,
     'ln1_b': 60.697,
     'ln2_g': 173.519,
     'ln2_b': 174.03}
    for name, (base, spread) in spreads.items():
        noise = np.random.default_rng([zlib.crc32(name.encode()), seed]).standard_normal(out[name].shape)
        drawn = base * np.exp(spread * noise) if base else spread * noise
        out[name] = __import__('jax').numpy.asarray(drawn.astype(out[name].dtype))
    for name, factor in factors.items():
        out[name] = (out[name] * factor).astype(out[name].dtype)
    return out
```

```python
import numpy as np
from contextlib import ExitStack

import concourse.bass as bass
from concourse import mybir

F32 = mybir.dt.float32
U32 = mybir.dt.uint32
I32 = mybir.dt.int32
ACT = mybir.ActivationFunctionType
ALU = mybir.AluOpType
AX = mybir.AxisListType.X

P = 128
D = 1024
KD = D // P
SEQ = 1024
NSEQ = 8
NQ = 8
PT = SEQ // P
TT = PT + 1
TPAD = TT * P
HEADS = 8
MH = 4
NMEM = 256
GG = 4
PAGES = 16
CHUNK_PAGES = 4
UW = 512
PH = 8
NK = 128
TOPK = 16
NEXP = NK * NK
SB_SCALE = P ** -0.5
MEM_SCALE = P ** -0.5
ALPHA = 2.0 ** 0.25
EPS = 1e-5
NEG = -1e30
CAP = 40.0
PEAK = 8
UNITS = PH * TOPK // PEAK


def apart(eng, unwaited):
    eng.sem_inc(unwaited, 1)


class Steps:

    def __init__(self, sem, names, credit=1):
        self.sem, self.names, self.credit = sem, names, credit
        self.index = {n: i for i, n in enumerate(names)}
        assert len(self.index) == len(names)
        self.last = -1

    def open(self, eng):
        eng.sem_inc(self.sem, self.credit * len(self.names))

    def done(self, ins, name):
        assert self.index[name] == (self.last + 1) % len(self.names), (name, self.last)
        self.last = self.index[name]
        ins.then_inc(self.sem, 1)

    def value(self, item, name):
        return (item + self.credit) * len(self.names) + self.index[name] + 1

    def wait(self, eng, item, name):
        eng.wait_ge(self.sem, self.value(item, name))


class Store:

    def __init__(self, sems):
        self.sems = sems
        self.n = [0] * len(sems)

    def wait_free(self, eng, slot):
        if self.n[slot]:
            eng.wait_ge(self.sems[slot], 16 * self.n[slot])

    def start(self, eng, slot, dst, src):
        eng.dma_start(dst, src).then_inc(self.sems[slot], 16)
        self.n[slot] += 1

    def wait_all(self, eng):
        for slot in range(len(self.sems)):
            self.wait_free(eng, slot)


class Phase:

    def __init__(self, nc, name):
        self.nc, self.name, self.ctx = nc, name, ExitStack()

    def sb(self, name, shape, dt=F32):
        return self.ctx.enter_context(self.nc.sbuf_tensor(f"{self.name}_{name}", shape, dt))

    def ps(self, name, shape, dt=F32):
        return self.ctx.enter_context(self.nc.psum_tensor(f"{self.name}_{name}", shape, dt))



def project(nc, sem, dr, g, tile0, tiles):
    T = tiles * P
    t0 = tile0 * P
    chunks = [(c, min(512, T - c)) for c in range(0, T, 512)]
    ph = Phase(nc, f"pr{g}")
    with ph.ctx:
        xT = ph.sb("xT", [P, KD, T])
        memT = ph.sb("memT", [P, KD, NMEM])
        wbuf = [ph.sb(f"w{i}", [P, KD, UW]) for i in range(2)]
        stage = [ph.sb(f"st{i}", [P, 512]) for i in range(4)]
        bank = [ph.ps(f"b{i}", [P, 512]) for i in range(4)]
        x_loaded = sem("x_loaded")
        w_loaded = [sem(f"w_loaded{i}") for i in range(2)]
        product = sem("product")
        evacuated = sem("evacuated")
        stored = Store([sem(f"stored{i}") for i in range(4)])

        FM, TM = 6, 3
        units = FM + TM + (2 if g == 0 else 0)
        per_fm, per_tm = 4 * len(chunks), tiles
        jobs_after = [per_fm * (u + 1) for u in range(FM)]
        jobs_after += [per_fm * FM + per_tm * (u + 1) for u in range(TM)]
        jobs_after += [jobs_after[-1] + 4, jobs_after[-1] + 6]

        jobs = []
        for u in range(FM):
            for b in range(4):
                for c0, n in chunks:
                    cols = slice(t0 + c0, t0 + c0 + n)
                    blk = 4 * u + b
                    if u == 0:
                        jobs.append((ACT.Gelu_apprx_tanh, 1.0, n, dr["uT"][b, :, cols]))
                    elif u == 1:
                        jobs.append((ACT.Copy, 1.0, n, dr["qmT"][b, :, cols]))
                    elif u < 4:
                        jobs.append((ACT.Copy, SB_SCALE, n, dr["qT"][blk - 8, :, cols]))
                    else:
                        jobs.append((ACT.Copy, 1.0, n, dr["kT"][blk - 16, :, cols]))
        for u in range(TM):
            for t in range(tile0, tile0 + tiles):
                if u == 0:
                    jobs.append((ACT.Gelu_apprx_tanh, 1.0, 512, dr["gv"][t]))
                else:
                    jobs.append((ACT.Copy, 1.0, 512, dr["v"][t, :, (u - 1) * 512:u * 512]))
        if g == 0:
            jobs += [(ACT.Copy, 1.0, NMEM, dr["mkT"][b]) for b in range(4)]
            jobs += [(ACT.Copy, 1.0, 512, dr["mv"][m]) for m in range(2)]

        with nc.Block() as block:
            @block.sync
            def _(sp):
                sp.dma_start(xT[:], dr["xT"][:, :, t0:t0 + T]).then_inc(x_loaded, 16)
                if g == 0:
                    sp.dma_start(memT[:], dr["memT"]).then_inc(x_loaded, 16)
                for u in range(units):
                    if u >= 2:
                        sp.wait_ge(product, jobs_after[u - 2])
                    src = dr["w_in"][u] if u < FM + TM else dr["w_mem"][u - FM - TM]
                    sp.dma_start(wbuf[u % 2][:], src).then_inc(w_loaded[u % 2], 16)

            @block.tensor
            def _(pe):
                def accumulate(job, base, out, lhsT, rhs):
                    pe.wait_ge(evacuated, base + job + 1)
                    for k in range(KD):
                        last = pe.matmul(out, lhsT(k), rhs(k), start=k == 0, stop=k == KD - 1)
                    last.then_inc(product, 1)

                pe.wait_ge(x_loaded, 32 if g == 0 else 16)
                with pe.Fori(0, FM // 2) as i:
                    job = 0
                    for s in range(2):
                        pe.wait_ge(w_loaded[s], 16 * i + 16)
                        for b in range(4):
                            for c0, n in chunks:
                                accumulate(job, 2 * per_fm * i, bank[job % 4][:, 0:n],
                                           lambda k: wbuf[s][:, k, b * P:(b + 1) * P],
                                           lambda k: xT[:, k, c0:c0 + n])
                                job += 1
                job = per_fm * FM
                for u in range(FM, FM + TM):
                    pe.wait_ge(w_loaded[u % 2], 16 * (u // 2 + 1))
                    for t in range(tiles):
                        accumulate(job, 0, bank[job % 4][:], lambda k: xT[:, k, t * P:(t + 1) * P],
                                   lambda k: wbuf[u % 2][:, k, :])
                        job += 1
                if g == 0:
                    pe.wait_ge(w_loaded[9 % 2], 16 * (9 // 2 + 1))
                    for b in range(4):
                        accumulate(job, 0, bank[job % 4][:, 0:NMEM],
                                   lambda k: wbuf[1][:, k, b * P:(b + 1) * P], lambda k: memT[:, k, :])
                        job += 1
                    pe.wait_ge(w_loaded[10 % 2], 16 * (10 // 2 + 1))
                    for m in range(2):
                        accumulate(job, 0, bank[job % 4][:], lambda k: memT[:, k, m * P:(m + 1) * P],
                                   lambda k: wbuf[0][:, k, :])
                        job += 1

            @block.scalar
            def _(act):
                act.sem_inc(evacuated, 4)
                for j, (func, scale, n, dst) in enumerate(jobs):
                    act.wait_ge(product, j + 1)
                    stored.wait_free(act, j % 4)
                    act.activation(stage[j % 4][:, 0:n], bank[j % 4][:, 0:n], func,
                                   scale=scale).then_inc(evacuated, 1)
                    act.wait_ge(evacuated, 4 + j + 1)
                    stored.start(act, j % 4, dst, stage[j % 4][:, 0:n])
                stored.wait_all(act)


def local_branches(nc, sem, dr, g, tile0, tiles):
    ph = Phase(nc, f"lb{g}")
    with ph.ctx:
        ident = ph.sb("ident", [P, P])
        ones = ph.sb("ones", [1, P])
        tril = ph.sb("tril", [P, P])
        ws = ph.sb("ws", [P, 2, GG, P])
        bs = ph.sb("bs", [1, 2, GG, P])
        lng = ph.sb("lng", [P, 512])
        lnb = ph.sb("lnb", [P, 512])
        mkT = ph.sb("mkT", [P, MH, NMEM])
        mv = ph.sb("mv", [P, 2, 512])
        gv = [ph.sb(f"gv{i}", [P, 512]) for i in range(2)]
        uT = [ph.sb(f"uT{i}", [P, GG, P]) for i in range(2)]
        qmT = [ph.sb(f"qmT{i}", [P, MH, P]) for i in range(2)]
        gout = [ph.sb(f"gout{i}", [P, GG, P]) for i in range(2)]
        mout = [ph.sb(f"mout{i}", [P, MH, P]) for i in range(2)]
        stats = ph.sb("stats", [P, 6])
        mean = ph.sb("mean", [P, 2])
        std = ph.sb("std", [P, 2])
        peak = ph.sb("peak", [P, MH])
        npeak = ph.sb("npeak", [P, MH])
        den = ph.sb("den", [P, MH])
        rden = ph.sb("rden", [P, MH])
        prob = ph.sb("prob", [P, MH, NMEM])
        probT = ph.sb("probT", [P, MH, 2, P])
        spat_ps = ph.ps("spat", [P, GG, P])
        score_ps = ph.ps("score", [P, MH, NMEM])
        probT_ps = ph.ps("probT_ps", [P, MH, 2, P])
        mout_ps = ph.ps("mout_ps", [P, MH, P])
        const_loaded = sem("const_loaded")
        tile_loaded = [sem(f"tile_loaded{i}") for i in range(2)]
        masked = sem("masked")
        dve = Steps(sem("dve_steps"), ["stats", "mean", "var", "peak", "npeak", "rstd", "norm", "scaled",
                                       "vnorm", "gout", "rden", "prob"])
        acts = Steps(sem("act_steps"), ["exp", "std", "probT", "mout"])
        pes = Steps(sem("pe_steps"), ["score", "spat", "probT", "mout"])
        gstored = Store([sem(f"gstored{i}") for i in range(2)])
        mstored = Store([sem(f"mstored{i}") for i in range(2)])
        is_prompt = [t < PT for t in range(tile0, tile0 + tiles)]

        with nc.Block() as block:
            @block.sync
            def _(sp):
                for dst, src in ((ident[:], "ident"), (ones[:], "ones"), (tril[:], "tril"), (ws[:], "w_spatial"),
                                 (bs[:], "b_spatial"), (lng[:], "gln_g"), (lnb[:], "gln_b"),
                                 (mkT[:], None), (mv[:], None)):
                    if src:
                        sp.dma_start(dst, dr[src]).then_inc(const_loaded, 16)
                sp.dma_start(mkT[:], dr["mkT"].rearrange("h p m -> p h m")).then_inc(const_loaded, 16)
                sp.dma_start(mv[:], dr["mv"].rearrange("m p c -> p m c")).then_inc(const_loaded, 16)
                for n in range(tiles):
                    t, s = tile0 + n, n % 2
                    if n >= 2:
                        acts.wait(sp, n - 2, "mout")
                        dve.wait(sp, n - 2, "prob")
                    cols = slice(t * P, (t + 1) * P)
                    sp.dma_start(gv[s][:], dr["gv"][t]).then_inc(tile_loaded[s], 16)
                    sp.dma_start(uT[s][:], dr["uT"][:, :, cols].rearrange("b p n -> p b n")).then_inc(tile_loaded[s], 16)
                    sp.dma_start(qmT[s][:], dr["qmT"][:, :, cols].rearrange("b p n -> p b n")).then_inc(tile_loaded[s], 16)

            @block.tensor
            def _(pe):
                pes.open(pe)
                pe.wait_ge(const_loaded, 16 * 9)
                pe.wait_ge(masked, 1)
                for n in range(tiles):
                    s, which = n % 2, 0 if is_prompt[n] else 1
                    pe.wait_ge(tile_loaded[s], 48 * (n // 2 + 1))
                    if n:
                        acts.wait(pe, n - 1, "exp")
                    for h in range(MH):
                        last = pe.matmul(score_ps[:, h, :], qmT[s][:, h, :], mkT[:, h, :], start=True, stop=True)
                    pes.done(last, "score")
                    dve.wait(pe, n, "vnorm")
                    if n:
                        dve.wait(pe, n - 1, "gout")
                    for k in range(GG):
                        pe.matmul(spat_ps[:, k, :], gv[s][:, k * P:(k + 1) * P], ws[:, which, k, :],
                                  start=True, stop=False)
                        last = pe.matmul(spat_ps[:, k, :], ones[:], bs[:, which, k, :], start=False, stop=True)
                    pes.done(last, "spat")
                    dve.wait(pe, n, "prob")
                    for h in range(MH):
                        for m in range(2):
                            last = pe.transpose(probT_ps[:, h, m, :], prob[:, h, m * P:(m + 1) * P], ident[:])
                    pes.done(last, "probT")
                    acts.wait(pe, n, "probT")
                    if n:
                        acts.wait(pe, n - 1, "mout")
                    for h in range(MH):
                        for m in range(2):
                            last = pe.matmul(mout_ps[:, h, :], mv[:, m, h * P:(h + 1) * P], probT[:, h, m, :],
                                             start=m == 0, stop=m == 1)
                    pes.done(last, "mout")

            @block.vector
            def _(v):
                dve.open(v)
                v.wait_ge(const_loaded, 16 * 9)
                v.tensor_tensor(ws[:], ws[:], tril[:].unsqueeze(1).unsqueeze(1).to_broadcast([P, 2, GG, P]),
                                op=ALU.mult).then_inc(masked, 1)
                for n in range(tiles):
                    s = n % 2
                    v.wait_ge(tile_loaded[s], 48 * (n // 2 + 1))
                    if n:
                        dve.wait(v, n - 1, "vnorm")
                    dve.done(v.bn_stats(stats[:], gv[s][:]), "stats")
                    dve.wait(v, n, "stats")
                    dve.done(v.bn_aggr(mean[:], stats[:]), "mean")
                    dve.wait(v, n, "mean")
                    if n:
                        acts.wait(v, n - 1, "std")
                    dve.done(v.tensor_scalar(std[:, 0:1], mean[:, 1:2], EPS, None, ALU.add), "var")
                    pes.wait(v, n, "score")
                    dve.done(v.reduce_max(peak[:], score_ps[:], axis=AX), "peak")
                    dve.wait(v, n, "peak")
                    if n:
                        acts.wait(v, n - 1, "exp")
                    dve.done(v.tensor_scalar(npeak[:], peak[:], -MEM_SCALE, None, ALU.mult), "npeak")
                    acts.wait(v, n, "std")
                    dve.done(v.reciprocal(std[:, 1:2], std[:, 1:2]), "rstd")
                    dve.wait(v, n, "rstd")
                    dve.done(v.tensor_scalar(gv[s][:], gv[s][:], mean[:, 0:1], std[:, 1:2],
                                             ALU.subtract, ALU.mult), "norm")
                    dve.wait(v, n, "norm")
                    dve.done(v.tensor_tensor(gv[s][:], gv[s][:], lng[:], op=ALU.mult), "scaled")
                    dve.wait(v, n, "scaled")
                    dve.done(v.tensor_tensor(gv[s][:], gv[s][:], lnb[:], op=ALU.add), "vnorm")
                    pes.wait(v, n, "spat")
                    gstored.wait_free(v, s)
                    gstored.n[s] += 1
                    dve.done(v.tensor_tensor(gout[s][:], uT[s][:], spat_ps[:], op=ALU.mult), "gout")
                    acts.wait(v, n, "exp")
                    dve.done(v.reciprocal(rden[:], den[:]), "rden")
                    dve.wait(v, n, "rden")
                    dve.done(v.tensor_tensor(prob[:], prob[:], rden[:].unsqueeze(2).to_broadcast([P, MH, NMEM]),
                                             op=ALU.mult), "prob")

            @block.scalar
            def _(act):
                acts.open(act)
                for n in range(tiles):
                    s = n % 2
                    dve.wait(act, n, "npeak")
                    if n:
                        pes.wait(act, n - 1, "probT")
                    for h in range(MH):
                        last = act.activation(prob[:, h, :], score_ps[:, h, :], ACT.Exp, bias=npeak[:, h:h + 1],
                                              scale=MEM_SCALE, accum_out=den[:, h:h + 1])
                    acts.done(last, "exp")
                    acts.done(act.activation(std[:, 1:2], std[:, 0:1], ACT.Sqrt), "std")
                    pes.wait(act, n, "probT")
                    acts.done(act.activation(probT[:], probT_ps[:], ACT.Copy), "probT")
                    pes.wait(act, n, "mout")
                    mstored.wait_free(act, s)
                    acts.done(act.activation(mout[s][:], mout_ps[:], ACT.Copy), "mout")
                    acts.wait(act, n, "mout")
                    t = tile0 + n
                    mstored.start(act, s, dr["mT"][:, :, t * P:(t + 1) * P].rearrange("b p n -> p b n"), mout[s][:])
                mstored.wait_all(act)

            @block.gpsimd
            def _(pool):
                done = [0, 0]
                for n in range(tiles):
                    t, s = tile0 + n, n % 2
                    dve.wait(pool, n, "gout")
                    pool.dma_start(dr["gT"][:, :, t * P:(t + 1) * P].rearrange("b p n -> p b n"),
                                   gout[s][:]).then_inc(gstored.sems[s], 16)
                    done[s] += 1
                    if not is_prompt[n]:
                        pool.dma_start(dr["gv_sample"], gv[s][0:NSEQ * NQ, :]).then_inc(gstored.sems[s], 16)
                        done[s] += 1
                for s in range(2):
                    pool.wait_ge(gstored.sems[s], 16 * done[s])


def attend_prompt(nc, sem, dr, g, tile0, tiles):
    NKEY = (tile0 + tiles) * P
    KT = NKEY // P
    ph = Phase(nc, f"at{g}")
    with ph.ctx:
        ident = ph.sb("ident", [P, P])
        neg = ph.sb("neg", [P, P])
        bias = ph.sb("bias", [P, HEADS])
        one = ph.sb("one", [P, 1])
        bh = ph.sb("bh", [P, 2])
        qh = [ph.sb(f"qh{i}", [P, tiles * P]) for i in range(2)]
        kh = [ph.sb(f"kh{i}", [P, NKEY]) for i in range(2)]
        vh = [ph.sb(f"vh{i}", [P, KT, P]) for i in range(2)]
        soft = [ph.sb(f"soft{i}", [P, NKEY]) for i in range(2)]
        loga = [ph.sb(f"loga{i}", [P, NKEY]) for i in range(2)]
        aT = [ph.sb(f"aT{i}", [P, NKEY]) for i in range(2)]
        oT = [ph.sb(f"oT{i}", [P, tiles * P]) for i in range(2)]
        z = [ph.ps(f"z{i}", [P, 1024]) for i in range(2)]
        aT_ps = [ph.ps(f"aTp{i}", [P, 512]) for i in range(2)]
        o_ps = [ph.ps(f"o{i}", [P, P]) for i in range(2)]
        const_loaded = sem("const_loaded")
        one_set = sem("one_set")
        head_loaded = [sem(f"head_loaded{i}") for i in range(2)]
        bias_set = sem("bias_set")
        scored = sem("scored")
        capped = sem("capped")
        logged = sem("logged")
        softened = sem("softened")
        weighed = sem("weighed")
        turned = sem("turned")
        copied = sem("copied")
        summed = sem("summed")
        kept = sem("kept")
        o_stored = [sem(f"o_stored{i}") for i in range(2)]
        units = [(s, q) for s in range(2) for q in range(tiles)]
        NU = len(units)
        width = [(tile0 + q + 1) * P for _, q in units]
        parts = [[(c, min(512, w - c)) for c in range(0, w, 512)] for w in width]
        bank_no = [sum(len(p) for p in parts[:u]) for u in range(NU + 1)]
        NB = bank_no[NU]

        with nc.Block() as block:
            @block.sync
            def _(sp):
                for dst, src in ((ident[:], "ident"), (neg[:], "neg"), (bias[:], "sb_bias")):
                    sp.dma_start(dst, dr[src]).then_inc(const_loaded, 16)
                with sp.Fori(0, HEADS // 2) as i:
                    for s in range(2):
                        h = 2 * i + s
                        sp.wait_ge(summed, NU * i + (s + 1) * tiles)
                        sp.dma_start(qh[s][:], dr["qT"][bass.ds(h, 1), :, tile0 * P:tile0 * P + tiles * P]
                                     .rearrange("a p n -> p (a n)")).then_inc(head_loaded[s], 16)
                        sp.dma_start(kh[s][:], dr["kT"][bass.ds(h, 1), :, 0:NKEY]
                                     .rearrange("a p n -> p (a n)")).then_inc(head_loaded[s], 16)
                        sp.dma_start(vh[s][:], dr["v"][0:KT, :, bass.ds(h * P, P)]
                                     .rearrange("t p c -> p t c")).then_inc(head_loaded[s], 16)

            @block.tensor
            def _(pe):
                pe.sem_inc(summed, NU)
                pe.sem_inc(turned, 1)
                pe.wait_ge(const_loaded, 48)
                with pe.Fori(0, HEADS // 2) as i:
                    def score(u):
                        s, q = units[u]
                        if q == 0:
                            pe.wait_ge(head_loaded[s], 48 * i + 48)
                        pe.wait_ge(softened, 3 * (NU * i + u) + 3)
                        d0 = width[u] - P
                        for c, n in parts[u]:
                            if c < d0:
                                n = min(n, d0 - c)
                                pe.matmul(z[u % 2][:, c:c + n], qh[s][:, q * P:(q + 1) * P], kh[s][:, c:c + n],
                                          start=True, stop=True)
                        pe.matmul(z[u % 2][:, d0:d0 + P], qh[s][:, q * P:(q + 1) * P], kh[s][:, d0:d0 + P],
                                  start=True, stop=False)
                        last = pe.matmul(z[u % 2][:, d0:d0 + P], ident[:], neg[:], start=False, stop=True)
                        last.then_inc(scored, 1)

                    def turn_and_sum(u):
                        s, q = units[u]
                        pe.wait_ge(weighed, NU * i + u + 1)
                        for j, (c, n) in enumerate(parts[u]):
                            b = bank_no[u] + j
                            pe.wait_ge(copied, NB * i + b + 1)
                            for k in range(c, c + n, P):
                                last = pe.transpose(aT_ps[b % 2][:, k - c:k - c + P], loga[u % 2][:, k:k + P], ident[:])
                            last.then_inc(turned, 1)
                        pe.wait_ge(copied, NB * i + bank_no[u + 1] + 2)
                        pe.wait_ge(kept, NU * i + u + 1)
                        n = width[u] // P
                        for k in range(n):
                            last = pe.matmul(o_ps[u % 2][:], vh[s][:, k, :], aT[u % 2][:, k * P:(k + 1) * P],
                                             start=k == 0, stop=k == n - 1)
                        last.then_inc(summed, 1)

                    score(0)
                    for u in range(NU):
                        if u + 1 < NU:
                            score(u + 1)
                        turn_and_sum(u)

            @block.vector
            def _(v):
                v.memset(one[:], 1.0).then_inc(one_set, 1)
                v.wait_ge(one_set, 1)
                v.wait_ge(const_loaded, 48)
                v.sem_inc(softened, 6)
                with v.Fori(0, HEADS // 2) as i:
                    v.wait_ge(softened, 3 * NU * i + 6)
                    v.tensor_copy(bh[:], bias[:, bass.ds(2 * i, 2)]).then_inc(bias_set, 1)
                    v.wait_ge(bias_set, i + 1)

                    def cap(u):
                        v.wait_ge(scored, NU * i + u + 1)
                        s, w = units[u][0], width[u]
                        v.wait_ge(softened, 3 * (NU * i + u) + 2)
                        v.tensor_scalar(soft[u % 2][:, 0:w], z[u % 2][:, 0:w], bh[:, s:s + 1], CAP,
                                        ALU.add, ALU.min).then_inc(capped, 1)

                    def suffix(u):
                        s, w = units[u][0], width[u]
                        sf, lg = soft[u % 2], loga[u % 2]
                        base = 3 * (NU * i + u) + 6
                        v.wait_ge(logged, 2 * (NU * i + u) + 2)
                        v.scalar_tensor_tensor(out=sf[:, 0:w], in0=z[u % 2][:, 0:w], scalar=bh[:, s:s + 1],
                                               in1=sf[:, 0:w], op0=ALU.add, op1=ALU.max).then_inc(softened, 1)
                        v.wait_ge(softened, base + 1)
                        v.wait_ge(turned, NB * i + (bank_no[u - 1] if u >= 2 else 0) + 1)
                        v.tensor_tensor_scan(out=lg[:, 0:w][:, ::-1], data0=one[:].to_broadcast([P, w]),
                                             data1=sf[:, 0:w][:, ::-1], initial=0.0, op0=ALU.mult,
                                             op1=ALU.add).then_inc(softened, 1)
                        v.wait_ge(softened, base + 2)
                        v.scalar_tensor_tensor(out=lg[:, 0:w], in0=z[u % 2][:, 0:w], scalar=bh[:, s:s + 1],
                                               in1=lg[:, 0:w], op0=ALU.add, op1=ALU.subtract).then_inc(softened, 1)

                    cap(0)
                    for u in range(NU):
                        if u + 1 < NU:
                            cap(u + 1)
                        suffix(u)

            @block.scalar
            def _(act):
                act.sem_inc(copied, 2)
                act.sem_inc(kept, 2)
                with act.Fori(0, HEADS // 2) as i:
                    def soften(u):
                        w = width[u]
                        sf = soft[u % 2]
                        act.wait_ge(capped, NU * i + u + 1)
                        act.activation(sf[:, 0:w], sf[:, 0:w], ACT.Exp).then_inc(logged, 1)
                        act.wait_ge(logged, 2 * (NU * i + u) + 1)
                        act.activation(sf[:, 0:w], sf[:, 0:w], ACT.Ln, bias=1.0).then_inc(logged, 1)

                    def weigh(u):
                        w = width[u]
                        act.wait_ge(softened, 3 * (NU * i + u) + 9)
                        act.activation(loga[u % 2][:, 0:w], loga[u % 2][:, 0:w], ACT.Exp).then_inc(weighed, 1)

                    def gather(u):
                        s, q = units[u]
                        act.wait_ge(summed, NU * i + NU + u - 1)
                        for j, (c, n) in enumerate(parts[u]):
                            b = bank_no[u] + j
                            act.wait_ge(turned, NB * i + b + 2)
                            act.activation(aT[u % 2][:, c:c + n], aT_ps[b % 2][:, 0:n], ACT.Copy).then_inc(copied, 1)
                        act.wait_ge(summed, NU * i + NU + u + 1)
                        act.activation(oT[s][:, q * P:(q + 1) * P], o_ps[u % 2][:], ACT.Copy).then_inc(kept, 1)
                        if q == tiles - 1:
                            act.wait_ge(kept, NU * i + u + 3)
                            act.dma_start(dr["sbT"][bass.ds(2 * i + s, 1), :, tile0 * P:(tile0 + tiles) * P]
                                          .rearrange("a p n -> p (a n)"), oT[s][:]).then_inc(o_stored[s], 16)

                    soften(0)
                    for u in range(NU):
                        if u + 1 < NU:
                            soften(u + 1)
                        weigh(u)
                        gather(u)
                    for s in range(2):
                        act.wait_ge(o_stored[s], 16 * i + 16)


def layer_norm_steps(prefix):
    return [prefix + x for x in ("stats", "mean", "var", "rstd", "norm", "scaled", "out")]


def layer_norm(v, dve, acts, n, prefix, x, out, stats, mean, std, gain, offset, unwaited):
    v.bn_stats(stats[:, 0:6], x[:, 0:512])
    dve.done(v.bn_stats(stats[:, 6:12], x[:, 512:1024]), prefix + "stats")
    dve.wait(v, n, prefix + "stats")
    apart(v, unwaited)
    dve.done(v.bn_aggr(mean[:], stats[:]), prefix + "mean")
    dve.wait(v, n, prefix + "mean")
    if not isinstance(n, int) or n:
        acts.wait(v, n - 1, prefix + "root")
    dve.done(v.tensor_scalar(std[:, 0:1], mean[:, 1:2], EPS, None, ALU.add), prefix + "var")
    acts.wait(v, n, prefix + "root")
    dve.done(v.reciprocal(std[:, 1:2], std[:, 1:2]), prefix + "rstd")
    dve.wait(v, n, prefix + "rstd")
    dve.done(v.tensor_scalar(out, x, mean[:, 0:1], std[:, 1:2], ALU.subtract, ALU.mult), prefix + "norm")
    dve.wait(v, n, prefix + "norm")
    dve.done(v.tensor_tensor(out, out, gain[:], op=ALU.mult), prefix + "scaled")
    dve.wait(v, n, prefix + "scaled")
    dve.done(v.tensor_tensor(out, out, offset[:], op=ALU.add), prefix + "out")


def merge(nc, sem, dr, g, tile0, tiles):
    T = tiles * P
    t0 = tile0 * P
    chunks = [(c, min(512, T - c)) for c in range(0, T, 512)]
    NC = len(chunks)
    ph = Phase(nc, f"mg{g}")
    with ph.ctx:
        ident = ph.sb("ident", [P, P])
        bgate = ph.sb("bgate", [P, 24])
        lng = ph.sb("lng", [P, D])
        lnb = ph.sb("lnb", [P, D])
        keysT = ph.sb("keysT", [P, 2 * PH, NK])
        xT = ph.sb("xT", [P, KD, T])
        brT = ph.sb("brT", [P, 16, T])
        zT = ph.sb("zT", [P, KD, T])
        wbuf = [ph.sb(f"w{i}", [P, KD, UW]) for i in range(4)]
        x1 = ph.sb("x1", [P, tiles, D])
        gate = [ph.sb(f"gate{i}", [P, 512]) for i in range(2)]
        term = ph.sb("term", [P, 512])
        stats = ph.sb("stats", [P, 12])
        mean = ph.sb("mean", [P, 2])
        std = ph.sb("std", [P, 2])
        bank = [ph.ps(f"b{i}", [P, 512]) for i in range(4)]
        score_ps = ph.ps("score", [P, 2 * PH, NK])
        gate_ps, branch_ps = bank[0:2], bank[2:4]
        const_loaded = sem("const_loaded")
        act_loaded = sem("act_loaded")
        x_loaded = sem("x_loaded")
        w_loaded = [sem(f"w_loaded{i}") for i in range(4)]
        gate_ready, gate_done = sem("gate_ready"), sem("gate_done")
        branch_ready, branch_done = sem("branch_ready"), sem("branch_done")
        mix_ready, mix_done = sem("mix_ready"), sem("mix_done")
        turned, turn_kept = sem("turned"), sem("turn_kept")
        query_ready, query_kept = sem("query_ready"), sem("query_kept")
        scored, score_kept = sem("scored"), sem("score_kept")
        term_done = sem("term_done")
        dve = Steps(sem("ln_dve"), layer_norm_steps(""))
        acts = Steps(sem("ln_act"), ["root"])
        x1_stored = sem("x1_stored")
        s_stored = Store([sem(f"s_stored{i}") for i in range(2)])
        pairs = [(hf, b) for hf in range(2) for b in range(3)]
        KB = {0: GG, 1: HEADS, 2: MH}
        KOFF = {0: 0, 1: GG, 2: GG + HEADS}
        srcs = []
        for hf, b in pairs:
            srcs.append((dr["w_in"][9 + 2 * b + hf], KD))
            srcs.append((dr[f"w_br{b}"][hf], KB[b]))
        srcs += [(dr["w_out"][c], KD) for c in range(2)] + [(dr["w_q"][c], KD) for c in range(4)]
        jobs = [(p, mf, c) for p in range(6) for mf in range(4) for c in range(NC)]
        per_pair = 4 * NC
        NZ = len(jobs)
        qjobs = [(u, b, c) for u in range(4) for b in range(4) for c in range(NC)]

        def keep_turned(act, n):
            for hf in range(2):
                act.wait_ge(turned, 2 * n + hf + 1)
                act.activation(xT[:, 4 * hf:4 * hf + 4, n * P:(n + 1) * P],
                               bank[2 + hf][:].rearrange("p (k n) -> p k n", k=4), ACT.Copy).then_inc(turn_kept, 1)

        with nc.Block() as block:
            @block.sync
            def _(sp):
                cols = slice(t0, t0 + T)
                for dst, src in ((ident[:], "ident"), (bgate[:], "b_gate"), (lng[:], "ln1_g"), (lnb[:], "ln1_b"),
                                 (keysT[:], "keysT")):
                    sp.dma_start(dst, dr[src]).then_inc(const_loaded, 16)
                sp.dma_start(xT[:], dr["xT"][:, :, cols]).then_inc(act_loaded, 16)

                def load(u):
                    src, k = srcs[u]
                    sp.dma_start(wbuf[u % 4][:, 0:k, :], src).then_inc(w_loaded[u % 4], 16)

                load(0)
                sp.dma_start(brT[:, 0:GG, :], dr["gT"][:, :, cols].rearrange("b p n -> p b n")).then_inc(act_loaded, 16)
                load(1)
                sp.dma_start(brT[:, GG:GG + HEADS, :], dr["sbT"][:, :, cols].rearrange("b p n -> p b n")).then_inc(act_loaded, 16)
                sp.dma_start(brT[:, GG + HEADS:, :], dr["mT"][:, :, cols].rearrange("b p n -> p b n")).then_inc(act_loaded, 16)
                load(2)
                load(3)
                sp.dma_start(x1[:], dr["x"][tile0:tile0 + tiles].rearrange("t p c -> p t c")).then_inc(x_loaded, 16)
                for u in range(4, len(srcs)):
                    v = u - 4
                    if v < 12:
                        sp.wait_ge(branch_ready, per_pair * (v // 2 + 1))
                    elif v < 14:
                        sp.wait_ge(mix_ready, tiles * (v - 11))
                    load(u)

            @block.tensor
            def _(pe):
                pe.wait_ge(act_loaded, 64)
                for j, (p, mf, c) in enumerate(jobs):
                    b = pairs[p][1]
                    c0, n = chunks[c]
                    ug, ub = 2 * p, 2 * p + 1
                    if mf == 0 and c == 0:
                        pe.wait_ge(w_loaded[ug % 4], 16 * (ug // 4 + 1))
                        pe.wait_ge(w_loaded[ub % 4], 16 * (ub // 4 + 1))
                    if j >= 2:
                        pe.wait_ge(gate_done, j - 1)
                    for k in range(KD):
                        last = pe.matmul(gate_ps[j % 2][:, 0:n], wbuf[ug % 4][:, k, mf * P:(mf + 1) * P],
                                         xT[:, k, c0:c0 + n], start=k == 0, stop=k == KD - 1)
                    last.then_inc(gate_ready, 1)
                    if j >= 2:
                        pe.wait_ge(branch_done, j - 1)
                    for k in range(KB[b]):
                        last = pe.matmul(branch_ps[j % 2][:, 0:n], wbuf[ub % 4][:, k, mf * P:(mf + 1) * P],
                                         brT[:, KOFF[b] + k, c0:c0 + n], start=k == 0, stop=k == KB[b] - 1)
                    last.then_inc(branch_ready, 1)
                pe.wait_ge(branch_done, NZ)
                for c in range(2):
                    u = 12 + c
                    pe.wait_ge(w_loaded[u % 4], 16 * (u // 4 + 1))
                    for n in range(tiles):
                        j = c * tiles + n
                        if j >= 2:
                            pe.wait_ge(mix_done, j - 1)
                        for k in range(KD):
                            last = pe.matmul(bank[j % 2][:], zT[:, k, n * P:(n + 1) * P], wbuf[u % 4][:, k, :],
                                             start=k == 0, stop=k == KD - 1)
                        last.then_inc(mix_ready, 1)
                pe.wait_ge(const_loaded, 80)
                for n in range(tiles):
                    dve.wait(pe, n, "out")
                    for hf in range(2):
                        j = 2 * n + hf
                        if j >= 2:
                            pe.wait_ge(turn_kept, j - 1)
                        for k in range(4):
                            kk = 4 * hf + k
                            last = pe.transpose(bank[2 + hf][:, k * P:(k + 1) * P], x1[:, n, kk * P:(kk + 1) * P], ident[:])
                        last.then_inc(turned, 1)
                pe.wait_ge(turn_kept, 2 * tiles)
                for j, (u, b, c) in enumerate(qjobs):
                    c0, n = chunks[c]
                    w = 14 + u
                    if b == 0 and c == 0:
                        pe.wait_ge(w_loaded[w % 4], 16 * (w // 4 + 1))
                    if j >= 4:
                        pe.wait_ge(query_kept, j - 3)
                    for k in range(KD):
                        last = pe.matmul(bank[j % 4][:, 0:n], wbuf[w % 4][:, k, b * P:(b + 1) * P],
                                         xT[:, k, c0:c0 + n], start=k == 0, stop=k == KD - 1)
                    last.then_inc(query_ready, 1)
                pe.wait_ge(query_kept, len(qjobs))
                for n in range(tiles):
                    if n:
                        pe.wait_ge(score_kept, n)
                    for hp in range(2 * PH):
                        last = pe.matmul(score_ps[:, hp, :], brT[:, hp, n * P:(n + 1) * P], keysT[:, hp, :],
                                         start=True, stop=True)
                    last.then_inc(scored, 1)

            @block.scalar
            def _(act):
                act.wait_ge(const_loaded, 80)
                acts.open(act)
                for j, (p, mf, c) in enumerate(jobs):
                    hf, b = pairs[p]
                    n = chunks[c][1]
                    col = b * KD + hf * 4 + mf
                    act.wait_ge(gate_ready, j + 1)
                    if j >= 2:
                        act.wait_ge(branch_done, j - 1)
                    act.activation(gate[j % 2][:, 0:n], gate_ps[j % 2][:, 0:n], ACT.Sigmoid,
                                   bias=bgate[:, col:col + 1]).then_inc(gate_done, 1)
                for n in range(tiles):
                    dve.wait(act, n, "var")
                    acts.done(act.activation(std[:, 1:2], std[:, 0:1], ACT.Sqrt), "root")
                    if n:
                        keep_turned(act, n - 1)
                keep_turned(act, tiles - 1)
                for j, (u, b, c) in enumerate(qjobs):
                    c0, n = chunks[c]
                    act.wait_ge(query_ready, j + 1)
                    act.activation(brT[:, 4 * u + b, c0:c0 + n], bank[j % 4][:, 0:n], ACT.Copy).then_inc(query_kept, 1)
                for n in range(tiles):
                    act.wait_ge(scored, n + 1)
                    s_stored.wait_free(act, n % 2)
                    out = zT[:, 4 * (n % 2):4 * (n % 2) + 4, 0:512]
                    act.activation(out, score_ps[:].rearrange("p (a b) n -> p a (b n)", a=4), ACT.Copy)\
                        .then_inc(score_kept, 1)
                    act.wait_ge(score_kept, n + 1)
                    s_stored.start(act, n % 2, dr["scores"][tile0 + n].rearrange("p (a n) -> p a n", a=4), out)
                s_stored.wait_all(act)

            @block.vector
            def _(v):
                dve.open(v)
                for j, (p, mf, c) in enumerate(jobs):
                    hf, b = pairs[p]
                    c0, n = chunks[c]
                    dst = zT[:, 4 * hf + mf, c0:c0 + n]
                    v.wait_ge(gate_done, j + 1)
                    v.wait_ge(branch_ready, j + 1)
                    if b == 0:
                        v.tensor_tensor(dst, gate[j % 2][:, 0:n], branch_ps[j % 2][:, 0:n], op=ALU.mult)\
                            .then_inc(branch_done, 1)
                        continue
                    v.wait_ge(branch_done, j)
                    v.tensor_tensor(term[:, 0:n], gate[j % 2][:, 0:n], branch_ps[j % 2][:, 0:n], op=ALU.mult)\
                        .then_inc(term_done, 1)
                    v.wait_ge(term_done, NC * 4 * (2 * hf + b - 1) + mf * NC + c + 1)
                    v.tensor_tensor(dst, dst, term[:, 0:n], op=ALU.add).then_inc(branch_done, 1)
                v.wait_ge(x_loaded, 16)
                v.wait_ge(const_loaded, 80)
                for c in range(2):
                    for n in range(tiles):
                        j = c * tiles + n
                        v.wait_ge(mix_ready, j + 1)
                        dst = x1[:, n, c * 512:(c + 1) * 512]
                        v.scalar_tensor_tensor(out=dst, in0=dst, scalar=ALPHA, in1=bank[j % 2][:], op0=ALU.mult,
                                               op1=ALU.add).then_inc(mix_done, 1)
                        if c == 1:
                            v.wait_ge(mix_done, j + 1)
                            layer_norm(v, dve, acts, n, "", x1[:, n, :], x1[:, n, :], stats, mean, std, lng, lnb, dr["unwaited"])

            @block.gpsimd
            def _(pool):
                for n in range(tiles):
                    dve.wait(pool, n, "out")
                    pool.dma_start(dr["x1"][tile0 + n], x1[:, n, :]).then_inc(x1_stored, 16)
                pool.wait_ge(x1_stored, 16 * tiles)


def attend_sample(nc, sem, dr):
    R = HEADS * NQ
    MR = MH * NQ
    CW = CHUNK_PAGES * P
    NCH = PAGES // CHUNK_PAGES
    ph = Phase(nc, "sa")
    with ph.ctx:
        ident = ph.sb("ident", [P, P])
        sel = ph.sb("sel", [R, HEADS, R])
        selm = ph.sb("selm", [MR, MH, MR])
        negn = ph.sb("negn", [R, NQ])
        bias = ph.sb("bias", [R, 1])
        one = ph.sb("one", [P, 1])
        table = ph.sb("table", [1, NSEQ * PAGES], I32)
        q = ph.sb("q", [P, HEADS, R])
        kn = ph.sb("kn", [P, HEADS, R])
        qm = ph.sb("qm", [P, MH, R])
        qpad = ph.sb("qpad", [P, HEADS * (R + NQ)])
        qmpad = ph.sb("qmpad", [P, MH * (MR + NQ)])
        vn = ph.sb("vn", [NQ, HEADS * P])
        mk = ph.sb("mk", [P, MH, NMEM])
        mv = ph.sb("mv", [P, 2, 512])
        kc = [ph.sb(f"kc{i}", [P, CHUNK_PAGES, HEADS * P]) for i in range(2)]
        vc = [ph.sb(f"vc{i}", [P, CHUNK_PAGES, HEADS * P]) for i in range(2)]
        soft = [ph.sb(f"soft{i}", [R, CW]) for i in range(2)]
        loga = [ph.sb(f"loga{i}", [R, CW]) for i in range(2)]
        first = [ph.sb(f"first{i}", [R, 1]) for i in range(2)]
        aT = [ph.sb(f"aT{i}", [P, CHUNK_PAGES * R]) for i in range(2)]
        osb = ph.sb("osb", [R, HEADS * P])
        so = ph.sb("so", [P, HEADS, P])
        smo = ph.sb("smo", [P, MH, P])
        prob = ph.sb("prob", [MR, NMEM])
        probT = ph.sb("probT", [P, 2, MR])
        om = ph.sb("om", [MR, 512])
        peak = ph.sb("peak", [MR, 1])
        npeak = ph.sb("npeak", [MR, 1])
        den = ph.sb("den", [MR, 1])
        rden = ph.sb("rden", [MR, 1])
        z = [ph.ps(f"z{i}", [R, CW]) for i in range(2)]
        aT_ps = [ph.ps(f"aTp{i}", [P, CHUNK_PAGES * R]) for i in range(2)]
        o_ps = ph.ps("o", [R, HEADS * P])
        fin_ps = ph.ps("fin", [P, 512])
        m_ps = ph.ps("m", [P, 512])
        const_loaded = sem("const_loaded")
        cleared = sem("cleared")
        mem_loaded = sem("mem_loaded")
        vn_loaded = sem("vn_loaded")
        k_loaded = [sem(f"k_loaded{i}") for i in range(2)]
        v_loaded = [sem(f"v_loaded{i}") for i in range(2)]
        o_stored = sem("o_stored")
        blocks = ["n"] + [str(c) for c in range(NCH)]
        dve = Steps(sem("dve_steps"), ["pads", "peak", "npeak", "rden", "prob"] +
                    [f"{b}_{x}" for b in blocks for x in ("cap", "sp", "cum", "first", "log")])
        acts = Steps(sem("act_steps"), ["mexp", "mprobT", "mom", "mout"] +
                     [f"{b}_{x}" for b in blocks for x in ("exp", "ln", "a", "aT")] + ["osb", "out"])
        pes = Steps(sem("pe_steps"), ["mscore", "mprobT", "mom", "mout", "n_z"] +
                    [x for c in range(NCH) for x in (f"{c}_z", f"{blocks[c]}_aT", f"{blocks[c]}_o")] +
                    [f"{NCH - 1}_aT", f"{NCH - 1}_o", "out"])

        with nc.Block() as block:
            @block.sync
            def _(sp):
                c0 = PT * P
                for dst, src in ((ident[:], dr["ident"]), (sel[:], dr["sel"]), (selm[:], dr["selm"]),
                                 (negn[:], dr["neg_new"]), (bias[:], dr["sb_bias_rows"]), (table[:], dr["table"]),
                                 (q[:], dr["qT"][:, :, c0:c0 + R].rearrange("h p n -> p h n")),
                                 (kn[:], dr["kT"][:, :, c0:c0 + R].rearrange("h p n -> p h n")),
                                 (qm[:], dr["qmT"][:, :, c0:c0 + R].rearrange("h p n -> p h n"))):
                    sp.dma_start(dst, src).then_inc(const_loaded, 16)
                sp.wait_ge(const_loaded, 16 * 9)
                with sp.Fori(0, NSEQ) as i:
                    acts.wait(sp, i - 1, "mout")
                    sp.dma_start(mk[:], dr["mem_k"][bass.ds(i, 1)].rearrange("a p h m -> p (a h) m")).then_inc(mem_loaded, 16)
                    sp.dma_start(mv[:], dr["mem_v"][bass.ds(i, 1)].rearrange("a p m c -> p (a m) c")).then_inc(mem_loaded, 16)
                    pes.wait(sp, i - 1, "n_o")
                    sp.dma_start(vn[:], dr["v"][PT, bass.ds(i * NQ, NQ), :]).then_inc(vn_loaded, 16)
                    for c in range(NCH):
                        s = c % 2
                        before = (i, c - 2) if c >= 2 else (i - 1, c + NCH - 2)
                        pes.wait(sp, before[0], f"{before[1]}_z")
                        apart(sp, dr["unwaited"])
                        for k in range(CHUNK_PAGES):
                            page = PAGES - CHUNK_PAGES * (c + 1) + k
                            reg = sp.value_load(table[0:1, bass.ds(i * PAGES + page, 1)], min_val=0,
                                                max_val=dr["cache_k"].shape[0] - 1)
                            sp.dma_start(kc[s][:, k, :], dr["cache_k"][bass.ds(reg, 1)]
                                         .rearrange("a p c -> p (a c)")).then_inc(k_loaded[s], 16)
                        pes.wait(sp, before[0], f"{before[1]}_o")
                        apart(sp, dr["unwaited"])
                        for k in range(CHUNK_PAGES):
                            page = PAGES - CHUNK_PAGES * (c + 1) + k
                            reg = sp.value_load(table[0:1, bass.ds(i * PAGES + page, 1)], min_val=0,
                                                max_val=dr["cache_v"].shape[0] - 1)
                            sp.dma_start(vc[s][:, k, :], dr["cache_v"][bass.ds(reg, 1)]
                                         .rearrange("a p c -> p (a c)")).then_inc(v_loaded[s], 16)

            @block.tensor
            def _(pe):
                pe.wait_ge(const_loaded, 16 * 9)
                pes.open(pe)
                with pe.Fori(0, NSEQ) as i:
                    dve.wait(pe, i, "pads")
                    pe.wait_ge(mem_loaded, 32 * i + 32)
                    for h in range(MH):
                        last = pe.matmul(m_ps[0:MR, 0:NMEM], qmpad[:, h * MR:(h + 1) * MR], mk[:, h, :],
                                         start=h == 0, stop=h == MH - 1)
                    pes.done(last, "mscore")
                    dve.wait(pe, i, "prob")
                    apart(pe, dr["unwaited"])
                    for m in range(2):
                        last = pe.transpose(m_ps[:, m * MR:(m + 1) * MR], prob[:, m * P:(m + 1) * P], ident[0:MR, 0:MR])
                    pes.done(last, "mprobT")
                    acts.wait(pe, i, "mprobT")
                    for m in range(2):
                        last = pe.matmul(m_ps[0:MR, :], probT[:, m, :], mv[:, m, :], start=m == 0, stop=m == 1)
                    pes.done(last, "mom")
                    acts.wait(pe, i, "mom")
                    for h in range(MH):
                        last = pe.matmul(m_ps[:, 0:MR], om[:, h * P:(h + 1) * P], selm[:, h, :],
                                         start=h == 0, stop=h == MH - 1)
                    pes.done(last, "mout")

                    for h in range(HEADS):
                        pe.matmul(fin_ps[0:R, 0:NQ], qpad[:, h * R:(h + 1) * R], kn[:, h, bass.ds(i * NQ, NQ)],
                                  start=h == 0, stop=False)
                    pes.done(pe.matmul(fin_ps[0:R, 0:NQ], ident[0:R, 0:R], negn[:], start=False, stop=True), "n_z")

                    def turn_and_sum(b):
                        acts.wait(pe, i, f"{b}_a")
                        apart(pe, dr["unwaited"])
                        if b == "n":
                            last = pe.transpose(aT_ps[1][0:NQ, 0:R], loga[1][:, 0:NQ], ident[0:R, 0:R])
                            pes.done(last, "n_aT")
                            acts.wait(pe, i, "n_aT")
                            pe.wait_ge(vn_loaded, 16 * i + 16)
                            acts.wait(pe, i - 1, "osb")
                            for hf in range(2):
                                last = pe.matmul(o_ps[:, hf * 512:(hf + 1) * 512], aT[1][0:NQ, 0:R],
                                                 vn[:, hf * 512:(hf + 1) * 512], start=True, stop=False)
                            pes.done(last, "n_o")
                            return
                        c = int(b)
                        s = c % 2
                        for k in range(CHUNK_PAGES):
                            last = pe.transpose(aT_ps[s][:, k * R:(k + 1) * R], loga[s][:, k * P:(k + 1) * P],
                                                ident[0:R, 0:R])
                        pes.done(last, f"{b}_aT")
                        acts.wait(pe, i, f"{b}_aT")
                        pe.wait_ge(v_loaded[s], 64 * (2 * i + c // 2) + 64)
                        for k in range(CHUNK_PAGES):
                            for hf in range(2):
                                last = pe.matmul(o_ps[:, hf * 512:(hf + 1) * 512], aT[s][:, k * R:(k + 1) * R],
                                                 vc[s][:, k, hf * 512:(hf + 1) * 512], start=False,
                                                 stop=c == NCH - 1 and k == CHUNK_PAGES - 1)
                        pes.done(last, f"{b}_o")

                    for c in range(NCH):
                        s = c % 2
                        pe.wait_ge(k_loaded[s], 64 * (2 * i + c // 2) + 64)
                        if c >= 2:
                            dve.wait(pe, i, f"{c - 2}_log")
                        for h in range(HEADS):
                            last = pe.matmul(z[s][:], qpad[:, h * R:(h + 1) * R], kc[s][:, :, h * P:(h + 1) * P],
                                             start=h == 0, stop=h == HEADS - 1)
                        pes.done(last, f"{c}_z")
                        turn_and_sum(blocks[c])
                    turn_and_sum(blocks[NCH])
                    acts.wait(pe, i, "osb")
                    for h in range(HEADS):
                        last = pe.matmul(fin_ps[:, 0:R], osb[:, h * P:(h + 1) * P], sel[:, h, :], start=h == 0,
                                         stop=h == HEADS - 1)
                    pes.done(last, "out")

            @block.vector
            def _(v):
                v.memset(one[:], 1.0).then_inc(cleared, 1)
                v.memset(qpad[:], 0.0).then_inc(cleared, 1)
                v.memset(qmpad[:], 0.0).then_inc(cleared, 1)
                v.memset(so[:], 0.0).then_inc(cleared, 1)
                v.memset(smo[:], 0.0).then_inc(cleared, 1)
                v.wait_ge(cleared, 5)
                v.wait_ge(const_loaded, 16 * 9)
                dve.open(v)
                with v.Fori(0, NSEQ) as i:
                    pes.wait(v, i - 1, "out")
                    v.tensor_copy(qpad[:].rearrange("p (h c) -> p h c", c=R + NQ)[:, :, 0:NQ],
                                  q[:, :, bass.ds(i * NQ, NQ)])
                    dve.done(v.tensor_copy(qmpad[:].rearrange("p (h c) -> p h c", c=MR + NQ)[:, :, 0:NQ],
                                           qm[:, :, bass.ds(i * NQ, NQ)]), "pads")
                    pes.wait(v, i, "mscore")
                    dve.done(v.reduce_max(peak[:], m_ps[0:MR, 0:NMEM], axis=AX), "peak")
                    dve.wait(v, i, "peak")
                    dve.done(v.tensor_scalar(npeak[:], peak[:], -MEM_SCALE, None, ALU.mult), "npeak")
                    acts.wait(v, i, "mexp")
                    dve.done(v.reciprocal(rden[:], den[:]), "rden")
                    dve.wait(v, i, "rden")
                    dve.done(v.tensor_scalar(prob[:], prob[:], rden[:], None, ALU.mult), "prob")
                    for b in blocks:
                        s = 1 if b == "n" else int(b) % 2
                        w = NQ if b == "n" else CW
                        zz = fin_ps[0:R, 0:NQ] if b == "n" else z[s][:]
                        sf, lg = soft[s][:, 0:w], loga[s][:, 0:w]
                        prev = None if b == "n" else first[1 - s]
                        pes.wait(v, i, f"{b}_z")
                        dve.done(v.tensor_scalar(sf, zz, bias[:], CAP, ALU.add, ALU.min), f"{b}_cap")
                        acts.wait(v, i, f"{b}_ln")
                        dve.done(v.scalar_tensor_tensor(out=sf, in0=zz, scalar=bias[:], in1=sf, op0=ALU.add,
                                                        op1=ALU.max), f"{b}_sp")
                        dve.wait(v, i, f"{b}_sp")
                        if b not in ("n", "0"):
                            pes.wait(v, i, "n_aT" if b == "1" else f"{int(b) - 2}_aT")
                        dve.done(v.tensor_tensor_scan(out=lg[:, ::-1], data0=one[0:R, :].to_broadcast([R, w]),
                                                      data1=sf[:, ::-1], initial=0.0 if prev is None else prev[:],
                                                      op0=ALU.mult, op1=ALU.add), f"{b}_cum")
                        dve.wait(v, i, f"{b}_cum")
                        dve.done(v.tensor_copy(first[s][:], lg[:, 0:1]), f"{b}_first")
                        dve.wait(v, i, f"{b}_first")
                        dve.done(v.scalar_tensor_tensor(out=lg, in0=zz, scalar=bias[:], in1=lg, op0=ALU.add,
                                                        op1=ALU.subtract), f"{b}_log")

            @block.scalar
            def _(act):
                act.wait_ge(cleared, 5)
                act.wait_ge(const_loaded, 16 * 9)
                acts.open(act)
                with act.Fori(0, NSEQ) as i:
                    dve.wait(act, i, "npeak")
                    acts.done(act.activation(prob[:], m_ps[0:MR, 0:NMEM], ACT.Exp, bias=npeak[:], scale=MEM_SCALE,
                                             accum_out=den[:]), "mexp")
                    pes.wait(act, i, "mprobT")
                    acts.done(act.activation(probT[:].rearrange("p m r -> p (m r)"), m_ps[:, 0:2 * MR], ACT.Copy), "mprobT")
                    pes.wait(act, i, "mom")
                    acts.done(act.activation(om[:], m_ps[0:MR, :], ACT.Copy), "mom")
                    pes.wait(act, i, "mout")
                    acts.done(act.activation(smo[:, :, bass.ds(i * NQ, NQ)],
                                             m_ps[:, 0:MR].rearrange("p (h q) -> p h q", h=MH), ACT.Copy), "mout")
                    for b in blocks:
                        s = 1 if b == "n" else int(b) % 2
                        w = NQ if b == "n" else CW
                        sf, lg = soft[s][:, 0:w], loga[s][:, 0:w]
                        dve.wait(act, i, f"{b}_cap")
                        acts.done(act.activation(sf, sf, ACT.Exp), f"{b}_exp")
                        acts.wait(act, i, f"{b}_exp")
                        acts.done(act.activation(sf, sf, ACT.Ln, bias=1.0), f"{b}_ln")
                        dve.wait(act, i, f"{b}_log")
                        acts.done(act.activation(lg, lg, ACT.Exp), f"{b}_a")
                        pes.wait(act, i, f"{b}_aT")
                        if b == "n":
                            acts.done(act.activation(aT[1][0:NQ, 0:R], aT_ps[1][0:NQ, 0:R], ACT.Copy), "n_aT")
                        else:
                            acts.done(act.activation(aT[s][:], aT_ps[s][:], ACT.Copy), f"{b}_aT")
                    pes.wait(act, i, f"{NCH - 1}_o")
                    acts.done(act.activation(osb[:], o_ps[:], ACT.Copy), "osb")
                    pes.wait(act, i, "out")
                    acts.done(act.activation(so[:, :, bass.ds(i * NQ, NQ)],
                                             fin_ps[:, 0:R].rearrange("p (h q) -> p h q", h=HEADS), ACT.Copy), "out")
                acts.wait(act, NSEQ - 1, "out")
                c0 = PT * P
                act.dma_start(dr["sbT"][:, :, c0:c0 + P].rearrange("h p n -> p h n"), so[:]).then_inc(o_stored, 16)
                act.dma_start(dr["mT"][:, :, c0:c0 + P].rearrange("h p n -> p h n"), smo[:]).then_inc(o_stored, 16)
                act.wait_ge(o_stored, 32)


def route_and_mix(nc, sem, dr, n_tiles):
    TKN = PH * TOPK
    ph = Phase(nc, "pe")
    with ph.ctx:
        lng = ph.sb("lng", [P, D])
        lnb = ph.sb("lnb", [P, D])
        iota = ph.sb("iota", [P, TOPK])
        score = ph.sb("score", [P, 2 * PH, NK])
        cand = ph.sb("cand", [P, PH, TOPK, TOPK])
        best = ph.sb("best", [P, PH, 2, TOPK])
        besti = ph.sb("besti", [P, PH, 2, TOPK], U32)
        bestf = ph.sb("bestf", [P, PH, 2, TOPK])
        top = ph.sb("top", [P, PH, TOPK])
        topi = ph.sb("topi", [P, PH, TOPK], U32)
        half = [ph.sb(f"half{i}", [P, PH, TOPK], U32) for i in range(2)]
        halff = [ph.sb(f"halff{i}", [P, PH, TOPK]) for i in range(2)]
        part = [ph.sb(f"part{i}", [P, PH, TOPK]) for i in range(2)]
        index_next = ph.sb("index_next", [P, TKN], U32)
        index = ph.sb("index", [P, TKN], U32)
        staged = [ph.sb(f"staged{i}", [P, PEAK], U32) for i in range(2)]
        share_next = ph.sb("share_next", [P, PH, TOPK])
        share = ph.sb("share", [P, TKN])
        total = ph.sb("total", [P, PH])
        x1_next = ph.sb("x1_next", [P, D])
        x1 = ph.sb("x1", [P, D])
        y = ph.sb("y", [P, D])
        out = ph.sb("out", [P, D])
        hid = ph.sb("hid", [P, TKN])
        coef = ph.sb("coef", [P, TKN])
        urow = [ph.sb(f"urow{i}", [P, D]) for i in range(PEAK)]
        vrow = [ph.sb(f"vrow{i}", [P, D]) for i in range(PEAK)]
        stats = ph.sb("stats", [P, 12])
        mean = ph.sb("mean", [P, 2])
        std = ph.sb("std", [P, 2])
        const_loaded = sem("const_loaded")
        score_loaded, x1_loaded = sem("score_loaded"), sem("x1_loaded")
        u_loaded = [sem(f"u_loaded{i}") for i in range(PEAK)]
        v_loaded = [sem(f"v_loaded{i}") for i in range(PEAK)]
        dotted = sem("dotted")
        added = sem("added")
        gelued = sem("gelued")
        weighted = sem("weighted")
        picked = sem("picked")
        exped = sem("exped")
        started = sem("started")
        shared = sem("shared")
        indexed = sem("indexed")
        staging = sem("staging")
        y_stored = sem("y_stored")
        out_free = sem("out_free")
        dve = Steps(sem("ln_dve"), layer_norm_steps(""))
        acts = Steps(sem("ln_act"), ["root"])

        KSTEP = PH * 5 + 1 + PH // 2 * 5 + 9

        class TopK:

            def __init__(self, v, tile):
                self.v, self.tile, self.n = v, tile, 0

            def round(self, *instructions):
                for ins in instructions[:-1]:
                    ins()
                instructions[-1]().then_inc(picked, 1)
                self.n += 1
                self.v.wait_ge(picked, KSTEP * self.tile + self.n)
                apart(self.v, dr["unwaited"])

            def keys(self, h):
                v, s = self.v, (score[:, 2 * h, :], score[:, 2 * h + 1, :])
                b = lambda p, lo: best[:, h, p, lo:lo + 8]
                bi = lambda p, lo: besti[:, h, p, lo:lo + 8]
                if h == 0:
                    v.wait_ge(score_loaded, 16 * self.tile + 16)
                    apart(v, dr["unwaited"])
                self.round(*[lambda p=p: v.max(b(p, 0), s[p]) for p in range(2)])
                self.round(*[lambda p=p: v.max_index(bi(p, 0), b(p, 0), s[p]) for p in range(2)])
                self.round(*[lambda p=p: v.match_replace(s[p], b(p, 0), s[p], NEG) for p in range(2)])
                self.round(*[lambda p=p: v.max(b(p, 8), s[p]) for p in range(2)])
                self.round(*[lambda p=p: v.max_index(bi(p, 8), b(p, 8), s[p]) for p in range(2)])

            def sums(self):
                v = self.v
                self.round(lambda: v.tensor_tensor(
                    cand[:], best[:, :, 0, :].unsqueeze(3).to_broadcast([P, PH, TOPK, TOPK]),
                    best[:, :, 1, :].unsqueeze(2).to_broadcast([P, PH, TOPK, TOPK]), op=ALU.add))

            def pairs(self, h0):
                v, hs = self.v, (h0, h0 + 1)
                c = lambda h: cand[:, h].rearrange("p a b -> p (a b)")
                self.round(*[lambda h=h: v.max(top[:, h, 0:8], c(h)) for h in hs])
                self.round(*[lambda h=h: v.max_index(topi[:, h, 0:8], top[:, h, 0:8], c(h)) for h in hs])
                self.round(*[lambda h=h: v.match_replace(c(h), top[:, h, 0:8], c(h), NEG) for h in hs])
                self.round(*[lambda h=h: v.max(top[:, h, 8:16], c(h)) for h in hs])
                self.round(*[lambda h=h: v.max_index(topi[:, h, 8:16], top[:, h, 8:16], c(h)) for h in hs])

            def experts(self):
                v = self.v
                wide = [P, PH, TOPK, TOPK]
                self.round(lambda: v.tensor_scalar(half[0][:], topi[:], 4, None, ALU.logical_shift_right),
                           lambda: v.tensor_scalar(half[1][:], topi[:], 15, None, ALU.bitwise_and),
                           lambda: v.tensor_copy(bestf[:], besti[:]))
                self.round(lambda: v.tensor_copy(halff[0][:], half[0][:]), lambda: v.tensor_copy(halff[1][:], half[1][:]))
                for p in range(2):
                    self.round(lambda: v.tensor_tensor(
                        cand[:], halff[p][:].unsqueeze(3).to_broadcast(wide),
                        iota[:].unsqueeze(1).unsqueeze(1).to_broadcast(wide), op=ALU.is_equal))
                    self.round(lambda: v.tensor_tensor(
                        cand[:], cand[:], bestf[:, :, p, :].unsqueeze(2).to_broadcast(wide), op=ALU.mult))
                    self.round(lambda: v.reduce_sum(part[p][:], cand[:], axis=AX))
                if not isinstance(self.tile, int):
                    v.wait_ge(indexed, self.tile)
                self.round(lambda: v.scalar_tensor_tensor(
                    out=index_next[:].rearrange("p (h k) -> p h k", h=PH), in0=part[0][:], scalar=float(NK),
                    in1=part[1][:], op0=ALU.mult, op1=ALU.add))

            def finish(self):
                assert self.n == KSTEP, (self.n, KSTEP)

        SH = 4

        with nc.Block() as block:
            @block.sync
            def _(sp):
                for dst, src in ((lng[:], "ln2_g"), (lnb[:], "ln2_b"), (iota[:], "iota")):
                    sp.dma_start(dst, dr[src]).then_inc(const_loaded, 16)
                sp.dma_start(score[:].rearrange("p a n -> p (a n)"), dr["scores"][0]).then_inc(score_loaded, 16)
                sp.dma_start(x1_next[:], dr["x1"][0]).then_inc(x1_loaded, 16)
                with sp.Fori(0, n_tiles - 1) as i:
                    sp.wait_ge(picked, KSTEP * i + PH * 5)
                    sp.dma_start(score[:].rearrange("p a n -> p (a n)"),
                                 dr["scores"][bass.ds(i + 1, 1)].rearrange("a p n -> p (a n)")).then_inc(score_loaded, 16)
                    sp.wait_ge(started, 2 * i + 2)
                    sp.dma_start(x1_next[:], dr["x1"][bass.ds(i + 1, 1)].rearrange("a p n -> p (a n)")).then_inc(x1_loaded, 16)

            @block.gpsimd
            def _(pool):
                def unit(m, s, first_of_tile):
                    pool.wait_ge(staging, m + 1)
                    for k in range(PEAK):
                        pool.wait_ge(dotted, PEAK * m + k + 1)
                        apart(pool, dr["unwaited"])
                        pool.indirect_dma_start(out=urow[k][:], out_offset=None, in_=dr["peer_u"],
                                                in_offset=bass.IndirectOffsetOnAxis(ap=staged[s][:, k:k + 1], axis=0)
                                                ).then_inc(u_loaded[k], 16)
                    for k in range(PEAK):
                        pool.wait_ge(added, PEAK * (m + 1) + k + 1)
                        apart(pool, dr["unwaited"])
                        pool.indirect_dma_start(out=vrow[k][:], out_offset=None, in_=dr["peer_v"],
                                                in_offset=bass.IndirectOffsetOnAxis(ap=staged[s][:, k:k + 1], axis=0)
                                                ).then_inc(v_loaded[k], 16)

                with pool.Fori(0, n_tiles) as t:
                    pool.wait_ge(picked, KSTEP * t + KSTEP)
                    apart(pool, dr["unwaited"])
                    pool.tensor_copy(index[:], index_next[:]).then_inc(indexed, 1)
                    pool.wait_ge(indexed, t + 1)
                    apart(pool, dr["unwaited"])
                    with pool.Fori(0, UNITS // 2) as i:
                        for s in range(2):
                            m = t * UNITS + i * 2 + s
                            pool.wait_ge(added, PEAK * m + PEAK)
                            apart(pool, dr["unwaited"])
                            pool.tensor_copy(staged[s][:], index[:, bass.ds((i * 2 + s) * PEAK, PEAK)]).then_inc(staging, 1)
                            unit(m, s, False)

            @block.scalar
            def _(act):
                acts.open(act)

                def start(n):
                    act.wait_ge(x1_loaded, 16 * n + 16)
                    act.wait_ge(dotted, PEAK * UNITS * n + PEAK)
                    act.activation(x1[:], x1_next[:], ACT.Copy).then_inc(started, 1)
                    dve.wait(act, n - 1, "norm")
                    act.activation(y[:], x1_next[:], ACT.Copy, scale=ALPHA).then_inc(started, 1)

                def gelus(n):
                    for j in range(UNITS):
                        act.wait_ge(dotted, PEAK * UNITS * n + PEAK * (j + 2))
                        c = slice(PEAK * j, PEAK * (j + 1))
                        act.activation(coef[:, c], hid[:, c], ACT.Gelu_apprx_tanh).then_inc(gelued, 1)

                def exp_shares(n):
                    act.wait_ge(shared, SH * n + 2)
                    act.activation(share_next[:], share_next[:], ACT.Exp).then_inc(exped, 1)

                def root_and_store(n, dst):
                    dve.wait(act, n, "var")
                    acts.done(act.activation(std[:, 1:2], std[:, 0:1], ACT.Sqrt), "root")
                    dve.wait(act, n, "out")
                    act.dma_start(dst, out[:]).then_inc(y_stored, 16)

                exp_shares(0)
                start(0)
                with act.Fori(0, n_tiles - 1) as n:
                    gelus(n)
                    exp_shares(n + 1)
                    root_and_store(n, dr["y"][bass.ds(n, 1)].rearrange("a p n -> p (a n)"))
                    start(n + 1)
                    act.wait_ge(y_stored, 16 * n + 16)
                    act.sem_inc(out_free, 1)
                gelus(n_tiles - 1)
                root_and_store(n_tiles - 1, dr["y"][n_tiles - 1])
                act.wait_ge(y_stored, 16 * n_tiles)

            @block.vector
            def _(v):
                v.wait_ge(const_loaded, 48)
                v.sem_inc(dotted, PEAK)
                v.sem_inc(added, 2 * PEAK)
                v.sem_inc(shared, 1)
                v.sem_inc(weighted, 1)
                v.sem_inc(out_free, 1)
                dve.open(v)

                def softmax_start(n):
                    v.wait_ge(shared, SH * n + 1)
                    v.tensor_tensor(share_next[:], top[:], top[:, :, 0:1].to_broadcast([P, PH, TOPK]),
                                    op=ALU.subtract).then_inc(shared, 1)

                def softmax_end(n):
                    v.wait_ge(exped, n + 1)
                    v.reduce_sum(total[:], share_next[:], axis=AX).then_inc(shared, 1)
                    v.wait_ge(shared, SH * n + 3)
                    v.reciprocal(total[:], total[:]).then_inc(shared, 1)

                def softmax_take(n):
                    v.wait_ge(shared, SH * n + 4)
                    v.wait_ge(weighted, UNITS * n + 1)
                    v.tensor_tensor(share[:].rearrange("p (h k) -> p h k", h=PH), share_next[:],
                                    total[:].unsqueeze(2).to_broadcast([P, PH, TOPK]), op=ALU.mult).then_inc(shared, 1)
                    v.wait_ge(shared, SH * n + 5)

                def dot(n, j, k):
                    v.wait_ge(u_loaded[k], 16 * UNITS * n + 16 * (j + 1))
                    col = PEAK * j + k
                    v.scalar_tensor_tensor(out=urow[k][:], in0=urow[k][:], scalar=1.0, in1=x1[:], op0=ALU.mult,
                                           op1=ALU.mult, accum_out=hid[:, col:col + 1]).then_inc(dotted, 1)

                def weigh(n, j):
                    v.wait_ge(gelued, UNITS * n + j + 1)
                    c = slice(PEAK * j, PEAK * (j + 1))
                    v.tensor_tensor(coef[:, c], coef[:, c], share[:, c], op=ALU.mult).then_inc(weighted, 1)
                    v.wait_ge(weighted, UNITS * n + j + 2)

                def add(n, j, k):
                    v.wait_ge(v_loaded[k], 16 * UNITS * n + 16 * (j + 1))
                    v.wait_ge(added, PEAK * UNITS * n + PEAK * (j + 2) + k)
                    col = PEAK * j + k
                    v.scalar_tensor_tensor(out=y[:], in0=vrow[k][:], scalar=coef[:, col:col + 1], in1=y[:],
                                           op0=ALU.mult, op1=ALU.add).then_inc(added, 1)

                def tile(n, following):
                    softmax_take(n)
                    v.wait_ge(started, 2 * n + 2)
                    pick = TopK(v, n + 1) if following else None
                    for j in range(UNITS):
                        for k in range(PEAK):
                            dot(n, j, k)
                            if j and k >= 1:
                                if k == 1:
                                    weigh(n, j - 1)
                                add(n, j - 1, k - 1)
                        if j:
                            add(n, j - 1, PEAK - 1)
                        if following:
                            if j < 8:
                                pick.keys(j)
                            elif j == 8:
                                pick.sums()
                            elif j < 13:
                                pick.pairs(2 * (j - 9))
                            elif j == 13:
                                pick.experts()
                                pick.finish()
                    weigh(n, UNITS - 1)
                    if following:
                        softmax_start(n + 1)
                    for k in range(PEAK):
                        add(n, UNITS - 1, k)
                    if following:
                        softmax_end(n + 1)
                    v.wait_ge(added, PEAK * UNITS * n + PEAK * (UNITS + 2))
                    v.wait_ge(out_free, n + 1)
                    layer_norm(v, dve, acts, n, "", y[:], out[:], stats, mean, std, lng, lnb, dr["unwaited"])

                pick = TopK(v, 0)
                for h in range(PH):
                    pick.keys(h)
                pick.sums()
                for h in range(0, PH, 2):
                    pick.pairs(h)
                pick.experts()
                pick.finish()
                softmax_start(0)
                softmax_end(0)
                with v.Fori(0, n_tiles - 1) as n:
                    tile(n, True)
                tile(n_tiles - 1, False)


def build(nc, dr):
    with nc.semaphore("unwaited") as unwaited:
        dr["unwaited"] = unwaited

        def scratch(name, *shape):
            dr[name] = nc.dram_tensor(f"scratch_{name}", shape, F32, kind="Internal").ap()

        scratch("uT", GG, P, TPAD)
        scratch("qmT", MH, P, TPAD)
        scratch("qT", HEADS, P, TPAD)
        scratch("gv", TT, P, 512)
        scratch("gT", GG, P, TPAD)
        scratch("mT", MH, P, TPAD)
        scratch("sbT", HEADS, P, TPAD)
        scratch("x1", TT, P, D)
        scratch("scores", TT, P, 2 * PH * NK)

        def run(name, phase, *args):
            with ExitStack() as own:
                sems = []

                def sem(label):
                    sems.append(own.enter_context(nc.semaphore(f"{name}_{label}")))
                    return sems[-1]

                phase(nc, sem, dr, *args)
                with nc.Block() as block:
                    @block.sync
                    def _(sp):
                        for s in sems:
                            sp.sem_clear(s)

        for g, (tile0, tiles) in enumerate([(0, 4), (4, 5)]):
            run(f"project{g}", project, g, tile0, tiles)
            run(f"local{g}", local_branches, g, tile0, tiles)
            run(f"prompt{g}", attend_prompt, g, tile0, 4)
            if g == 1:
                run("sample", attend_sample)
            run(f"merge{g}", merge, g, tile0, tiles)
        run("peer", route_and_mix, TT)


def kernel(**inputs):
    import concourse.bacc as bacc
    from concourse.bass_utils import run_bass_kernel_spmd

    a = {k: np.asarray(v) for k, v in inputs.items()}

    def pad_tokens():
        x = np.zeros((TPAD, D), np.float32)
        x[0:SEQ] = a["x_prompt"][0]
        x[SEQ:SEQ + NSEQ * NQ] = a["x_sample"].reshape(NSEQ * NQ, D)
        return x

    def feature_major(x):
        return x.T.reshape(-1, P, x.shape[0]).transpose(1, 0, 2)

    def units(w, width=UW):
        return w.reshape(w.shape[0] // P, P, w.shape[1] // width, width).transpose(2, 1, 0, 3)

    def rows(x, n=P):
        return np.broadcast_to(x, (n, x.size))

    x = pad_tokens()
    w = a["w_in"][0]
    u, gv, q, k, v, qm, gates = np.split(w, np.cumsum([512, 512, 1024, 1024, 1024, 512]), axis=1)
    spatial = a["w_spatial"][0].transpose(2, 0, 1)
    spatial_new = np.zeros((P, GG, P), np.float32)
    bias_new = np.zeros((GG, P), np.float32)
    for s in range(P // NQ):
        at = slice(s * NQ, (s + 1) * NQ)
        spatial_new[at, :, at] = spatial[0:NQ, :, 0:NQ]
        bias_new[:, at] = a["b_spatial"][0][:, 0:NQ]
    sel = np.zeros((HEADS * NQ, HEADS, HEADS * NQ), np.float32)
    for r in range(HEADS * NQ):
        sel[r, r // NQ, r] = 1.0
    n_phys = a["cache_sb_k"].shape[1]
    at_query = np.arange(HEADS * NQ) % NQ
    ins = {
        "x": x.reshape(TT, P, D),
        "xT": feature_major(x),
        "memT": feature_major(a["mem_prompt"][0]),
        "w_in": units(np.concatenate([u, qm, q, k, gv, v, gates], axis=1)),
        "w_mem": units(a["w_mem_kv"][0]),
        "w_br0": units(a["w_br_gmlp"][0]),
        "w_br1": units(a["w_br_sb"][0]),
        "w_br2": units(a["w_br_mem"][0]),
        "w_out": units(a["w_out"][0]),
        "w_q": units(a["peer_wq"][0]),
        "b_gate": a["b_gate"][0].reshape(24, P).T,
        "gln_g": rows(a["gmlp_ln_g"][0]),
        "gln_b": rows(a["gmlp_ln_b"][0]),
        "w_spatial": np.stack([spatial, spatial_new], axis=1),
        "b_spatial": np.stack([a["b_spatial"][0], bias_new])[None],
        "sb_bias": rows(a["sb_bias"][0]),
        "sb_bias_rows": np.repeat(a["sb_bias"][0], NQ)[:, None],
        "ln1_g": rows(a["ln1_g"][0]),
        "ln1_b": rows(a["ln1_b"][0]),
        "ln2_g": rows(a["ln2_g"][0]),
        "ln2_b": rows(a["ln2_b"][0]),
        "keysT": a["peer_subkeys"][0].reshape(2 * PH, NK, P).transpose(2, 0, 1),
        "peer_u": a["peer_u"][0],
        "peer_v": a["peer_v"][0],
        "cache_k": a["cache_sb_k"][0].transpose(0, 3, 2, 1).reshape(n_phys, P, HEADS * P),
        "cache_v": a["cache_sb_v"][0].reshape(n_phys, P, HEADS * P),
        "mem_k": a["cache_mem_k"][0].transpose(0, 3, 2, 1),
        "mem_v": a["cache_mem_v"][0].reshape(NSEQ, 2, P, 512).transpose(0, 2, 1, 3),
        "table": a["page_table"].reshape(1, -1).astype(np.int32),
        "ident": np.eye(P, dtype=np.float32),
        "ones": np.ones((1, P), np.float32),
        "tril": np.triu(np.ones((P, P), np.float32)),
        "neg": np.where(np.arange(P)[None] >= np.arange(P)[:, None], NEG, 0.0).astype(np.float32),
        "neg_new": np.where(np.arange(NQ)[None] >= at_query[:, None], NEG, 0.0).astype(np.float32),
        "sel": sel,
        "selm": sel[0:MH * NQ, 0:MH, 0:MH * NQ],
        "iota": rows(np.arange(TOPK, dtype=np.float32)),
    }
    outs = {
        "kT": (HEADS, P, TPAD), "v": (TT, P, HEADS * P), "mkT": (MH, P, NMEM), "mv": (2, P, 512),
        "gv_sample": (NSEQ * NQ, 512), "y": (TT, P, D),
    }
    nc = bacc.Bacc("TRN2", target_bir_lowering=False, num_devices=1)
    arrays, dr = {}, {}
    for name, value in ins.items():
        arrays[f"in_{name}"] = np.ascontiguousarray(value)
        dr[name] = nc.dram_tensor(f"in_{name}", value.shape, mybir.dt.from_np(value.dtype), kind="ExternalInput").ap()
    for name, shape in outs.items():
        dr[name] = nc.dram_tensor(f"out_{name}", shape, F32, kind="ExternalOutput").ap()
    build(nc, dr)
    res = run_bass_kernel_spmd(nc, [arrays], core_ids=[0]).results[0]
    got = {name: np.asarray(res[f"out_{name}"]) for name in outs}
    y = got["y"].reshape(TPAD, D)
    k = got["kT"].reshape(HEADS * P, TPAD).T
    v = got["v"].reshape(TPAD, HEADS * P)
    new = slice(SEQ, SEQ + NSEQ * NQ)
    return (y[0:SEQ].reshape(1, SEQ, D), y[new].reshape(NSEQ, NQ, D),
            k[0:SEQ].reshape(1, 1, SEQ, HEADS, P), v[0:SEQ].reshape(1, 1, SEQ, HEADS, P),
            got["mkT"].reshape(MH * P, NMEM).T.reshape(1, 1, NMEM, MH, P), got["mv"].reshape(1, 1, NMEM, MH, P),
            k[new].reshape(1, NSEQ, NQ, HEADS, P), v[new].reshape(1, NSEQ, NQ, HEADS, P),
            got["gv_sample"].reshape(1, NSEQ, NQ, GG, P))
```

```python
import numpy as np
from contextlib import ExitStack

import concourse.bass as bass
from concourse import mybir

F32 = mybir.dt.float32
U32 = mybir.dt.uint32
I32 = mybir.dt.int32
ACT = mybir.ActivationFunctionType
ALU = mybir.AluOpType
AX = mybir.AxisListType.X

P = 128
D = 1024
KD = D // P
SEQ = 1024
NSEQ = 8
NQ = 8
PT = SEQ // P
TT = PT + 1
TPAD = TT * P
HEADS = 8
MH = 4
NMEM = 256
GG = 4
PAGES = 16
CHUNK_PAGES = 4
UW = 512
PH = 8
NK = 128
TOPK = 16
NEXP = NK * NK
SB_SCALE = P ** -0.5
MEM_SCALE = P ** -0.5
ALPHA = 2.0 ** 0.25
EPS = 1e-5
NEG = -1e30
CAP = 40.0
GATE_W = 256
ROWS = 4
UNITS = PH * TOPK // ROWS


def apart(eng, unwaited):
    eng.sem_inc(unwaited, 1)


class Steps:

    def __init__(self, sem, names, credit=1):
        self.sem, self.names, self.credit = sem, names, credit
        self.index = {n: i for i, n in enumerate(names)}
        assert len(self.index) == len(names)
        self.last = -1

    def open(self, eng):
        eng.sem_inc(self.sem, self.credit * len(self.names))

    def done(self, ins, name):
        assert self.index[name] == (self.last + 1) % len(self.names), (name, self.last)
        self.last = self.index[name]
        ins.then_inc(self.sem, 1)

    def value(self, item, name):
        return (item + self.credit) * len(self.names) + self.index[name] + 1

    def wait(self, eng, item, name):
        eng.wait_ge(self.sem, self.value(item, name))


class Gate:

    def __init__(self, sem):
        self.sem, self.n = sem, 0

    def close(self, block):
        self.n += 4

        def meet(eng):
            eng.drain().then_inc(self.sem, 1)
            eng.wait_ge(self.sem, self.n)

        block.sync(meet)
        block.tensor(meet)
        block.scalar(meet)
        block.vector(meet)


class Store:

    def __init__(self, sems):
        self.sems = sems
        self.n = [0] * len(sems)

    def wait_free(self, eng, slot):
        if self.n[slot]:
            eng.wait_ge(self.sems[slot], 16 * self.n[slot])

    def start(self, eng, slot, dst, src):
        eng.dma_start(dst, src).then_inc(self.sems[slot], 16)
        self.n[slot] += 1

    def wait_all(self, eng):
        for slot in range(len(self.sems)):
            self.wait_free(eng, slot)


class NoBackground:

    def scalar(self, act, stage, i, places):
        pass

    def vector(self, v, stage, i, places):
        pass


class Background:

    def __init__(self, peer, shares, limit):
        self.peer, self.shares, self.limit = peer, shares, limit

    def steps(self, stage, i, places):
        n = self.shares[stage]
        return (i + 1) * n // places - i * n // places

    def scalar(self, act, stage, i, places):
        self.peer.scalar(act, self.steps(stage, i, places), self.limit)

    def vector(self, v, stage, i, places):
        self.peer.vector(v, self.steps(stage, i, places), self.limit)


class Phase:

    def __init__(self, nc, name):
        self.nc, self.name, self.ctx = nc, name, ExitStack()

    def sb(self, name, shape, dt=F32):
        return self.ctx.enter_context(self.nc.sbuf_tensor(f"{self.name}_{name}", shape, dt))

    def ps(self, name, shape, dt=F32):
        return self.ctx.enter_context(self.nc.psum_tensor(f"{self.name}_{name}", shape, dt))



def project(nc, block, sem, dr, bg, g, tile0, tiles):
    T = tiles * P
    t0 = tile0 * P
    chunks = [(c, min(512, T - c)) for c in range(0, T, 512)]
    ph = Phase(nc, f"pr{g}")
    with ph.ctx:
        xT = ph.sb("xT", [P, KD, T])
        memT = ph.sb("memT", [P, KD, NMEM])
        wbuf = [ph.sb(f"w{i}", [P, KD, UW]) for i in range(2)]
        stage = [ph.sb(f"st{i}", [P, 512]) for i in range(4)]
        bank = [ph.ps(f"b{i}", [P, 512]) for i in range(4)]
        x_loaded = sem("x_loaded")
        w_loaded = [sem(f"w_loaded{i}") for i in range(2)]
        product = sem("product")
        evacuated = sem("evacuated")
        stored = Store([sem(f"stored{i}") for i in range(4)])

        FM, TM = 6, 3
        units = FM + TM + (2 if g == 0 else 0)
        per_fm, per_tm = 4 * len(chunks), tiles
        jobs_after = [per_fm * (u + 1) for u in range(FM)]
        jobs_after += [per_fm * FM + per_tm * (u + 1) for u in range(TM)]
        jobs_after += [jobs_after[-1] + 4, jobs_after[-1] + 6]

        jobs = []
        for u in range(FM):
            for b in range(4):
                for c0, n in chunks:
                    cols = slice(t0 + c0, t0 + c0 + n)
                    blk = 4 * u + b
                    if u == 0:
                        jobs.append((ACT.Gelu_apprx_tanh, 1.0, n, dr["uT"][b, :, cols]))
                    elif u == 1:
                        jobs.append((ACT.Copy, 1.0, n, dr["qmT"][b, :, cols]))
                    elif u < 4:
                        jobs.append((ACT.Copy, SB_SCALE, n, dr["qT"][blk - 8, :, cols]))
                    else:
                        jobs.append((ACT.Copy, 1.0, n, dr["kT"][blk - 16, :, cols]))
        for u in range(TM):
            for t in range(tile0, tile0 + tiles):
                if u == 0:
                    jobs.append((ACT.Gelu_apprx_tanh, 1.0, 512, dr["gv"][t]))
                else:
                    jobs.append((ACT.Copy, 1.0, 512, dr["v"][t, :, (u - 1) * 512:u * 512]))
        if g == 0:
            jobs += [(ACT.Copy, 1.0, NMEM, dr["mkT"][b]) for b in range(4)]
            jobs += [(ACT.Copy, 1.0, 512, dr["mv"][m]) for m in range(2)]

        @block.sync
        def _(sp):
            sp.dma_start(xT[:], dr["xT"][:, :, t0:t0 + T]).then_inc(x_loaded, 16)
            if g == 0:
                sp.dma_start(memT[:], dr["memT"]).then_inc(x_loaded, 16)
            for u in range(units):
                if u >= 2:
                    sp.wait_ge(product, jobs_after[u - 2])
                src = dr["w_in"][u] if u < FM + TM else dr["w_mem"][u - FM - TM]
                sp.dma_start(wbuf[u % 2][:], src).then_inc(w_loaded[u % 2], 16)

        @block.tensor
        def _(pe):
            def accumulate(job, base, out, lhsT, rhs):
                pe.wait_ge(evacuated, base + job + 1)
                for k in range(KD):
                    last = pe.matmul(out, lhsT(k), rhs(k), start=k == 0, stop=k == KD - 1)
                last.then_inc(product, 1)

            pe.wait_ge(x_loaded, 32 if g == 0 else 16)
            with pe.Fori(0, FM // 2) as i:
                job = 0
                for s in range(2):
                    pe.wait_ge(w_loaded[s], 16 * i + 16)
                    for b in range(4):
                        for c0, n in chunks:
                            accumulate(job, 2 * per_fm * i, bank[job % 4][:, 0:n],
                                       lambda k: wbuf[s][:, k, b * P:(b + 1) * P],
                                       lambda k: xT[:, k, c0:c0 + n])
                            job += 1
            job = per_fm * FM
            for u in range(FM, FM + TM):
                pe.wait_ge(w_loaded[u % 2], 16 * (u // 2 + 1))
                for t in range(tiles):
                    accumulate(job, 0, bank[job % 4][:], lambda k: xT[:, k, t * P:(t + 1) * P],
                               lambda k: wbuf[u % 2][:, k, :])
                    job += 1
            if g == 0:
                pe.wait_ge(w_loaded[9 % 2], 16 * (9 // 2 + 1))
                for b in range(4):
                    accumulate(job, 0, bank[job % 4][:, 0:NMEM],
                               lambda k: wbuf[1][:, k, b * P:(b + 1) * P], lambda k: memT[:, k, :])
                    job += 1
                pe.wait_ge(w_loaded[10 % 2], 16 * (10 // 2 + 1))
                for m in range(2):
                    accumulate(job, 0, bank[job % 4][:], lambda k: memT[:, k, m * P:(m + 1) * P],
                               lambda k: wbuf[0][:, k, :])
                    job += 1

        @block.scalar
        def _(act):
            act.sem_inc(evacuated, 4)
            for j, (func, scale, n, dst) in enumerate(jobs):
                act.wait_ge(product, j + 1)
                stored.wait_free(act, j % 4)
                act.activation(stage[j % 4][:, 0:n], bank[j % 4][:, 0:n], func,
                               scale=scale).then_inc(evacuated, 1)
                act.wait_ge(evacuated, 4 + j + 1)
                stored.start(act, j % 4, dst, stage[j % 4][:, 0:n])
                bg.scalar(act, "project", j, len(jobs))
            stored.wait_all(act)

        @block.vector
        def _(v):
            for j in range(len(jobs)):
                bg.vector(v, "project", j, len(jobs))


def local_branches(nc, block, sem, dr, bg, g, tile0, tiles):
    ph = Phase(nc, f"lb{g}")
    with ph.ctx:
        ident = ph.sb("ident", [P, P])
        ones = ph.sb("ones", [1, P])
        tril = ph.sb("tril", [P, P])
        ws = ph.sb("ws", [P, 2, GG, P])
        bs = ph.sb("bs", [1, 2, GG, P])
        lng = ph.sb("lng", [P, 512])
        lnb = ph.sb("lnb", [P, 512])
        mkT = ph.sb("mkT", [P, MH, NMEM])
        mv = ph.sb("mv", [P, 2, 512])
        gv = [ph.sb(f"gv{i}", [P, 512]) for i in range(2)]
        uT = [ph.sb(f"uT{i}", [P, GG, P]) for i in range(2)]
        qmT = [ph.sb(f"qmT{i}", [P, MH, P]) for i in range(2)]
        gout = [ph.sb(f"gout{i}", [P, GG, P]) for i in range(2)]
        mout = [ph.sb(f"mout{i}", [P, MH, P]) for i in range(2)]
        stats = ph.sb("stats", [P, 6])
        mean = ph.sb("mean", [P, 2])
        std = ph.sb("std", [P, 2])
        peak = ph.sb("peak", [P, MH])
        npeak = ph.sb("npeak", [P, MH])
        den = ph.sb("den", [P, MH])
        rden = ph.sb("rden", [P, MH])
        prob = ph.sb("prob", [P, MH, NMEM])
        probT = ph.sb("probT", [P, MH, 2, P])
        spat_ps = ph.ps("spat", [P, GG, P])
        score_ps = ph.ps("score", [P, MH, NMEM])
        probT_ps = ph.ps("probT_ps", [P, MH, 2, P])
        mout_ps = ph.ps("mout_ps", [P, MH, P])
        const_loaded = sem("const_loaded")
        tile_loaded = [sem(f"tile_loaded{i}") for i in range(2)]
        masked = sem("masked")
        dve = Steps(sem("dve_steps"), ["stats", "mean", "var", "peak", "npeak", "rstd", "norm", "scaled",
                                       "vnorm", "gout", "rden", "prob"])
        acts = Steps(sem("act_steps"), ["exp", "std", "probT", "mout"])
        pes = Steps(sem("pe_steps"), ["score", "spat", "probT", "mout"])
        gstored = Store([sem(f"gstored{i}") for i in range(2)])
        mstored = Store([sem(f"mstored{i}") for i in range(2)])
        is_prompt = [t < PT for t in range(tile0, tile0 + tiles)]

        @block.sync
        def _(sp):
            for dst, src in ((ident[:], "ident"), (ones[:], "ones"), (tril[:], "tril"), (ws[:], "w_spatial"),
                             (bs[:], "b_spatial"), (lng[:], "gln_g"), (lnb[:], "gln_b"),
                             (mkT[:], None), (mv[:], None)):
                if src:
                    sp.dma_start(dst, dr[src]).then_inc(const_loaded, 16)
            sp.dma_start(mkT[:], dr["mkT"].rearrange("h p m -> p h m")).then_inc(const_loaded, 16)
            sp.dma_start(mv[:], dr["mv"].rearrange("m p c -> p m c")).then_inc(const_loaded, 16)

            def keep(n):
                t, s = tile0 + n, n % 2
                dve.wait(sp, n, "gout")
                sp.dma_start(dr["gT"][:, :, t * P:(t + 1) * P].rearrange("b p n -> p b n"),
                             gout[s][:]).then_inc(gstored.sems[s], 16)
                if not is_prompt[n]:
                    sp.dma_start(dr["gv_sample"], gv[s][0:NSEQ * NQ, :]).then_inc(gstored.sems[s], 16)

            for n in range(tiles):
                t, s = tile0 + n, n % 2
                if n >= 2:
                    keep(n - 2)
                    acts.wait(sp, n - 2, "mout")
                    dve.wait(sp, n - 2, "prob")
                cols = slice(t * P, (t + 1) * P)
                sp.dma_start(gv[s][:], dr["gv"][t]).then_inc(tile_loaded[s], 16)
                sp.dma_start(uT[s][:], dr["uT"][:, :, cols].rearrange("b p n -> p b n")).then_inc(tile_loaded[s], 16)
                sp.dma_start(qmT[s][:], dr["qmT"][:, :, cols].rearrange("b p n -> p b n")).then_inc(tile_loaded[s], 16)
            for n in range(max(tiles - 2, 0), tiles):
                keep(n)
            for s in range(min(2, tiles)):
                mine = [n for n in range(tiles) if n % 2 == s]
                sp.wait_ge(gstored.sems[s], 16 * (len(mine) + sum(not is_prompt[n] for n in mine)))

        @block.tensor
        def _(pe):
            pes.open(pe)
            pe.wait_ge(const_loaded, 16 * 9)
            pe.wait_ge(masked, 1)
            for n in range(tiles):
                s, which = n % 2, 0 if is_prompt[n] else 1
                pe.wait_ge(tile_loaded[s], 48 * (n // 2 + 1))
                if n:
                    acts.wait(pe, n - 1, "exp")
                for h in range(MH):
                    last = pe.matmul(score_ps[:, h, :], qmT[s][:, h, :], mkT[:, h, :], start=True, stop=True)
                pes.done(last, "score")
                dve.wait(pe, n, "vnorm")
                if n:
                    dve.wait(pe, n - 1, "gout")
                for k in range(GG):
                    pe.matmul(spat_ps[:, k, :], gv[s][:, k * P:(k + 1) * P], ws[:, which, k, :],
                              start=True, stop=False)
                    last = pe.matmul(spat_ps[:, k, :], ones[:], bs[:, which, k, :], start=False, stop=True)
                pes.done(last, "spat")
                dve.wait(pe, n, "prob")
                for h in range(MH):
                    for m in range(2):
                        last = pe.transpose(probT_ps[:, h, m, :], prob[:, h, m * P:(m + 1) * P], ident[:])
                pes.done(last, "probT")
                acts.wait(pe, n, "probT")
                if n:
                    acts.wait(pe, n - 1, "mout")
                for h in range(MH):
                    for m in range(2):
                        last = pe.matmul(mout_ps[:, h, :], mv[:, m, h * P:(h + 1) * P], probT[:, h, m, :],
                                         start=m == 0, stop=m == 1)
                pes.done(last, "mout")

        @block.vector
        def _(v):
            dve.open(v)
            v.wait_ge(const_loaded, 16 * 9)
            v.tensor_tensor(ws[:], ws[:], tril[:].unsqueeze(1).unsqueeze(1).to_broadcast([P, 2, GG, P]),
                            op=ALU.mult).then_inc(masked, 1)
            for n in range(tiles):
                s = n % 2
                v.wait_ge(tile_loaded[s], 48 * (n // 2 + 1))
                if n:
                    dve.wait(v, n - 1, "vnorm")
                dve.done(v.bn_stats(stats[:], gv[s][:]), "stats")
                dve.wait(v, n, "stats")
                dve.done(v.bn_aggr(mean[:], stats[:]), "mean")
                dve.wait(v, n, "mean")
                if n:
                    acts.wait(v, n - 1, "std")
                dve.done(v.tensor_scalar(std[:, 0:1], mean[:, 1:2], EPS, None, ALU.add), "var")
                pes.wait(v, n, "score")
                dve.done(v.reduce_max(peak[:], score_ps[:], axis=AX), "peak")
                dve.wait(v, n, "peak")
                if n:
                    acts.wait(v, n - 1, "exp")
                dve.done(v.tensor_scalar(npeak[:], peak[:], -MEM_SCALE, None, ALU.mult), "npeak")
                acts.wait(v, n, "std")
                dve.done(v.reciprocal(std[:, 1:2], std[:, 1:2]), "rstd")
                dve.wait(v, n, "rstd")
                dve.done(v.tensor_scalar(gv[s][:], gv[s][:], mean[:, 0:1], std[:, 1:2],
                                         ALU.subtract, ALU.mult), "norm")
                dve.wait(v, n, "norm")
                dve.done(v.tensor_tensor(gv[s][:], gv[s][:], lng[:], op=ALU.mult), "scaled")
                dve.wait(v, n, "scaled")
                dve.done(v.tensor_tensor(gv[s][:], gv[s][:], lnb[:], op=ALU.add), "vnorm")
                pes.wait(v, n, "spat")
                if n >= 2:
                    v.wait_ge(gstored.sems[s], 16 * (n // 2))
                dve.done(v.tensor_tensor(gout[s][:], uT[s][:], spat_ps[:], op=ALU.mult), "gout")
                acts.wait(v, n, "exp")
                dve.done(v.reciprocal(rden[:], den[:]), "rden")
                dve.wait(v, n, "rden")
                dve.done(v.tensor_tensor(prob[:], prob[:], rden[:].unsqueeze(2).to_broadcast([P, MH, NMEM]),
                                         op=ALU.mult), "prob")
                bg.vector(v, "local", n, tiles)

        @block.scalar
        def _(act):
            acts.open(act)
            for n in range(tiles):
                s = n % 2
                dve.wait(act, n, "npeak")
                if n:
                    pes.wait(act, n - 1, "probT")
                for h in range(MH):
                    last = act.activation(prob[:, h, :], score_ps[:, h, :], ACT.Exp, bias=npeak[:, h:h + 1],
                                          scale=MEM_SCALE, accum_out=den[:, h:h + 1])
                acts.done(last, "exp")
                acts.done(act.activation(std[:, 1:2], std[:, 0:1], ACT.Sqrt), "std")
                pes.wait(act, n, "probT")
                acts.done(act.activation(probT[:], probT_ps[:], ACT.Copy), "probT")
                pes.wait(act, n, "mout")
                mstored.wait_free(act, s)
                acts.done(act.activation(mout[s][:], mout_ps[:], ACT.Copy), "mout")
                acts.wait(act, n, "mout")
                t = tile0 + n
                mstored.start(act, s, dr["mT"][:, :, t * P:(t + 1) * P].rearrange("b p n -> p b n"), mout[s][:])
                bg.scalar(act, "local", n, tiles)
            mstored.wait_all(act)


def attend_prompt(nc, block, sem, dr, bg, g, tile0, tiles):
    NKEY = (tile0 + tiles) * P
    KT = NKEY // P
    ph = Phase(nc, f"at{g}")
    RING = 4
    HR = 3
    with ph.ctx:
        ident = ph.sb("ident", [P, P])
        neg = ph.sb("neg", [P, P])
        bias = ph.sb("bias", [P, HEADS])
        one = ph.sb("one", [P, 1])
        qh = [ph.sb(f"qh{i}", [P, tiles * P]) for i in range(HR)]
        kh = [ph.sb(f"kh{i}", [P, NKEY]) for i in range(HR)]
        vh = [ph.sb(f"vh{i}", [P, KT, P]) for i in range(HR)]
        soft = [ph.sb(f"soft{i}", [P, 512]) for i in range(RING)]
        loga = [ph.sb(f"loga{i}", [P, 512]) for i in range(RING)]
        first = [ph.sb(f"first{i}", [P, 1]) for i in range(2)]
        aT = [ph.sb(f"aT{i}", [P, 512]) for i in range(2)]
        oT = [ph.sb(f"oT{i}", [P, tiles * P]) for i in range(2)]
        z = [ph.ps(f"z{i}", [P, 512]) for i in range(RING)]
        aT_ps = [ph.ps(f"aTp{i}", [P, 512]) for i in range(2)]
        o_ps = [ph.ps(f"o{i}", [P, P]) for i in range(2)]
        const_loaded = sem("const_loaded")
        one_set = sem("one_set")
        head_loaded = [sem(f"head_loaded{i}") for i in range(HR)]
        scored = sem("scored")
        capped = sem("capped")
        logged = sem("logged")
        softened = sem("softened")
        weighed = sem("weighed")
        turned = sem("turned")
        copied = sem("copied")
        summed = sem("summed")
        kept = sem("kept")
        o_stored = Store([sem(f"o_stored{i}") for i in range(2)])
        pieces = []
        for h in range(HEADS):
            for q in range(tiles):
                w = (tile0 + q + 1) * P
                starts = list(range(0, w, 512))[::-1]
                for c in starts:
                    pieces.append((h, q, c, min(512, w - c), c == starts[0], c == 0, h * tiles + q))
        N = len(pieces)
        last_piece = {p[6]: k for k, p in enumerate(pieces) if p[5]}

        @block.sync
        def _(sp):
            for dst, src in ((ident[:], "ident"), (neg[:], "neg"), (bias[:], "sb_bias")):
                sp.dma_start(dst, dr[src]).then_inc(const_loaded, 16)
            for h in range(HEADS):
                s = h % HR
                if h >= HR:
                    sp.wait_ge(summed, last_piece[(h - HR + 1) * tiles - 1] + 1)
                sp.dma_start(qh[s][:], dr["qT"][h, :, tile0 * P:(tile0 + tiles) * P]).then_inc(head_loaded[s], 16)
                sp.dma_start(kh[s][:], dr["kT"][h, :, 0:NKEY]).then_inc(head_loaded[s], 16)
                sp.dma_start(vh[s][:], dr["v"][0:KT, :, h * P:(h + 1) * P]
                             .rearrange("t p c -> p t c")).then_inc(head_loaded[s], 16)

        @block.tensor
        def _(pe):
            pe.wait_ge(const_loaded, 48)

            def score(k):
                h, q, c, n, is_first, _, _ = pieces[k]
                s = h % HR
                if q == 0:
                    pe.wait_ge(head_loaded[s], 48 * (h // HR + 1))
                if k >= RING:
                    pe.wait_ge(softened, 4 * (k - RING) + 4)
                zz, qq = z[k % RING], qh[s][:, q * P:(q + 1) * P]
                rest = n - P if is_first else n
                if rest:
                    last = pe.matmul(zz[:, 0:rest], qq, kh[s][:, c:c + rest], start=True, stop=True)
                if is_first:
                    pe.matmul(zz[:, rest:n], qq, kh[s][:, c + rest:c + n], start=True, stop=False)
                    last = pe.matmul(zz[:, rest:n], ident[:], neg[:], start=False, stop=True)
                last.then_inc(scored, 1)

            def turn(k):
                n = pieces[k][3]
                pe.wait_ge(weighed, k + 1)
                if k >= 2:
                    pe.wait_ge(copied, k - 1)
                for j in range(0, n, P):
                    last = pe.transpose(aT_ps[k % 2][:, j:j + P], loga[k % RING][:, j:j + P], ident[:])
                last.then_inc(turned, 1)

            def gather(k):
                h, q, c, n, is_first, is_last, u = pieces[k]
                pe.wait_ge(copied, k + 1)
                if is_first and u >= 2:
                    pe.wait_ge(kept, u - 1)
                for j in range(0, n, P):
                    last = pe.matmul(o_ps[u % 2][:], vh[h % HR][:, (c + j) // P, :], aT[k % 2][:, j:j + P],
                                     start=is_first and j == 0, stop=is_last and j == n - P)
                last.then_inc(summed, 1)

            for k in range(3):
                score(k)
            for k in range(N):
                if k + 3 < N:
                    score(k + 3)
                turn(k)
                if k:
                    gather(k - 1)
            gather(N - 1)

        @block.vector
        def _(v):
            v.memset(one[:], 1.0).then_inc(one_set, 1)
            v.wait_ge(one_set, 1)
            v.wait_ge(const_loaded, 48)

            def cap(k):
                h, n = pieces[k][0], pieces[k][3]
                v.wait_ge(scored, k + 1)
                if k >= RING:
                    v.wait_ge(softened, 4 * (k - RING) + 2)
                v.tensor_scalar(soft[k % RING][:, 0:n], z[k % RING][:, 0:n], bias[:, h:h + 1], CAP,
                                ALU.add, ALU.min).then_inc(capped, 1)

            def suffix(k):
                h, q, c, n, is_first, _, _ = pieces[k]
                zz, sf, lg = z[k % RING][:, 0:n], soft[k % RING][:, 0:n], loga[k % RING][:, 0:n]
                b = bias[:, h:h + 1]
                v.wait_ge(logged, 2 * k + 2)
                v.scalar_tensor_tensor(out=sf, in0=zz, scalar=b, in1=sf, op0=ALU.add,
                                       op1=ALU.max).then_inc(softened, 1)
                v.wait_ge(softened, 4 * k + 1)
                if k >= RING:
                    v.wait_ge(turned, k - RING + 1)
                v.tensor_tensor_scan(out=lg[:, ::-1], data0=one[:].to_broadcast([P, n]), data1=sf[:, ::-1],
                                     initial=0.0 if is_first else first[(k - 1) % 2][:], op0=ALU.mult,
                                     op1=ALU.add).then_inc(softened, 1)
                v.wait_ge(softened, 4 * k + 2)
                v.tensor_copy(first[k % 2][:], lg[:, 0:1]).then_inc(softened, 1)
                v.wait_ge(softened, 4 * k + 3)
                v.scalar_tensor_tensor(out=lg, in0=zz, scalar=b, in1=lg, op0=ALU.add,
                                       op1=ALU.subtract).then_inc(softened, 1)

            cap(0)
            cap(1)
            for k in range(N):
                if k + 2 < N:
                    cap(k + 2)
                suffix(k)
                bg.vector(v, "prompt", k, N)

        @block.scalar
        def _(act):
            def soften(k):
                sf = soft[k % RING][:, 0:pieces[k][3]]
                act.wait_ge(capped, k + 1)
                act.activation(sf, sf, ACT.Exp).then_inc(logged, 1)
                act.wait_ge(logged, 2 * k + 1)
                act.activation(sf, sf, ACT.Ln, bias=1.0).then_inc(logged, 1)

            def weigh(k):
                lg = loga[k % RING][:, 0:pieces[k][3]]
                act.wait_ge(softened, 4 * k + 4)
                act.activation(lg, lg, ACT.Exp).then_inc(weighed, 1)

            def copy(k):
                n = pieces[k][3]
                act.wait_ge(turned, k + 1)
                if k >= 2:
                    act.wait_ge(summed, k - 1)
                act.activation(aT[k % 2][:, 0:n], aT_ps[k % 2][:, 0:n], ACT.Copy).then_inc(copied, 1)

            def keep(k):
                h, q, _, _, _, is_last, u = pieces[k]
                if not is_last:
                    return
                s = h % 2
                act.wait_ge(summed, k + 1)
                if q == 0:
                    o_stored.wait_free(act, s)
                act.activation(oT[s][:, q * P:(q + 1) * P], o_ps[u % 2][:], ACT.Copy).then_inc(kept, 1)
                if q == tiles - 1:
                    act.wait_ge(kept, u + 1)
                    o_stored.start(act, s, dr["sbT"][h, :, tile0 * P:(tile0 + tiles) * P], oT[s][:])

            soften(0)
            for k in range(N):
                if k + 1 < N:
                    soften(k + 1)
                weigh(k)
                if k >= 1:
                    copy(k - 1)
                if k >= 2:
                    keep(k - 2)
                bg.scalar(act, "prompt", k, N)
            copy(N - 1)
            for k in range(N - 2, N):
                keep(k)
            o_stored.wait_all(act)


def layer_norm_steps(prefix):
    return [prefix + x for x in ("stats", "mean", "var", "rstd", "norm", "scaled", "out")]


def layer_norm(v, dve, acts, n, prefix, x, out, stats, mean, std, gain, offset, unwaited):
    v.bn_stats(stats[:, 0:6], x[:, 0:512])
    dve.done(v.bn_stats(stats[:, 6:12], x[:, 512:1024]), prefix + "stats")
    dve.wait(v, n, prefix + "stats")
    apart(v, unwaited)
    dve.done(v.bn_aggr(mean[:], stats[:]), prefix + "mean")
    dve.wait(v, n, prefix + "mean")
    if not isinstance(n, int) or n:
        acts.wait(v, n - 1, prefix + "root")
    dve.done(v.tensor_scalar(std[:, 0:1], mean[:, 1:2], EPS, None, ALU.add), prefix + "var")
    acts.wait(v, n, prefix + "root")
    dve.done(v.reciprocal(std[:, 1:2], std[:, 1:2]), prefix + "rstd")
    dve.wait(v, n, prefix + "rstd")
    dve.done(v.tensor_scalar(out, x, mean[:, 0:1], std[:, 1:2], ALU.subtract, ALU.mult), prefix + "norm")
    dve.wait(v, n, prefix + "norm")
    dve.done(v.tensor_tensor(out, out, gain[:], op=ALU.mult), prefix + "scaled")
    dve.wait(v, n, prefix + "scaled")
    dve.done(v.tensor_tensor(out, out, offset[:], op=ALU.add), prefix + "out")


def merge(nc, block, sem, gate, dr, bg, g, tile0, tiles):
    T = tiles * P
    t0 = tile0 * P
    cols = slice(t0, t0 + T)
    chunks = [(c, min(512, T - c)) for c in range(0, T, 512)]
    NC = len(chunks)
    ph = Phase(nc, f"mg{g}")
    with ph.ctx:
        zT = ph.sb("zT", [P, KD, T])
        gated_sum(nc, block, sem, dr, bg, g, T, cols, chunks, zT)
        gate.close(block)
        mix_and_norm(nc, block, sem, dr, bg, g, tile0, tiles, zT)
        gate.close(block)
        route(nc, block, sem, dr, bg, g, tile0, tiles, chunks, zT)
        gate.close(block)


def gated_sum(nc, block, sem, dr, bg, g, T, cols, chunks, zT):
    NC = len(chunks)
    ph = Phase(nc, f"gs{g}")
    with ph.ctx:
        bgate = ph.sb("bgate", [P, 24])
        xT = ph.sb("xT", [P, KD, T])
        brT = ph.sb("brT", [P, 16, T])
        wbuf = [ph.sb(f"w{i}", [P, KD, GATE_W]) for i in range(4)]
        gates = [ph.sb(f"gate{i}", [P, 512]) for i in range(2)]
        term = ph.sb("term", [P, 512])
        gate_ps = [ph.ps(f"gp{i}", [P, 512]) for i in range(2)]
        branch_ps = [ph.ps(f"bp{i}", [P, 512]) for i in range(2)]
        bias_loaded = sem("bias_loaded")
        act_loaded = sem("act_loaded")
        w_loaded = [sem(f"gw_loaded{i}") for i in range(4)]
        gate_ready, gate_done = sem("gate_ready"), sem("gate_done")
        branch_ready, branch_done = sem("branch_ready"), sem("branch_done")
        term_done = sem("term_done")
        pairs = [(qt, b) for qt in range(4) for b in range(3)]
        KB = {0: GG, 1: HEADS, 2: MH}
        KOFF = {0: 0, 1: GG, 2: GG + HEADS}
        jobs = [(p, mf, c) for p in range(len(pairs)) for mf in range(2) for c in range(NC)]
        per_pair = 2 * NC

        @block.sync
        def _(sp):
            sp.dma_start(bgate[:], dr["b_gate"]).then_inc(bias_loaded, 16)
            sp.dma_start(xT[:], dr["xT"][:, :, cols]).then_inc(act_loaded, 16)

            def load(p):
                qt, b = pairs[p]
                s = 2 * (p % 2)
                sp.dma_start(wbuf[s][:], dr["w_gate"][4 * b + qt]).then_inc(w_loaded[s], 16)
                sp.dma_start(wbuf[s + 1][:, 0:KB[b], :], dr[f"w_br{b}"][qt]).then_inc(w_loaded[s + 1], 16)

            load(0)
            sp.dma_start(brT[:, 0:GG, :], dr["gT"][:, :, cols].rearrange("b p n -> p b n")).then_inc(act_loaded, 16)
            sp.dma_start(brT[:, GG:GG + HEADS, :], dr["sbT"][:, :, cols].rearrange("b p n -> p b n")).then_inc(act_loaded, 16)
            sp.dma_start(brT[:, GG + HEADS:, :], dr["mT"][:, :, cols].rearrange("b p n -> p b n")).then_inc(act_loaded, 16)
            load(1)
            for p in range(2, len(pairs)):
                sp.wait_ge(branch_ready, per_pair * (p - 1))
                load(p)

        @block.tensor
        def _(pe):
            pe.wait_ge(act_loaded, 64)
            for j, (p, mf, c) in enumerate(jobs):
                b = pairs[p][1]
                c0, n = chunks[c]
                s = 2 * (p % 2)
                if mf == 0 and c == 0:
                    pe.wait_ge(w_loaded[s], 16 * (p // 2 + 1))
                    pe.wait_ge(w_loaded[s + 1], 16 * (p // 2 + 1))
                if j >= 2:
                    pe.wait_ge(gate_done, j - 1)
                for k in range(KD):
                    last = pe.matmul(gate_ps[j % 2][:, 0:n], wbuf[s][:, k, mf * P:(mf + 1) * P],
                                     xT[:, k, c0:c0 + n], start=k == 0, stop=k == KD - 1)
                last.then_inc(gate_ready, 1)
                if j >= 2:
                    pe.wait_ge(branch_done, j - 1)
                for k in range(KB[b]):
                    last = pe.matmul(branch_ps[j % 2][:, 0:n], wbuf[s + 1][:, k, mf * P:(mf + 1) * P],
                                     brT[:, KOFF[b] + k, c0:c0 + n], start=k == 0, stop=k == KB[b] - 1)
                last.then_inc(branch_ready, 1)

        @block.scalar
        def _(act):
            act.wait_ge(bias_loaded, 16)
            for j, (p, mf, c) in enumerate(jobs):
                qt, b = pairs[p]
                n = chunks[c][1]
                col = b * KD + qt * 2 + mf
                act.wait_ge(gate_ready, j + 1)
                if j >= 2:
                    act.wait_ge(branch_done, j - 1)
                act.activation(gates[j % 2][:, 0:n], gate_ps[j % 2][:, 0:n], ACT.Sigmoid,
                               bias=bgate[:, col:col + 1]).then_inc(gate_done, 1)
                bg.scalar(act, "sum", j, len(jobs))

        @block.vector
        def _(v):
            terms = 0
            for j, (p, mf, c) in enumerate(jobs):
                qt, b = pairs[p]
                c0, n = chunks[c]
                dst = zT[:, 2 * qt + mf, c0:c0 + n]
                v.wait_ge(gate_done, j + 1)
                v.wait_ge(branch_ready, j + 1)
                if b == 0:
                    v.tensor_tensor(dst, gates[j % 2][:, 0:n], branch_ps[j % 2][:, 0:n], op=ALU.mult)\
                        .then_inc(branch_done, 1)
                else:
                    terms += 1
                    v.wait_ge(branch_done, j)
                    v.tensor_tensor(term[:, 0:n], gates[j % 2][:, 0:n], branch_ps[j % 2][:, 0:n], op=ALU.mult)\
                        .then_inc(term_done, 1)
                    v.wait_ge(term_done, terms)
                    v.tensor_tensor(dst, dst, term[:, 0:n], op=ALU.add).then_inc(branch_done, 1)
                bg.vector(v, "sum", j, len(jobs))


def mix_and_norm(nc, block, sem, dr, bg, g, tile0, tiles, zT):
    ph = Phase(nc, f"mx{g}")
    with ph.ctx:
        ident = ph.sb("ident", [P, P])
        lng = ph.sb("lng", [P, D])
        lnb = ph.sb("lnb", [P, D])
        w = ph.sb("w", [P, 2, KD, 512])
        x1 = ph.sb("x1", [P, tiles, D])
        stats = ph.sb("stats", [P, 12])
        mean = ph.sb("mean", [P, 2])
        std = ph.sb("std", [P, 2])
        mix_ps = [ph.ps(f"mp{i}", [P, 512]) for i in range(4)]
        turn_ps = [ph.ps(f"tp{i}", [P, 512]) for i in range(2)]
        const_loaded = sem("ln1_loaded")
        w_loaded = sem("wo_loaded")
        x_loaded = sem("x_loaded")
        mix_ready, mix_done = sem("mix_ready"), sem("mix_done")
        turned, turn_kept = sem("turned"), sem("turn_kept")
        x1_stored = sem("x1_stored")
        dve = Steps(sem("ln_dve"), layer_norm_steps(""))
        acts = Steps(sem("ln_act"), ["root"])

        @block.sync
        def _(sp):
            for c in range(2):
                sp.dma_start(w[:, c], dr["w_out"][c]).then_inc(w_loaded, 16)
            sp.dma_start(x1[:], dr["x"][tile0:tile0 + tiles].rearrange("t p c -> p t c")).then_inc(x_loaded, 16)
            for dst, src in ((ident[:], "ident"), (lng[:], "ln1_g"), (lnb[:], "ln1_b")):
                sp.dma_start(dst, dr[src]).then_inc(const_loaded, 16)
            for n in range(tiles):
                dve.wait(sp, n, "out")
                sp.dma_start(dr["x1"][tile0 + n], x1[:, n, :]).then_inc(x1_stored, 16)
            sp.wait_ge(x1_stored, 16 * tiles)

        @block.tensor
        def _(pe):
            pe.wait_ge(w_loaded, 32)
            pe.wait_ge(const_loaded, 48)

            def turn(n):
                dve.wait(pe, n, "out")
                for hf in range(2):
                    if n:
                        pe.wait_ge(turn_kept, 2 * n + hf - 1)
                    for k in range(4):
                        kk = 4 * hf + k
                        last = pe.transpose(turn_ps[hf][:, k * P:(k + 1) * P], x1[:, n, kk * P:(kk + 1) * P], ident[:])
                    last.then_inc(turned, 1)

            for n in range(tiles):
                for c in range(2):
                    j = 2 * n + c
                    if j >= 4:
                        pe.wait_ge(mix_done, j - 3)
                    for k in range(KD):
                        last = pe.matmul(mix_ps[j % 4][:], zT[:, k, n * P:(n + 1) * P], w[:, c, k, :],
                                         start=k == 0, stop=k == KD - 1)
                    last.then_inc(mix_ready, 1)
                if n:
                    turn(n - 1)
            turn(tiles - 1)

        @block.scalar
        def _(act):
            acts.open(act)
            for n in range(tiles):
                dve.wait(act, n, "var")
                acts.done(act.activation(std[:, 1:2], std[:, 0:1], ACT.Sqrt), "root")
                bg.scalar(act, "mix", n, tiles)
                for hf in range(2):
                    act.wait_ge(turned, 2 * n + hf + 1)
                    act.activation(zT[:, 4 * hf:4 * hf + 4, n * P:(n + 1) * P],
                                   turn_ps[hf][:].rearrange("p (k n) -> p k n", k=4), ACT.Copy).then_inc(turn_kept, 1)

        @block.vector
        def _(v):
            dve.open(v)
            v.wait_ge(x_loaded, 16)
            v.wait_ge(const_loaded, 48)
            for n in range(tiles):
                for c in range(2):
                    j = 2 * n + c
                    v.wait_ge(mix_ready, j + 1)
                    dst = x1[:, n, c * 512:(c + 1) * 512]
                    v.scalar_tensor_tensor(out=dst, in0=dst, scalar=ALPHA, in1=mix_ps[j % 4][:], op0=ALU.mult,
                                           op1=ALU.add).then_inc(mix_done, 1)
                v.wait_ge(mix_done, 2 * n + 2)
                layer_norm(v, dve, acts, n, "", x1[:, n, :], x1[:, n, :], stats, mean, std, lng, lnb, dr["unwaited"])
                bg.vector(v, "mix", n, tiles)


def route(nc, block, sem, dr, bg, g, tile0, tiles, chunks, xT):
    T = tiles * P
    NC = len(chunks)
    ph = Phase(nc, f"rt{g}")
    with ph.ctx:
        keysT = ph.sb("keysT", [P, 2 * PH, NK])
        queries = ph.sb("queries", [P, 2 * PH, T])
        wbuf = [ph.sb(f"w{i}", [P, KD, GATE_W]) for i in range(4)]
        stage = [ph.sb(f"st{i}", [P, 2 * PH * NK]) for i in range(2)]
        bank = [ph.ps(f"b{i}", [P, 512]) for i in range(4)]
        score_ps = ph.ps("score", [P, 2 * PH * NK])
        keys_loaded = sem("keys_loaded")
        w_loaded = [sem(f"wq_loaded{i}") for i in range(4)]
        query_ready, query_kept = sem("query_ready"), sem("query_kept")
        scored, score_kept = sem("scored"), sem("score_kept")
        s_stored = Store([sem(f"s_stored{i}") for i in range(2)])
        per_unit = 2 * NC
        jobs = [(u, b, c) for u in range(8) for b in range(2) for c in range(NC)]

        @block.sync
        def _(sp):
            sp.dma_start(keysT[:], dr["keysT"]).then_inc(keys_loaded, 16)
            for u in range(8):
                if u >= 4:
                    sp.wait_ge(query_ready, per_unit * (u - 3))
                sp.dma_start(wbuf[u % 4][:], dr["w_q"][u]).then_inc(w_loaded[u % 4], 16)

        @block.tensor
        def _(pe):
            for j, (u, b, c) in enumerate(jobs):
                c0, n = chunks[c]
                if b == 0 and c == 0:
                    pe.wait_ge(w_loaded[u % 4], 16 * (u // 4 + 1))
                if j >= 4:
                    pe.wait_ge(query_kept, j - 3)
                for k in range(KD):
                    last = pe.matmul(bank[j % 4][:, 0:n], wbuf[u % 4][:, k, b * P:(b + 1) * P],
                                     xT[:, k, c0:c0 + n], start=k == 0, stop=k == KD - 1)
                last.then_inc(query_ready, 1)
            pe.wait_ge(keys_loaded, 16)
            pe.wait_ge(query_kept, len(jobs))
            for n in range(tiles):
                if n:
                    pe.wait_ge(score_kept, n)
                for hp in range(2 * PH):
                    last = pe.matmul(score_ps[:, hp * NK:(hp + 1) * NK], queries[:, hp, n * P:(n + 1) * P],
                                     keysT[:, hp, :], start=True, stop=True)
                last.then_inc(scored, 1)

        @block.scalar
        def _(act):
            for j, (u, b, c) in enumerate(jobs):
                c0, n = chunks[c]
                act.wait_ge(query_ready, j + 1)
                act.activation(queries[:, 2 * u + b, c0:c0 + n], bank[j % 4][:, 0:n], ACT.Copy).then_inc(query_kept, 1)
                bg.scalar(act, "route", j, len(jobs))
            for n in range(tiles):
                act.wait_ge(scored, n + 1)
                s_stored.wait_free(act, n % 2)
                act.activation(stage[n % 2][:], score_ps[:], ACT.Copy).then_inc(score_kept, 1)
                act.wait_ge(score_kept, n + 1)
                s_stored.start(act, n % 2, dr["scores"][tile0 + n], stage[n % 2][:])
            s_stored.wait_all(act)

        @block.vector
        def _(v):
            for j in range(len(jobs)):
                bg.vector(v, "route", j, len(jobs))


def attend_sample(nc, block, sem, dr, bg):
    R = HEADS * NQ
    MR = MH * NQ
    CW = CHUNK_PAGES * P
    NCH = PAGES // CHUNK_PAGES
    ph = Phase(nc, "sa")
    with ph.ctx:
        ident = ph.sb("ident", [P, P])
        sel = ph.sb("sel", [R, HEADS, R])
        selm = ph.sb("selm", [MR, MH, MR])
        negn = ph.sb("negn", [R, NQ])
        bias = ph.sb("bias", [R, 1])
        one = ph.sb("one", [P, 1])
        table = ph.sb("table", [1, NSEQ * PAGES], I32)
        q = ph.sb("q", [P, HEADS, R])
        kn = ph.sb("kn", [P, HEADS, R])
        qm = ph.sb("qm", [P, MH, R])
        qpad = ph.sb("qpad", [P, HEADS * (R + NQ)])
        qmpad = ph.sb("qmpad", [P, MH * (MR + NQ)])
        vn = ph.sb("vn", [NQ, HEADS * P])
        mk = ph.sb("mk", [P, MH, NMEM])
        mv = ph.sb("mv", [P, 2, 512])
        kc = [ph.sb(f"kc{i}", [P, CHUNK_PAGES, HEADS * P]) for i in range(2)]
        vc = [ph.sb(f"vc{i}", [P, CHUNK_PAGES, HEADS * P]) for i in range(2)]
        soft = [ph.sb(f"soft{i}", [R, CW]) for i in range(2)]
        loga = [ph.sb(f"loga{i}", [R, CW]) for i in range(2)]
        first = [ph.sb(f"first{i}", [R, 1]) for i in range(2)]
        aT = [ph.sb(f"aT{i}", [P, CHUNK_PAGES * R]) for i in range(2)]
        osb = ph.sb("osb", [R, HEADS * P])
        so = ph.sb("so", [P, HEADS, P])
        smo = ph.sb("smo", [P, MH, P])
        prob = ph.sb("prob", [MR, NMEM])
        probT = ph.sb("probT", [P, 2, MR])
        om = ph.sb("om", [MR, 512])
        peak = ph.sb("peak", [MR, 1])
        npeak = ph.sb("npeak", [MR, 1])
        den = ph.sb("den", [MR, 1])
        rden = ph.sb("rden", [MR, 1])
        z = [ph.ps(f"z{i}", [R, CW]) for i in range(2)]
        aT_ps = [ph.ps(f"aTp{i}", [P, CHUNK_PAGES * R]) for i in range(2)]
        o_ps = ph.ps("o", [R, HEADS * P])
        fin_ps = ph.ps("fin", [P, 512])
        m_ps = ph.ps("m", [P, 512])
        const_loaded = sem("const_loaded")
        cleared = sem("cleared")
        mem_loaded = sem("mem_loaded")
        vn_loaded = sem("vn_loaded")
        k_loaded = [sem(f"k_loaded{i}") for i in range(2)]
        v_loaded = [sem(f"v_loaded{i}") for i in range(2)]
        o_stored = sem("o_stored")
        blocks = ["n"] + [str(c) for c in range(NCH)]
        per_seq = 1 + 2 * len(blocks)
        places = NSEQ * per_seq
        dve = Steps(sem("dve_steps"), ["pads", "peak", "npeak", "rden", "prob"] +
                    [f"{b}_{x}" for b in blocks for x in ("cap", "sp", "cum", "first", "log")])
        acts = Steps(sem("act_steps"), ["mexp", "mprobT", "mom", "mout"] +
                     [f"{b}_{x}" for b in blocks for x in ("exp", "ln", "a", "aT")] + ["osb", "out"])
        pes = Steps(sem("pe_steps"), ["mscore", "mprobT", "mom", "mout", "n_z"] +
                    [x for c in range(NCH) for x in (f"{c}_z", f"{blocks[c]}_aT", f"{blocks[c]}_o")] +
                    [f"{NCH - 1}_aT", f"{NCH - 1}_o", "out"])

        @block.sync
        def _(sp):
            c0 = PT * P
            for dst, src in ((ident[:], dr["ident"]), (sel[:], dr["sel"]), (selm[:], dr["selm"]),
                             (negn[:], dr["neg_new"]), (bias[:], dr["sb_bias_rows"]), (table[:], dr["table"]),
                             (q[:], dr["qT"][:, :, c0:c0 + R].rearrange("h p n -> p h n")),
                             (kn[:], dr["kT"][:, :, c0:c0 + R].rearrange("h p n -> p h n")),
                             (qm[:], dr["qmT"][:, :, c0:c0 + R].rearrange("h p n -> p h n"))):
                sp.dma_start(dst, src).then_inc(const_loaded, 16)
            sp.wait_ge(const_loaded, 16 * 9)
            with sp.Fori(0, NSEQ) as i:
                acts.wait(sp, i - 1, "mout")
                sp.dma_start(mk[:], dr["mem_k"][bass.ds(i, 1)].rearrange("a p h m -> p (a h) m")).then_inc(mem_loaded, 16)
                sp.dma_start(mv[:], dr["mem_v"][bass.ds(i, 1)].rearrange("a p m c -> p (a m) c")).then_inc(mem_loaded, 16)
                pes.wait(sp, i - 1, "n_o")
                sp.dma_start(vn[:], dr["v"][PT, bass.ds(i * NQ, NQ), :]).then_inc(vn_loaded, 16)
                for c in range(NCH):
                    s = c % 2
                    before = (i, c - 2) if c >= 2 else (i - 1, c + NCH - 2)
                    pes.wait(sp, before[0], f"{before[1]}_z")
                    apart(sp, dr["unwaited"])
                    for k in range(CHUNK_PAGES):
                        page = PAGES - CHUNK_PAGES * (c + 1) + k
                        reg = sp.value_load(table[0:1, bass.ds(i * PAGES + page, 1)], min_val=0,
                                            max_val=dr["cache_k"].shape[0] - 1)
                        sp.dma_start(kc[s][:, k, :], dr["cache_k"][bass.ds(reg, 1)]
                                     .rearrange("a p c -> p (a c)")).then_inc(k_loaded[s], 16)
                    pes.wait(sp, before[0], f"{before[1]}_o")
                    apart(sp, dr["unwaited"])
                    for k in range(CHUNK_PAGES):
                        page = PAGES - CHUNK_PAGES * (c + 1) + k
                        reg = sp.value_load(table[0:1, bass.ds(i * PAGES + page, 1)], min_val=0,
                                            max_val=dr["cache_v"].shape[0] - 1)
                        sp.dma_start(vc[s][:, k, :], dr["cache_v"][bass.ds(reg, 1)]
                                     .rearrange("a p c -> p (a c)")).then_inc(v_loaded[s], 16)

        @block.tensor
        def _(pe):
            pe.wait_ge(const_loaded, 16 * 9)
            pes.open(pe)
            with pe.Fori(0, NSEQ) as i:
                dve.wait(pe, i, "pads")
                pe.wait_ge(mem_loaded, 32 * i + 32)
                for h in range(MH):
                    last = pe.matmul(m_ps[0:MR, 0:NMEM], qmpad[:, h * MR:(h + 1) * MR], mk[:, h, :],
                                     start=h == 0, stop=h == MH - 1)
                pes.done(last, "mscore")
                dve.wait(pe, i, "prob")
                apart(pe, dr["unwaited"])
                for m in range(2):
                    last = pe.transpose(m_ps[:, m * MR:(m + 1) * MR], prob[:, m * P:(m + 1) * P], ident[0:MR, 0:MR])
                pes.done(last, "mprobT")
                acts.wait(pe, i, "mprobT")
                for m in range(2):
                    last = pe.matmul(m_ps[0:MR, :], probT[:, m, :], mv[:, m, :], start=m == 0, stop=m == 1)
                pes.done(last, "mom")
                acts.wait(pe, i, "mom")
                for h in range(MH):
                    last = pe.matmul(m_ps[:, 0:MR], om[:, h * P:(h + 1) * P], selm[:, h, :],
                                     start=h == 0, stop=h == MH - 1)
                pes.done(last, "mout")

                for h in range(HEADS):
                    pe.matmul(fin_ps[0:R, 0:NQ], qpad[:, h * R:(h + 1) * R], kn[:, h, bass.ds(i * NQ, NQ)],
                              start=h == 0, stop=False)
                pes.done(pe.matmul(fin_ps[0:R, 0:NQ], ident[0:R, 0:R], negn[:], start=False, stop=True), "n_z")

                def turn_and_sum(b):
                    acts.wait(pe, i, f"{b}_a")
                    apart(pe, dr["unwaited"])
                    if b == "n":
                        last = pe.transpose(aT_ps[1][0:NQ, 0:R], loga[1][:, 0:NQ], ident[0:R, 0:R])
                        pes.done(last, "n_aT")
                        acts.wait(pe, i, "n_aT")
                        pe.wait_ge(vn_loaded, 16 * i + 16)
                        acts.wait(pe, i - 1, "osb")
                        for hf in range(2):
                            last = pe.matmul(o_ps[:, hf * 512:(hf + 1) * 512], aT[1][0:NQ, 0:R],
                                             vn[:, hf * 512:(hf + 1) * 512], start=True, stop=False)
                        pes.done(last, "n_o")
                        return
                    c = int(b)
                    s = c % 2
                    for k in range(CHUNK_PAGES):
                        last = pe.transpose(aT_ps[s][:, k * R:(k + 1) * R], loga[s][:, k * P:(k + 1) * P],
                                            ident[0:R, 0:R])
                    pes.done(last, f"{b}_aT")
                    acts.wait(pe, i, f"{b}_aT")
                    pe.wait_ge(v_loaded[s], 64 * (2 * i + c // 2) + 64)
                    for k in range(CHUNK_PAGES):
                        for hf in range(2):
                            last = pe.matmul(o_ps[:, hf * 512:(hf + 1) * 512], aT[s][:, k * R:(k + 1) * R],
                                             vc[s][:, k, hf * 512:(hf + 1) * 512], start=False,
                                             stop=c == NCH - 1 and k == CHUNK_PAGES - 1)
                    pes.done(last, f"{b}_o")

                for c in range(NCH):
                    s = c % 2
                    pe.wait_ge(k_loaded[s], 64 * (2 * i + c // 2) + 64)
                    if c >= 2:
                        dve.wait(pe, i, f"{c - 2}_log")
                    for h in range(HEADS):
                        last = pe.matmul(z[s][:], qpad[:, h * R:(h + 1) * R], kc[s][:, :, h * P:(h + 1) * P],
                                         start=h == 0, stop=h == HEADS - 1)
                    pes.done(last, f"{c}_z")
                    turn_and_sum(blocks[c])
                turn_and_sum(blocks[NCH])
                acts.wait(pe, i, "osb")
                for h in range(HEADS):
                    last = pe.matmul(fin_ps[:, 0:R], osb[:, h * P:(h + 1) * P], sel[:, h, :], start=h == 0,
                                     stop=h == HEADS - 1)
                pes.done(last, "out")

        @block.vector
        def _(v):
            v.memset(one[:], 1.0).then_inc(cleared, 1)
            v.memset(qpad[:], 0.0).then_inc(cleared, 1)
            v.memset(qmpad[:], 0.0).then_inc(cleared, 1)
            v.memset(so[:], 0.0).then_inc(cleared, 1)
            v.memset(smo[:], 0.0).then_inc(cleared, 1)
            v.wait_ge(cleared, 5)
            v.wait_ge(const_loaded, 16 * 9)
            dve.open(v)
            for i in range(NSEQ):
                pes.wait(v, i - 1, "out")
                v.tensor_copy(qpad[:].rearrange("p (h c) -> p h c", c=R + NQ)[:, :, 0:NQ],
                              q[:, :, bass.ds(i * NQ, NQ)])
                dve.done(v.tensor_copy(qmpad[:].rearrange("p (h c) -> p h c", c=MR + NQ)[:, :, 0:NQ],
                                       qm[:, :, bass.ds(i * NQ, NQ)]), "pads")
                bg.vector(v, "sample", i * per_seq, places)
                pes.wait(v, i, "mscore")
                dve.done(v.reduce_max(peak[:], m_ps[0:MR, 0:NMEM], axis=AX), "peak")
                dve.wait(v, i, "peak")
                dve.done(v.tensor_scalar(npeak[:], peak[:], -MEM_SCALE, None, ALU.mult), "npeak")
                acts.wait(v, i, "mexp")
                dve.done(v.reciprocal(rden[:], den[:]), "rden")
                dve.wait(v, i, "rden")
                dve.done(v.tensor_scalar(prob[:], prob[:], rden[:], None, ALU.mult), "prob")
                for at, b in enumerate(blocks):
                    at = i * per_seq + 1 + 2 * at
                    s = 1 if b == "n" else int(b) % 2
                    w = NQ if b == "n" else CW
                    zz = fin_ps[0:R, 0:NQ] if b == "n" else z[s][:]
                    sf, lg = soft[s][:, 0:w], loga[s][:, 0:w]
                    prev = None if b == "n" else first[1 - s]
                    pes.wait(v, i, f"{b}_z")
                    dve.done(v.tensor_scalar(sf, zz, bias[:], CAP, ALU.add, ALU.min), f"{b}_cap")
                    bg.vector(v, "sample", at, places)
                    acts.wait(v, i, f"{b}_ln")
                    dve.done(v.scalar_tensor_tensor(out=sf, in0=zz, scalar=bias[:], in1=sf, op0=ALU.add,
                                                    op1=ALU.max), f"{b}_sp")
                    dve.wait(v, i, f"{b}_sp")
                    if b not in ("n", "0"):
                        pes.wait(v, i, "n_aT" if b == "1" else f"{int(b) - 2}_aT")
                    dve.done(v.tensor_tensor_scan(out=lg[:, ::-1], data0=one[0:R, :].to_broadcast([R, w]),
                                                  data1=sf[:, ::-1], initial=0.0 if prev is None else prev[:],
                                                  op0=ALU.mult, op1=ALU.add), f"{b}_cum")
                    dve.wait(v, i, f"{b}_cum")
                    dve.done(v.tensor_copy(first[s][:], lg[:, 0:1]), f"{b}_first")
                    dve.wait(v, i, f"{b}_first")
                    dve.done(v.scalar_tensor_tensor(out=lg, in0=zz, scalar=bias[:], in1=lg, op0=ALU.add,
                                                    op1=ALU.subtract), f"{b}_log")
                    bg.vector(v, "sample", at + 1, places)

        @block.scalar
        def _(act):
            act.wait_ge(cleared, 5)
            act.wait_ge(const_loaded, 16 * 9)
            acts.open(act)
            for i in range(NSEQ):
                bg.scalar(act, "sample", i * per_seq, places)
                dve.wait(act, i, "npeak")
                acts.done(act.activation(prob[:], m_ps[0:MR, 0:NMEM], ACT.Exp, bias=npeak[:], scale=MEM_SCALE,
                                         accum_out=den[:]), "mexp")
                pes.wait(act, i, "mprobT")
                acts.done(act.activation(probT[:].rearrange("p m r -> p (m r)"), m_ps[:, 0:2 * MR], ACT.Copy), "mprobT")
                pes.wait(act, i, "mom")
                acts.done(act.activation(om[:], m_ps[0:MR, :], ACT.Copy), "mom")
                pes.wait(act, i, "mout")
                acts.done(act.activation(smo[:, :, bass.ds(i * NQ, NQ)],
                                         m_ps[:, 0:MR].rearrange("p (h q) -> p h q", h=MH), ACT.Copy), "mout")
                for at, b in enumerate(blocks):
                    at = i * per_seq + 1 + 2 * at
                    s = 1 if b == "n" else int(b) % 2
                    w = NQ if b == "n" else CW
                    sf, lg = soft[s][:, 0:w], loga[s][:, 0:w]
                    dve.wait(act, i, f"{b}_cap")
                    acts.done(act.activation(sf, sf, ACT.Exp), f"{b}_exp")
                    acts.wait(act, i, f"{b}_exp")
                    acts.done(act.activation(sf, sf, ACT.Ln, bias=1.0), f"{b}_ln")
                    bg.scalar(act, "sample", at, places)
                    dve.wait(act, i, f"{b}_log")
                    acts.done(act.activation(lg, lg, ACT.Exp), f"{b}_a")
                    pes.wait(act, i, f"{b}_aT")
                    if b == "n":
                        acts.done(act.activation(aT[1][0:NQ, 0:R], aT_ps[1][0:NQ, 0:R], ACT.Copy), "n_aT")
                    else:
                        acts.done(act.activation(aT[s][:], aT_ps[s][:], ACT.Copy), f"{b}_aT")
                    bg.scalar(act, "sample", at + 1, places)
                pes.wait(act, i, f"{NCH - 1}_o")
                acts.done(act.activation(osb[:], o_ps[:], ACT.Copy), "osb")
                pes.wait(act, i, "out")
                acts.done(act.activation(so[:, :, bass.ds(i * NQ, NQ)],
                                         fin_ps[:, 0:R].rearrange("p (h q) -> p h q", h=HEADS), ACT.Copy), "out")
            acts.wait(act, NSEQ - 1, "out")
            c0 = PT * P
            act.dma_start(dr["sbT"][:, :, c0:c0 + P].rearrange("h p n -> p h n"), so[:]).then_inc(o_stored, 16)
            act.dma_start(dr["mT"][:, :, c0:c0 + P].rearrange("h p n -> p h n"), smo[:]).then_inc(o_stored, 16)
            act.wait_ge(o_stored, 32)


class TopK:

    def __init__(self, peer, v, tile):
        self.peer, self.v, self.tile, self.n = peer, v, tile, 0

    def round(self, *instructions):
        for ins in instructions[:-1]:
            ins()
        instructions[-1]().then_inc(self.peer.picked, 1)
        self.n += 1
        self.v.wait_ge(self.peer.picked, self.peer.KSTEP * self.tile + self.n)
        apart(self.v, self.peer.dr["unwaited"])

    def keys(self, h):
        v, s = self.v, (self.peer.score[:, 2 * h, :], self.peer.score[:, 2 * h + 1, :])
        b = lambda p, lo: self.peer.best[:, h, p, lo:lo + 8]
        bi = lambda p, lo: self.peer.besti[:, h, p, lo:lo + 8]
        if h == 0:
            v.wait_ge(self.peer.score_loaded, 16 * self.tile + 16)
            apart(v, self.peer.dr["unwaited"])
        self.round(*[lambda p=p: v.max(b(p, 0), s[p]) for p in range(2)])
        self.round(*[lambda p=p: v.max_index(bi(p, 0), b(p, 0), s[p]) for p in range(2)])
        self.round(*[lambda p=p: v.match_replace(s[p], b(p, 0), s[p], NEG) for p in range(2)])
        self.round(*[lambda p=p: v.max(b(p, 8), s[p]) for p in range(2)])
        self.round(*[lambda p=p: v.max_index(bi(p, 8), b(p, 8), s[p]) for p in range(2)])

    def sums(self):
        v = self.v
        self.round(lambda: v.tensor_tensor(
            self.peer.cand[:], self.peer.best[:, :, 0, :].unsqueeze(3).to_broadcast([P, PH, TOPK, TOPK]),
            self.peer.best[:, :, 1, :].unsqueeze(2).to_broadcast([P, PH, TOPK, TOPK]), op=ALU.add))

    def pairs(self, h0):
        v, hs = self.v, (h0, h0 + 1)
        c = lambda h: self.peer.cand[:, h].rearrange("p a b -> p (a b)")
        self.round(*[lambda h=h: v.max(self.peer.top[:, h, 0:8], c(h)) for h in hs])
        self.round(*[lambda h=h: v.max_index(self.peer.topi[:, h, 0:8], self.peer.top[:, h, 0:8], c(h)) for h in hs])
        self.round(*[lambda h=h: v.match_replace(c(h), self.peer.top[:, h, 0:8], c(h), NEG) for h in hs])
        self.round(*[lambda h=h: v.max(self.peer.top[:, h, 8:16], c(h)) for h in hs])
        self.round(*[lambda h=h: v.max_index(self.peer.topi[:, h, 8:16], self.peer.top[:, h, 8:16], c(h)) for h in hs])

    def experts(self):
        v = self.v
        wide = [P, PH, TOPK, TOPK]
        self.round(lambda: v.tensor_scalar(self.peer.half[0][:], self.peer.topi[:], 4, None, ALU.logical_shift_right),
                   lambda: v.tensor_scalar(self.peer.half[1][:], self.peer.topi[:], 15, None, ALU.bitwise_and),
                   lambda: v.tensor_copy(self.peer.bestf[:], self.peer.besti[:]))
        self.round(lambda: v.tensor_copy(self.peer.halff[0][:], self.peer.half[0][:]), lambda: v.tensor_copy(self.peer.halff[1][:], self.peer.half[1][:]))
        for p in range(2):
            self.round(lambda: v.tensor_tensor(
                self.peer.cand[:], self.peer.halff[p][:].unsqueeze(3).to_broadcast(wide),
                self.peer.iota[:].unsqueeze(1).unsqueeze(1).to_broadcast(wide), op=ALU.is_equal))
            self.round(lambda: v.tensor_tensor(
                self.peer.cand[:], self.peer.cand[:], self.peer.bestf[:, :, p, :].unsqueeze(2).to_broadcast(wide), op=ALU.mult))
            self.round(lambda: v.reduce_sum(self.peer.part[p][:], self.peer.cand[:], axis=AX))
        if not isinstance(self.tile, int):
            v.wait_ge(self.peer.indexed, self.tile)
        self.round(lambda: v.scalar_tensor_tensor(
            out=self.peer.index_next[:].rearrange("p (h k) -> p h k", h=PH), in0=self.peer.part[0][:], scalar=float(NK),
            in1=self.peer.part[1][:], op0=ALU.mult, op1=ALU.add))

    def finish(self):
        assert self.n == self.peer.KSTEP, (self.n, self.peer.KSTEP)


class Peer:

    KSTEP = PH * 5 + 1 + PH // 2 * 5 + 9
    SH = 4
    BLOCK = 4
    LATE = UNITS // 2
    PARTS = [("keys", h) for h in range(PH)] + [("sums",)] + [("pairs", h) for h in range(0, PH, 2)] + \
        [("experts",), ("share",), ("total",)]
    EARLY_PART = dict(zip(range(1, UNITS, 2), PARTS))
    LATE_PART = dict(zip(range(LATE, UNITS), PARTS))

    def __init__(self, sem, dr, ph, n_tiles, late):
        self.dr, self.n_tiles, self.late = dr, n_tiles, late
        TKN = PH * TOPK
        self.lng = ph.sb("lng", [P, D])
        self.lnb = ph.sb("lnb", [P, D])
        self.iota = ph.sb("iota", [P, TOPK])
        self.score = ph.sb("score", [P, 2 * PH, NK])
        self.cand = ph.sb("cand", [P, PH, TOPK, TOPK])
        self.best = ph.sb("best", [P, PH, 2, TOPK])
        self.besti = ph.sb("besti", [P, PH, 2, TOPK], U32)
        self.bestf = ph.sb("bestf", [P, PH, 2, TOPK])
        self.top = ph.sb("top", [P, PH, TOPK])
        self.topi = ph.sb("topi", [P, PH, TOPK], U32)
        self.half = [ph.sb(f"half{i}", [P, PH, TOPK], U32) for i in range(2)]
        self.halff = [ph.sb(f"halff{i}", [P, PH, TOPK]) for i in range(2)]
        self.part = [ph.sb(f"part{i}", [P, PH, TOPK]) for i in range(2)]
        self.index_next = ph.sb("index_next", [P, TKN], U32)
        self.index = ph.sb("index", [P, TKN], U32)
        self.staged = [ph.sb(f"staged{i}", [P, ROWS], U32) for i in range(self.BLOCK)]
        self.share_next = ph.sb("share_next", [P, PH, TOPK])
        self.share = ph.sb("share", [P, TKN])
        self.total = ph.sb("total", [P, PH])
        self.x1_next = ph.sb("x1_next", [P, D])
        self.x1 = ph.sb("x1", [P, D])
        self.y = ph.sb("y", [P, D])
        self.out = ph.sb("out", [P, D])
        self.hid = ph.sb("hid", [P, TKN])
        self.coef = ph.sb("coef", [P, TKN])
        self.urow = [ph.sb(f"urow{i}", [P, D]) for i in range(ROWS)]
        self.vrow = [ph.sb(f"vrow{i}", [P, D]) for i in range(ROWS)]
        self.stats = ph.sb("stats", [P, 12])
        self.mean = ph.sb("mean", [P, 2])
        self.std = ph.sb("std", [P, 2])
        self.tile_ready = sem("tile_ready")
        self.const_loaded = sem("const_loaded")
        self.score_loaded, self.x1_loaded = sem("score_loaded"), sem("x1_loaded")
        self.u_loaded = [sem(f"u_loaded{i}") for i in range(ROWS)]
        self.v_loaded = [sem(f"v_loaded{i}") for i in range(ROWS)]
        self.dotted = sem("dotted")
        self.added = sem("added")
        self.gelued = sem("gelued")
        self.weighted = sem("weighted")
        self.picked = sem("picked")
        self.exped = sem("exped")
        self.x1_set = sem("x1_set")
        self.y_set = sem("y_set")
        self.shared = sem("shared")
        self.indexed = sem("indexed")
        self.staging = sem("staging")
        self.y_stored = sem("y_stored")
        self.out_free = sem("out_free")
        self.dve = Steps(sem("ln_dve"), layer_norm_steps(""))
        self.acts = Steps(sem("ln_act"), ["root"])
        self.v_at = self.a_at = -len(self.PARTS)

    def gather(self, block):
        dr, last = self.dr, self.n_tiles - 1

        def load(pool, n, dst, name, loaded):
            src = dr[name][n] if isinstance(n, int) else dr[name][bass.ds(n, 1)].rearrange("a p n -> p (a n)")
            pool.dma_start(dst, src).then_inc(loaded, 16)

        def load_score(pool, n):
            pool.wait_ge(self.tile_ready, n + 1)
            apart(pool, dr["unwaited"])
            load(pool, n, self.score[:].rearrange("p a n -> p (a n)"), "scores", self.score_loaded)

        def fetch(pool, rows, k, loaded, table, slot):
            pool.indirect_dma_start(
                out=rows[k][:], out_offset=None, in_=dr[table],
                in_offset=bass.IndirectOffsetOnAxis(ap=self.staged[slot][:, k:k + 1], axis=0)
            ).then_inc(loaded[k], 16)

        def fetch_v(pool, m, k, slot):
            pool.wait_ge(self.added, ROWS * m + k + 1)
            apart(pool, dr["unwaited"])
            fetch(pool, self.vrow, k, self.v_loaded, "peer_v", slot)

        def units(pool, n, i, first=False):
            for s in range(self.BLOCK):
                m = n * UNITS + i * self.BLOCK + s
                pool.tensor_copy(self.staged[s][:], self.index[:, bass.ds((i * self.BLOCK + s) * ROWS, ROWS)])\
                    .then_inc(self.staging, 1)
                pool.wait_ge(self.staging, m + 1)
                for k in range(ROWS):
                    pool.wait_ge(self.dotted, ROWS * m + k + 1)
                    apart(pool, dr["unwaited"])
                    fetch(pool, self.urow, k, self.u_loaded, "peer_u", s)
                    if s or not first:
                        fetch_v(pool, m, k, (s - 1) % self.BLOCK)

        def tile(pool, n, late=False):
            blocks, half = UNITS // self.BLOCK, self.LATE // self.BLOCK
            following = not isinstance(n, int) or n < last
            pool.wait_ge(self.picked, self.KSTEP * n + self.KSTEP)
            apart(pool, dr["unwaited"])
            pool.tensor_copy(self.index[:], self.index_next[:]).then_inc(self.indexed, 1)
            pool.wait_ge(self.indexed, n + 1)
            apart(pool, dr["unwaited"])
            if following and not late:
                load_score(pool, n + 1)
            start = 0
            if isinstance(n, int) and n == 0:
                units(pool, 0, 0, first=True)
                start = 1
            if late:
                with pool.Fori(start, half) as i:
                    units(pool, n, i)
                load_score(pool, n + 1)
                start = half
            with pool.Fori(start, blocks) as i:
                units(pool, n, i)
            if following:
                pool.wait_ge(self.y_set, n + 1)
                apart(pool, dr["unwaited"])
                load(pool, n + 1, self.x1_next[:], "x1", self.x1_loaded)

        @block.gpsimd
        def _(pool):
            for dst, src in ((self.lng[:], "ln2_g"), (self.lnb[:], "ln2_b"), (self.iota[:], "iota")):
                pool.dma_start(dst, dr[src]).then_inc(self.const_loaded, 16)
            load_score(pool, 0)
            load(pool, 0, self.x1_next[:], "x1", self.x1_loaded)
            n = 0
            for stop in sorted({0, last, *self.late}):
                if stop - n > 1:
                    with pool.Fori(n, stop) as i:
                        tile(pool, i)
                elif stop - n == 1:
                    tile(pool, n)
                tile(pool, stop, late=stop in self.late)
                n = stop + 1
            for k in range(ROWS):
                fetch_v(pool, self.n_tiles * UNITS, k, self.BLOCK - 1)

    def scalar_open(self, act, part):
        if part == 0:
            self.acts.open(act)
        elif self.PARTS[part][0] == "share":
            self.exp_shares(act, 0)
        elif self.PARTS[part][0] == "total":
            self.set_x1(act, 0)
            self.set_y(act, 0)

    def exp_shares(self, act, n):
        act.wait_ge(self.shared, self.SH * n + 2)
        act.activation(self.share_next[:], self.share_next[:], ACT.Exp).then_inc(self.exped, 1)

    def set_x1(self, act, n):
        act.wait_ge(self.x1_loaded, 16 * n + 16)
        act.wait_ge(self.dotted, ROWS * UNITS * n + ROWS)
        act.activation(self.x1[:], self.x1_next[:], ACT.Copy).then_inc(self.x1_set, 1)

    def set_y(self, act, n):
        self.dve.wait(act, n - 1, "norm")
        act.activation(self.y[:], self.x1_next[:], ACT.Copy, scale=ALPHA).then_inc(self.y_set, 1)

    def scalar_unit(self, act, n, j, before, following):
        m = n * UNITS + j
        act.wait_ge(self.dotted, ROWS * m + 2 * ROWS)
        c = slice(ROWS * j, ROWS * (j + 1))
        act.activation(self.coef[:, c], self.hid[:, c], ACT.Gelu_apprx_tanh).then_inc(self.gelued, 1)
        if j == 0 and before:
            self.finish_tile(act, n - 1)
            self.store_tile(act, n - 1, n)
        if j == 2 and before:
            act.wait_ge(self.y_stored, 16 * n)
            act.sem_inc(self.out_free, 1)
        if following and following.get(j) == ("share",):
            self.exp_shares(act, n + 1)
        if j == UNITS - 1 and following:
            self.set_x1(act, n + 1)

    def finish_tile(self, act, n):
        self.dve.wait(act, n, "var")
        self.acts.done(act.activation(self.std[:, 1:2], self.std[:, 0:1], ACT.Sqrt), "root")

    def store_tile(self, act, n, next_tile):
        if next_tile is not None:
            self.set_y(act, next_tile)
        self.dve.wait(act, n, "out")
        dst = self.dr["y"][n] if isinstance(n, int) else self.dr["y"][bass.ds(n, 1)].rearrange("a p n -> p (a n)")
        act.dma_start(dst, self.out[:]).then_inc(self.y_stored, 16)

    def scalar_close(self, act):
        self.finish_tile(act, self.n_tiles - 1)
        self.store_tile(act, self.n_tiles - 1, None)
        act.wait_ge(self.y_stored, 16 * self.n_tiles)

    def vector_open(self, v, part):
        if part == 0:
            v.wait_ge(self.const_loaded, 48)
            v.sem_inc(self.dotted, ROWS)
            v.sem_inc(self.added, 2 * ROWS)
            v.sem_inc(self.shared, 1)
            v.sem_inc(self.weighted, 1)
            v.sem_inc(self.out_free, 1)
            self.dve.open(v)
        self.next_tile_part(v, 0, self.PARTS[part])
        if part == len(self.PARTS) - 1:
            self.softmax_take(v, 0)

    def next_tile_part(self, v, n, part):
        what = part[0]
        if what == "keys":
            if part[1] == 0:
                self.pick = TopK(self, v, n)
            self.pick.keys(part[1])
        elif what == "sums":
            self.pick.sums()
        elif what == "pairs":
            self.pick.pairs(part[1])
        elif what == "experts":
            self.pick.experts()
            self.pick.finish()
        elif what == "share":
            self.softmax_start(v, n)
        else:
            self.softmax_end(v, n)

    def softmax_start(self, v, n):
        v.wait_ge(self.shared, self.SH * n + 1)
        v.tensor_tensor(self.share_next[:], self.top[:], self.top[:, :, 0:1].to_broadcast([P, PH, TOPK]),
                        op=ALU.subtract).then_inc(self.shared, 1)

    def softmax_end(self, v, n):
        v.wait_ge(self.exped, n + 1)
        v.reduce_sum(self.total[:], self.share_next[:], axis=AX).then_inc(self.shared, 1)
        v.wait_ge(self.shared, self.SH * n + 3)
        v.reciprocal(self.total[:], self.total[:]).then_inc(self.shared, 1)

    def softmax_take(self, v, n):
        v.wait_ge(self.shared, self.SH * n + 4)
        v.wait_ge(self.weighted, UNITS * n + 1)
        v.tensor_tensor(self.share[:].rearrange("p (h k) -> p h k", h=PH), self.share_next[:],
                        self.total[:].unsqueeze(2).to_broadcast([P, PH, TOPK]), op=ALU.mult).then_inc(self.shared, 1)
        v.wait_ge(self.shared, self.SH * n + 5)

    def dot(self, v, n, j, k):
        v.wait_ge(self.u_loaded[k], 16 * UNITS * n + 16 * (j + 1))
        if j == 0 and k == 0:
            v.wait_ge(self.x1_set, n + 1)
        col = ROWS * j + k
        v.scalar_tensor_tensor(out=self.urow[k][:], in0=self.urow[k][:], scalar=1.0, in1=self.x1[:], op0=ALU.mult,
                               op1=ALU.mult, accum_out=self.hid[:, col:col + 1]).then_inc(self.dotted, 1)

    def weigh(self, v, n, j):
        v.wait_ge(self.gelued, UNITS * n + j + 1)
        c = slice(ROWS * j, ROWS * (j + 1))
        v.tensor_tensor(self.coef[:, c], self.coef[:, c], self.share[:, c], op=ALU.mult).then_inc(self.weighted, 1)
        v.wait_ge(self.weighted, UNITS * n + j + 2)

    def add(self, v, n, j, k):
        v.wait_ge(self.v_loaded[k], 16 * UNITS * n + 16 * (j + 1))
        if j == 0 and k == 0:
            v.wait_ge(self.y_set, n + 1)
        v.wait_ge(self.added, ROWS * UNITS * n + ROWS * (j + 2) + k)
        col = ROWS * j + k
        v.scalar_tensor_tensor(out=self.y[:], in0=self.vrow[k][:], scalar=self.coef[:, col:col + 1], in1=self.y[:],
                               op0=ALU.mult, op1=ALU.add).then_inc(self.added, 1)

    def norm(self, v, n):
        v.wait_ge(self.added, ROWS * UNITS * n + ROWS * (UNITS + 2))
        v.wait_ge(self.out_free, n + 1)
        layer_norm(v, self.dve, self.acts, n, "", self.y[:], self.out[:], self.stats, self.mean, self.std,
                   self.lng, self.lnb, self.dr["unwaited"])

    def vector_step(self, v, n, j, k, before, following):
        pn, pj = (n, j - 1) if j else (n - 1, UNITS - 1)
        self.dot(v, n, j, k)
        if j or before:
            if k == 0:
                self.weigh(v, pn, pj)
            self.add(v, pn, pj, k)
        if k < ROWS - 1:
            return
        if j == 0 and before:
            self.softmax_take(v, n)
            self.norm(v, n - 1)
        if following and j in following:
            self.next_tile_part(v, n + 1, following[j])

    def vector_close(self, v):
        n = self.n_tiles - 1
        self.weigh(v, n, UNITS - 1)
        for k in range(ROWS):
            self.add(v, n, UNITS - 1, k)
        self.norm(v, n)

    def parts(self, n):
        if n == self.n_tiles - 1:
            return None
        return self.LATE_PART if n in self.late else self.EARLY_PART

    def vector(self, v, steps, limit):
        for at in range(self.v_at, max(self.v_at, min(self.v_at + steps, limit))):
            n, row = divmod(at, UNITS * ROWS)
            if at < 0:
                self.vector_open(v, at + len(self.PARTS))
            else:
                self.vector_step(v, n, row // ROWS, row % ROWS, n > 0, self.parts(n))
            self.v_at = at + 1

    def scalar(self, act, steps, limit):
        for at in range(self.a_at, max(self.a_at, min(self.a_at + steps, limit))):
            n, row = divmod(at, UNITS * ROWS)
            if at < 0:
                self.scalar_open(act, at + len(self.PARTS))
            elif row % ROWS == ROWS - 1:
                self.scalar_unit(act, n, row // ROWS, n > 0, self.parts(n))
            self.a_at = at + 1

    def rest(self, block):
        per_tile = UNITS * ROWS
        last = self.n_tiles - 1

        @block.scalar
        def _(act):
            n0 = -(-self.a_at // per_tile)
            assert max(self.late) < n0 < last
            self.scalar(act, per_tile, n0 * per_tile)
            with act.Fori(n0, last) as n:
                for j in range(UNITS):
                    self.scalar_unit(act, n, j, True, self.EARLY_PART)
            for j in range(UNITS):
                self.scalar_unit(act, last, j, True, None)
            self.scalar_close(act)

        @block.vector
        def _(v):
            n0 = -(-self.v_at // per_tile)
            self.vector(v, per_tile, n0 * per_tile)
            with v.Fori(n0, last) as n:
                for j in range(UNITS):
                    for k in range(ROWS):
                        self.vector_step(v, n, j, k, True, self.EARLY_PART)
            for j in range(UNITS):
                for k in range(ROWS):
                    self.vector_step(v, last, j, k, True, None)
            self.vector_close(v)


GROUPS = (
    dict(tiles=2, shares=None),
    dict(tiles=3, shares=dict(project=60, local=20, prompt=50, sum=45, mix=13, route=20)),
    dict(tiles=4, shares=dict(project=90, local=25, prompt=75, sample=100, sum=60, mix=16, route=18)),
)
assert sum(g["tiles"] for g in GROUPS) == TT


def build(nc, dr):
    with nc.semaphore("unwaited") as unwaited:
        dr["unwaited"] = unwaited

        def scratch(name, *shape):
            dr[name] = nc.dram_tensor(f"scratch_{name}", shape, F32, kind="Internal").ap()

        scratch("uT", GG, P, TPAD)
        scratch("qmT", MH, P, TPAD)
        scratch("qT", HEADS, P, TPAD)
        scratch("gv", TT, P, 512)
        scratch("gT", GG, P, TPAD)
        scratch("mT", MH, P, TPAD)
        scratch("sbT", HEADS, P, TPAD)
        scratch("x1", TT, P, D)
        scratch("scores", TT, P, 2 * PH * NK)

        def sem_of(own, stage, made):
            def sem(label):
                made.append(own.enter_context(nc.semaphore(f"{stage}_{label}")))
                return made[-1]
            return sem

        def front(block, made, gate, own, bg, g, tile0, tiles):
            def sem(stage):
                return sem_of(own, f"g{g}_{stage}", made)

            prompt_tiles = min(tiles, PT - tile0)
            project(nc, block, sem("project"), dr, bg, g, tile0, tiles)
            gate.close(block)
            local_branches(nc, block, sem("local"), dr, bg, g, tile0, tiles)
            gate.close(block)
            attend_prompt(nc, block, sem("prompt"), dr, bg, g, tile0, prompt_tiles)
            gate.close(block)
            if prompt_tiles < tiles:
                attend_sample(nc, block, sem("sample"), dr, bg)
                gate.close(block)
            merge(nc, block, sem("merge"), gate, dr, bg, g, tile0, tiles)

        ph, sems = Phase(nc, "peer"), []
        with ph.ctx, ExitStack() as own:
            starts = [sum(x["tiles"] for x in GROUPS[:g]) for g in range(len(GROUPS) + 1)]
            with nc.Block() as block:
                peer = Peer(sem_of(own, "peer", sems), dr, ph, TT, late=[s - 1 for s in starts[1:-1]])
                peer.gather(block)
                gate = Gate(sem_of(own, "gate", sems)("passed"))
                for g, group in enumerate(GROUPS):
                    bg = NoBackground() if g == 0 else \
                        Background(peer, group["shares"], ((starts[g] - 1) * UNITS + peer.LATE) * ROWS)
                    with ExitStack() as front_own:
                        made = []
                        front(block, made, gate, front_own, bg, g, starts[g], group["tiles"])

                        @block.sync
                        def _(sp):
                            sp.sem_inc(peer.tile_ready, group["tiles"])
                            for s in made:
                                sp.sem_clear(s)

                        gate.close(block)
                peer.rest(block)


def kernel(**inputs):
    import concourse.bacc as bacc
    from concourse.bass_utils import run_bass_kernel_spmd

    a = {k: np.asarray(v) for k, v in inputs.items()}

    def pad_tokens():
        x = np.zeros((TPAD, D), np.float32)
        x[0:SEQ] = a["x_prompt"][0]
        x[SEQ:SEQ + NSEQ * NQ] = a["x_sample"].reshape(NSEQ * NQ, D)
        return x

    def feature_major(x):
        return x.T.reshape(-1, P, x.shape[0]).transpose(1, 0, 2)

    def units(w, width=UW):
        return w.reshape(w.shape[0] // P, P, w.shape[1] // width, width).transpose(2, 1, 0, 3)

    def rows(x, n=P):
        return np.broadcast_to(x, (n, x.size))

    x = pad_tokens()
    w = a["w_in"][0]
    u, gv, q, k, v, qm, gates = np.split(w, np.cumsum([512, 512, 1024, 1024, 1024, 512]), axis=1)
    spatial = a["w_spatial"][0].transpose(2, 0, 1)
    spatial_new = np.zeros((P, GG, P), np.float32)
    bias_new = np.zeros((GG, P), np.float32)
    for s in range(P // NQ):
        at = slice(s * NQ, (s + 1) * NQ)
        spatial_new[at, :, at] = spatial[0:NQ, :, 0:NQ]
        bias_new[:, at] = a["b_spatial"][0][:, 0:NQ]
    sel = np.zeros((HEADS * NQ, HEADS, HEADS * NQ), np.float32)
    for r in range(HEADS * NQ):
        sel[r, r // NQ, r] = 1.0
    n_phys = a["cache_sb_k"].shape[1]
    at_query = np.arange(HEADS * NQ) % NQ
    ins = {
        "x": x.reshape(TT, P, D),
        "xT": feature_major(x),
        "memT": feature_major(a["mem_prompt"][0]),
        "w_in": units(np.concatenate([u, qm, q, k, gv, v], axis=1)),
        "w_gate": units(gates, GATE_W),
        "w_mem": units(a["w_mem_kv"][0]),
        "w_br0": units(a["w_br_gmlp"][0], GATE_W),
        "w_br1": units(a["w_br_sb"][0], GATE_W),
        "w_br2": units(a["w_br_mem"][0], GATE_W),
        "w_out": units(a["w_out"][0]),
        "w_q": units(a["peer_wq"][0], GATE_W),
        "b_gate": a["b_gate"][0].reshape(24, P).T,
        "gln_g": rows(a["gmlp_ln_g"][0]),
        "gln_b": rows(a["gmlp_ln_b"][0]),
        "w_spatial": np.stack([spatial, spatial_new], axis=1),
        "b_spatial": np.stack([a["b_spatial"][0], bias_new])[None],
        "sb_bias": rows(a["sb_bias"][0]),
        "sb_bias_rows": np.repeat(a["sb_bias"][0], NQ)[:, None],
        "ln1_g": rows(a["ln1_g"][0]),
        "ln1_b": rows(a["ln1_b"][0]),
        "ln2_g": rows(a["ln2_g"][0]),
        "ln2_b": rows(a["ln2_b"][0]),
        "keysT": a["peer_subkeys"][0].reshape(2 * PH, NK, P).transpose(2, 0, 1),
        "peer_u": a["peer_u"][0],
        "peer_v": a["peer_v"][0],
        "cache_k": a["cache_sb_k"][0].transpose(0, 3, 2, 1).reshape(n_phys, P, HEADS * P),
        "cache_v": a["cache_sb_v"][0].reshape(n_phys, P, HEADS * P),
        "mem_k": a["cache_mem_k"][0].transpose(0, 3, 2, 1),
        "mem_v": a["cache_mem_v"][0].reshape(NSEQ, 2, P, 512).transpose(0, 2, 1, 3),
        "table": a["page_table"].reshape(1, -1).astype(np.int32),
        "ident": np.eye(P, dtype=np.float32),
        "ones": np.ones((1, P), np.float32),
        "tril": np.triu(np.ones((P, P), np.float32)),
        "neg": np.where(np.arange(P)[None] >= np.arange(P)[:, None], NEG, 0.0).astype(np.float32),
        "neg_new": np.where(np.arange(NQ)[None] >= at_query[:, None], NEG, 0.0).astype(np.float32),
        "sel": sel,
        "selm": sel[0:MH * NQ, 0:MH, 0:MH * NQ],
        "iota": rows(np.arange(TOPK, dtype=np.float32)),
    }
    outs = {
        "kT": (HEADS, P, TPAD), "v": (TT, P, HEADS * P), "mkT": (MH, P, NMEM), "mv": (2, P, 512),
        "gv_sample": (NSEQ * NQ, 512), "y": (TT, P, D),
    }
    nc = bacc.Bacc("TRN2", target_bir_lowering=False, num_devices=1)
    arrays, dr = {}, {}
    for name, value in ins.items():
        arrays[f"in_{name}"] = np.ascontiguousarray(value)
        dr[name] = nc.dram_tensor(f"in_{name}", value.shape, mybir.dt.from_np(value.dtype), kind="ExternalInput").ap()
    for name, shape in outs.items():
        dr[name] = nc.dram_tensor(f"out_{name}", shape, F32, kind="ExternalOutput").ap()
    build(nc, dr)
    res = run_bass_kernel_spmd(nc, [arrays], core_ids=[0]).results[0]
    got = {name: np.asarray(res[f"out_{name}"]) for name in outs}
    y = got["y"].reshape(TPAD, D)
    k = got["kT"].reshape(HEADS * P, TPAD).T
    v = got["v"].reshape(TPAD, HEADS * P)
    new = slice(SEQ, SEQ + NSEQ * NQ)
    return (y[0:SEQ].reshape(1, SEQ, D), y[new].reshape(NSEQ, NQ, D),
            k[0:SEQ].reshape(1, 1, SEQ, HEADS, P), v[0:SEQ].reshape(1, 1, SEQ, HEADS, P),
            got["mkT"].reshape(MH * P, NMEM).T.reshape(1, 1, NMEM, MH, P), got["mv"].reshape(1, 1, NMEM, MH, P),
            k[new].reshape(1, NSEQ, NQ, HEADS, P), v[new].reshape(1, NSEQ, NQ, HEADS, P),
            got["gv_sample"].reshape(1, NSEQ, NQ, GG, P))
```

```python
import numpy as np
from contextlib import ExitStack

import concourse.bass as bass
from concourse import mybir

F32 = mybir.dt.float32
U32 = mybir.dt.uint32
I32 = mybir.dt.int32
ACT = mybir.ActivationFunctionType
ALU = mybir.AluOpType
AX = mybir.AxisListType.X

P = 128
D = 1024
KD = D // P
SEQ = 1024
NSEQ = 8
NQ = 8
PT = SEQ // P
TT = PT + 1
TPAD = TT * P
HEADS = 8
MH = 4
NMEM = 256
GG = 4
PAGES = 16
CHUNK_PAGES = 4
UW = 512
PH = 8
NK = 128
TOPK = 16
NEXP = NK * NK
SB_SCALE = P ** -0.5
MEM_SCALE = P ** -0.5
ALPHA = 2.0 ** 0.25
EPS = 1e-5
NEG = -1e30
CAP = 40.0
GATE_W = 256
ROWS = 4
UNITS = PH * TOPK // ROWS
NEW = NSEQ * NQ
assert 2 * NEW == P


def apart(eng, unwaited):
    eng.sem_inc(unwaited, 1)


class Steps:

    def __init__(self, sem, names, credit=1):
        self.sem, self.names, self.credit = sem, names, credit
        self.index = {n: i for i, n in enumerate(names)}
        assert len(self.index) == len(names)
        self.last = -1

    def open(self, eng):
        eng.sem_inc(self.sem, self.credit * len(self.names))

    def done(self, ins, name):
        assert self.index[name] == (self.last + 1) % len(self.names), (name, self.last)
        self.last = self.index[name]
        ins.then_inc(self.sem, 1)

    def value(self, item, name):
        return (item + self.credit) * len(self.names) + self.index[name] + 1

    def wait(self, eng, item, name):
        eng.wait_ge(self.sem, self.value(item, name))


class Gate:

    def __init__(self, sem):
        self.sem, self.n = sem, 0

    def close(self, block):
        self.n += 4

        def meet(eng):
            eng.drain().then_inc(self.sem, 1)
            eng.wait_ge(self.sem, self.n)

        block.sync(meet)
        block.tensor(meet)
        block.scalar(meet)
        block.vector(meet)


class Store:

    def __init__(self, sems):
        self.sems = sems
        self.n = [0] * len(sems)

    def wait_free(self, eng, slot):
        if self.n[slot]:
            eng.wait_ge(self.sems[slot], 16 * self.n[slot])

    def start(self, eng, slot, dst, src):
        eng.dma_start(dst, src).then_inc(self.sems[slot], 16)
        self.n[slot] += 1

    def wait_all(self, eng):
        for slot in range(len(self.sems)):
            self.wait_free(eng, slot)


class NoBackground:

    def scalar(self, act, stage, i, places):
        pass

    def vector(self, v, stage, i, places):
        pass


class Background:

    def __init__(self, peer, shares, limit):
        self.peer, self.shares, self.limit = peer, shares, limit

    def steps(self, stage, i, places):
        n = self.shares[stage]
        return (i + 1) * n // places - i * n // places

    def scalar(self, act, stage, i, places):
        self.peer.scalar(act, self.steps(stage, i, places), self.limit)

    def vector(self, v, stage, i, places):
        self.peer.vector(v, self.steps(stage, i, places), self.limit)


class Phase:

    def __init__(self, nc, name):
        self.nc, self.name, self.ctx = nc, name, ExitStack()

    def sb(self, name, shape, dt=F32):
        return self.ctx.enter_context(self.nc.sbuf_tensor(f"{self.name}_{name}", shape, dt))

    def ps(self, name, shape, dt=F32):
        return self.ctx.enter_context(self.nc.psum_tensor(f"{self.name}_{name}", shape, dt))



def project(nc, block, sem, dr, bg, g, tile0, tiles):
    T = tiles * P
    t0 = tile0 * P
    chunks = [(c, min(512, T - c)) for c in range(0, T, 512)]
    ph = Phase(nc, f"pr{g}")
    with ph.ctx:
        xT = ph.sb("xT", [P, KD, T])
        memT = ph.sb("memT", [P, KD, NMEM])
        wbuf = [ph.sb(f"w{i}", [P, KD, UW]) for i in range(2)]
        stage = [ph.sb(f"st{i}", [P, 512]) for i in range(4)]
        bank = [ph.ps(f"b{i}", [P, 512]) for i in range(4)]
        x_loaded = sem("x_loaded")
        mem_loaded = sem("mem_loaded")
        w_loaded = [sem(f"w_loaded{i}") for i in range(2)]
        product = sem("product")
        evacuated = sem("evacuated")
        stored = Store([sem(f"stored{i}") for i in range(4)])

        FM, TM = 6, 3
        units = FM + TM + (2 if g == 0 else 0)
        per_fm, per_tm = 4 * len(chunks), tiles
        jobs_after = [per_fm * (u + 1) for u in range(FM)]
        jobs_after += [per_fm * FM + per_tm * (u + 1) for u in range(TM)]
        jobs_after += [jobs_after[-1] + 4, jobs_after[-1] + 6]

        jobs = []
        for u in range(FM):
            for b in range(4):
                for c0, n in chunks:
                    cols = slice(t0 + c0, t0 + c0 + n)
                    blk = 4 * u + b
                    if u == 0:
                        jobs.append((ACT.Gelu_apprx_tanh, 1.0, n, dr["uT"][b, :, cols]))
                    elif u == 1:
                        jobs.append((ACT.Copy, 1.0, n, dr["qmT"][b, :, cols]))
                    elif u < 4:
                        jobs.append((ACT.Copy, SB_SCALE, n, dr["qT"][blk - 8, :, cols]))
                    else:
                        jobs.append((ACT.Copy, 1.0, n, dr["kT"][blk - 16, :, cols]))
        for u in range(TM):
            for t in range(tile0, tile0 + tiles):
                if u == 0:
                    jobs.append((ACT.Gelu_apprx_tanh, 1.0, 512, dr["gv"][t]))
                else:
                    jobs.append((ACT.Copy, 1.0, 512, dr["v"][t, :, (u - 1) * 512:u * 512]))
        if g == 0:
            jobs += [(ACT.Copy, 1.0, NMEM, dr["mkT"][b]) for b in range(4)]
            jobs += [(ACT.Copy, 1.0, 512, dr["mv"][m]) for m in range(2)]

        @block.sync
        def _(sp):
            for u in range(units):
                if u == 1:
                    sp.dma_start(xT[:], dr["xT"][:, :, t0:t0 + T]).then_inc(x_loaded, 16)
                if u == 2 and g == 0:
                    sp.dma_start(memT[:], dr["memT"]).then_inc(mem_loaded, 16)
                if u >= 2:
                    sp.wait_ge(product, jobs_after[u - 2])
                src = dr["w_in"][u] if u < FM + TM else dr["w_mem"][u - FM - TM]
                sp.dma_start(wbuf[u % 2][:], src).then_inc(w_loaded[u % 2], 16)

        @block.tensor
        def _(pe):
            def accumulate(job, base, out, lhsT, rhs):
                pe.wait_ge(evacuated, base + job + 1)
                for k in range(KD):
                    last = pe.matmul(out, lhsT(k), rhs(k), start=k == 0, stop=k == KD - 1)
                last.then_inc(product, 1)

            pe.wait_ge(x_loaded, 16)
            with pe.Fori(0, FM // 2) as i:
                job = 0
                for s in range(2):
                    pe.wait_ge(w_loaded[s], 16 * i + 16)
                    for b in range(4):
                        for c0, n in chunks:
                            accumulate(job, 2 * per_fm * i, bank[job % 4][:, 0:n],
                                       lambda k: wbuf[s][:, k, b * P:(b + 1) * P],
                                       lambda k: xT[:, k, c0:c0 + n])
                            job += 1
            job = per_fm * FM
            for u in range(FM, FM + TM):
                pe.wait_ge(w_loaded[u % 2], 16 * (u // 2 + 1))
                for t in range(tiles):
                    accumulate(job, 0, bank[job % 4][:], lambda k: xT[:, k, t * P:(t + 1) * P],
                               lambda k: wbuf[u % 2][:, k, :])
                    job += 1
            if g == 0:
                pe.wait_ge(mem_loaded, 16)
                pe.wait_ge(w_loaded[9 % 2], 16 * (9 // 2 + 1))
                for b in range(4):
                    accumulate(job, 0, bank[job % 4][:, 0:NMEM],
                               lambda k: wbuf[1][:, k, b * P:(b + 1) * P], lambda k: memT[:, k, :])
                    job += 1
                pe.wait_ge(w_loaded[10 % 2], 16 * (10 // 2 + 1))
                for m in range(2):
                    accumulate(job, 0, bank[job % 4][:], lambda k: memT[:, k, m * P:(m + 1) * P],
                               lambda k: wbuf[0][:, k, :])
                    job += 1

        @block.scalar
        def _(act):
            act.sem_inc(evacuated, 4)
            bg.scalar(act, "project", 0, len(jobs) + 1)
            for j, (func, scale, n, dst) in enumerate(jobs):
                act.wait_ge(product, j + 1)
                stored.wait_free(act, j % 4)
                act.activation(stage[j % 4][:, 0:n], bank[j % 4][:, 0:n], func,
                               scale=scale).then_inc(evacuated, 1)
                act.wait_ge(evacuated, 4 + j + 1)
                stored.start(act, j % 4, dst, stage[j % 4][:, 0:n])
                bg.scalar(act, "project", j + 1, len(jobs) + 1)
            stored.wait_all(act)

        @block.vector
        def _(v):
            for j in range(len(jobs) + 1):
                bg.vector(v, "project", j, len(jobs) + 1)


def local_branches(nc, block, sem, dr, bg, g, tile0, tiles):
    ph = Phase(nc, f"lb{g}")
    with ph.ctx:
        ident = ph.sb("ident", [P, P])
        ones = ph.sb("ones", [1, P])
        tril = ph.sb("tril", [P, P])
        ws = ph.sb("ws", [P, 2, GG, P])
        bs = ph.sb("bs", [1, 2, GG, P])
        lng = ph.sb("lng", [P, 512])
        lnb = ph.sb("lnb", [P, 512])
        mkT = ph.sb("mkT", [P, MH, NMEM])
        mv = ph.sb("mv", [P, 2, 512])
        gv = [ph.sb(f"gv{i}", [P, 512]) for i in range(2)]
        uT = [ph.sb(f"uT{i}", [P, GG, P]) for i in range(2)]
        qmT = [ph.sb(f"qmT{i}", [P, MH, P]) for i in range(2)]
        gout = [ph.sb(f"gout{i}", [P, GG, P]) for i in range(2)]
        mout = [ph.sb(f"mout{i}", [P, MH, P]) for i in range(2)]
        stats = ph.sb("stats", [P, 6])
        mean = ph.sb("mean", [P, 2])
        std = ph.sb("std", [P, 2])
        peak = ph.sb("peak", [P, MH])
        npeak = ph.sb("npeak", [P, MH])
        den = ph.sb("den", [P, MH])
        rden = ph.sb("rden", [P, MH])
        prob = ph.sb("prob", [P, MH, NMEM])
        probT = ph.sb("probT", [P, MH, 2, P])
        spat_ps = ph.ps("spat", [P, GG, P])
        score_ps = ph.ps("score", [P, MH, NMEM])
        probT_ps = ph.ps("probT_ps", [P, MH, 2, P])
        mout_ps = ph.ps("mout_ps", [P, MH, P])
        mk_loaded = sem("mk_loaded")
        const_loaded = sem("const_loaded")
        tile_loaded = [sem(f"tile_loaded{i}") for i in range(2)]
        masked = sem("masked")
        dve = Steps(sem("dve_steps"), ["stats", "mean", "var", "peak", "npeak", "rstd", "norm", "scaled",
                                       "vnorm", "gout", "rden", "prob"])
        acts = Steps(sem("act_steps"), ["exp", "std", "probT", "mout"])
        pes = Steps(sem("pe_steps"), ["spat", "probT", "mout"])
        scored = sem("scored")
        gstored = Store([sem(f"gstored{i}") for i in range(2)])
        mstored = Store([sem(f"mstored{i}") for i in range(2)])
        is_prompt = [t < PT for t in range(tile0, tile0 + tiles)]
        places = 5 * tiles

        @block.sync
        def _(sp):
            def fetch(n):
                s, t = n % 2, tile0 + n
                cols = slice(t * P, (t + 1) * P)
                sp.dma_start(gv[s][:], dr["gv"][t]).then_inc(tile_loaded[s], 16)
                sp.dma_start(qmT[s][:], dr["qmT"][:, :, cols].rearrange("b p n -> p b n")).then_inc(tile_loaded[s], 16)
                sp.dma_start(uT[s][:], dr["uT"][:, :, cols].rearrange("b p n -> p b n")).then_inc(tile_loaded[s], 16)

            fetch(0)
            sp.dma_start(mkT[:], dr["mkT"].rearrange("h p m -> p h m")).then_inc(mk_loaded, 16)
            for dst, src in ((tril[:], dr["tril"]), (ws[:], dr["w_spatial"]), (lng[:], dr["gln_g"]),
                             (lnb[:], dr["gln_b"]), (ones[:], dr["ones"]), (bs[:], dr["b_spatial"]),
                             (ident[:], dr["ident"]), (mv[:], dr["mv"].rearrange("m p c -> p m c"))):
                sp.dma_start(dst, src).then_inc(const_loaded, 16)

            def keep(n):
                t, s = tile0 + n, n % 2
                dve.wait(sp, n, "gout")
                sp.dma_start(dr["gT"][:, :, t * P:(t + 1) * P].rearrange("b p n -> p b n"),
                             gout[s][:]).then_inc(gstored.sems[s], 16)
                if not is_prompt[n]:
                    sp.dma_start(dr["gv_sample"], gv[s][0:NEW, :]).then_inc(gstored.sems[s], 16)

            for n in range(1, tiles):
                if n >= 2:
                    keep(n - 2)
                    acts.wait(sp, n - 2, "mout")
                    dve.wait(sp, n - 2, "prob")
                fetch(n)
            for n in range(max(tiles - 2, 0), tiles):
                keep(n)
            for s in range(min(2, tiles)):
                mine = [n for n in range(tiles) if n % 2 == s]
                sp.wait_ge(gstored.sems[s], 16 * (len(mine) + sum(not is_prompt[n] for n in mine)))

        @block.tensor
        def _(pe):
            pes.open(pe)
            pe.wait_ge(mk_loaded, 16)

            def score(n):
                pe.wait_ge(tile_loaded[n % 2], 48 * (n // 2 + 1))
                if n:
                    acts.wait(pe, n - 1, "exp")
                for h in range(MH):
                    last = pe.matmul(score_ps[:, h, :], qmT[n % 2][:, h, :], mkT[:, h, :], start=True, stop=True)
                last.then_inc(scored, 1)

            score(0)
            for n in range(tiles):
                s, which = n % 2, 0 if is_prompt[n] else 1
                if n == 0:
                    pe.wait_ge(const_loaded, 16 * 8)
                    pe.wait_ge(masked, 1)
                dve.wait(pe, n, "vnorm")
                if n:
                    dve.wait(pe, n - 1, "gout")
                for k in range(GG):
                    pe.matmul(spat_ps[:, k, :], gv[s][:, k * P:(k + 1) * P], ws[:, which, k, :],
                              start=True, stop=False)
                    last = pe.matmul(spat_ps[:, k, :], ones[:], bs[:, which, k, :], start=False, stop=True)
                pes.done(last, "spat")
                if n + 1 < tiles:
                    score(n + 1)
                dve.wait(pe, n, "prob")
                for h in range(MH):
                    for m in range(2):
                        last = pe.transpose(probT_ps[:, h, m, :], prob[:, h, m * P:(m + 1) * P], ident[:])
                pes.done(last, "probT")
                acts.wait(pe, n, "probT")
                if n:
                    acts.wait(pe, n - 1, "mout")
                for h in range(MH):
                    for m in range(2):
                        last = pe.matmul(mout_ps[:, h, :], mv[:, m, h * P:(h + 1) * P], probT[:, h, m, :],
                                         start=m == 0, stop=m == 1)
                pes.done(last, "mout")

        @block.vector
        def _(v):
            dve.open(v)
            for n in range(tiles):
                s = n % 2
                v.wait_ge(tile_loaded[s], 48 * (n // 2 + 1))
                if n:
                    dve.wait(v, n - 1, "vnorm")
                dve.done(v.bn_stats(stats[:], gv[s][:]), "stats")
                dve.wait(v, n, "stats")
                dve.done(v.bn_aggr(mean[:], stats[:]), "mean")
                dve.wait(v, n, "mean")
                if n:
                    acts.wait(v, n - 1, "std")
                dve.done(v.tensor_scalar(std[:, 0:1], mean[:, 1:2], EPS, None, ALU.add), "var")
                v.wait_ge(scored, n + 1)
                dve.done(v.reduce_max(peak[:], score_ps[:], axis=AX), "peak")
                dve.wait(v, n, "peak")
                if n:
                    acts.wait(v, n - 1, "exp")
                dve.done(v.tensor_scalar(npeak[:], peak[:], -MEM_SCALE, None, ALU.mult), "npeak")
                if n == 0:
                    v.wait_ge(const_loaded, 16 * 8)
                    v.tensor_tensor(ws[:], ws[:], tril[:].unsqueeze(1).unsqueeze(1).to_broadcast([P, 2, GG, P]),
                                    op=ALU.mult).then_inc(masked, 1)
                bg.vector(v, "local", 5 * n, places)
                acts.wait(v, n, "std")
                dve.done(v.reciprocal(std[:, 1:2], std[:, 1:2]), "rstd")
                dve.wait(v, n, "rstd")
                dve.done(v.tensor_scalar(gv[s][:], gv[s][:], mean[:, 0:1], std[:, 1:2],
                                         ALU.subtract, ALU.mult), "norm")
                dve.wait(v, n, "norm")
                dve.done(v.tensor_tensor(gv[s][:], gv[s][:], lng[:], op=ALU.mult), "scaled")
                dve.wait(v, n, "scaled")
                dve.done(v.tensor_tensor(gv[s][:], gv[s][:], lnb[:], op=ALU.add), "vnorm")
                bg.vector(v, "local", 5 * n + 1, places)
                pes.wait(v, n, "spat")
                if n >= 2:
                    v.wait_ge(gstored.sems[s], 16 * (n // 2))
                dve.done(v.tensor_tensor(gout[s][:], uT[s][:], spat_ps[:], op=ALU.mult), "gout")
                bg.vector(v, "local", 5 * n + 2, places)
                acts.wait(v, n, "exp")
                dve.done(v.reciprocal(rden[:], den[:]), "rden")
                dve.wait(v, n, "rden")
                dve.done(v.tensor_tensor(prob[:], prob[:], rden[:].unsqueeze(2).to_broadcast([P, MH, NMEM]),
                                         op=ALU.mult), "prob")
                bg.vector(v, "local", 5 * n + 3, places)
                bg.vector(v, "local", 5 * n + 4, places)

        @block.scalar
        def _(act):
            acts.open(act)
            for n in range(tiles):
                s = n % 2
                dve.wait(act, n, "npeak")
                if n:
                    pes.wait(act, n - 1, "probT")
                for h in range(MH):
                    last = act.activation(prob[:, h, :], score_ps[:, h, :], ACT.Exp, bias=npeak[:, h:h + 1],
                                          scale=MEM_SCALE, accum_out=den[:, h:h + 1])
                acts.done(last, "exp")
                acts.done(act.activation(std[:, 1:2], std[:, 0:1], ACT.Sqrt), "std")
                for i in range(4):
                    bg.scalar(act, "local", 5 * n + i, places)
                pes.wait(act, n, "probT")
                acts.done(act.activation(probT[:], probT_ps[:], ACT.Copy), "probT")
                pes.wait(act, n, "mout")
                mstored.wait_free(act, s)
                acts.done(act.activation(mout[s][:], mout_ps[:], ACT.Copy), "mout")
                acts.wait(act, n, "mout")
                t = tile0 + n
                mstored.start(act, s, dr["mT"][:, :, t * P:(t + 1) * P].rearrange("b p n -> p b n"), mout[s][:])
                bg.scalar(act, "local", 5 * n + 4, places)
            mstored.wait_all(act)


def attend_prompt(nc, block, sem, dr, bg, g, tile0, tiles):
    NKEY = (tile0 + tiles) * P
    KT = NKEY // P
    ph = Phase(nc, f"at{g}")
    RING = 4
    HR = 3
    with ph.ctx:
        ident = ph.sb("ident", [P, P])
        neg = ph.sb("neg", [P, P])
        bias = ph.sb("bias", [P, HEADS])
        one = ph.sb("one", [P, 1])
        qh = [ph.sb(f"qh{i}", [P, tiles * P]) for i in range(HR)]
        kh = [ph.sb(f"kh{i}", [P, NKEY]) for i in range(HR)]
        vh = [ph.sb(f"vh{i}", [P, KT, P]) for i in range(HR)]
        soft = [ph.sb(f"soft{i}", [P, 512]) for i in range(RING)]
        sums = [ph.sb(f"sums{i}", [P, 512]) for i in range(2)]
        aT = [ph.sb(f"aT{i}", [P, 512]) for i in range(2)]
        oT = [ph.sb(f"oT{i}", [P, tiles * P]) for i in range(2)]
        z = [ph.ps(f"z{i}", [P, 512]) for i in range(RING)]
        aT_ps = [ph.ps(f"aTp{i}", [P, 512]) for i in range(2)]
        o_ps = [ph.ps(f"o{i}", [P, P]) for i in range(2)]
        const_loaded = sem("const_loaded")
        one_set = sem("one_set")
        head_loaded = [sem(f"head_loaded{i}") for i in range(HR)]
        scored = sem("scored")
        capped = sem("capped")
        logged = sem("logged")
        softened = sem("softened")
        weighed = sem("weighed")
        turned = sem("turned")
        copied = sem("copied")
        summed = sem("summed")
        kept = sem("kept")
        o_stored = Store([sem(f"o_stored{i}") for i in range(2)])
        pieces = []
        for h in range(HEADS):
            for q in range(tiles):
                w = (tile0 + q + 1) * P
                starts = list(range(0, w, 512))[::-1]
                for c in starts:
                    pieces.append((h, q, c, min(512, w - c), c == starts[0], c == 0, h * tiles + q))
        N = len(pieces)
        last_piece = {p[6]: k for k, p in enumerate(pieces) if p[5]}

        @block.sync
        def _(sp):
            for dst, src in ((neg[:], "neg"), (ident[:], "ident"), (bias[:], "sb_bias")):
                sp.dma_start(dst, dr[src]).then_inc(const_loaded, 16)
            for h in range(HEADS):
                s = h % HR
                if h >= HR:
                    sp.wait_ge(summed, last_piece[(h - HR + 1) * tiles - 1] + 1)
                sp.dma_start(qh[s][:], dr["qT"][h, :, tile0 * P:(tile0 + tiles) * P]).then_inc(head_loaded[s], 16)
                sp.dma_start(kh[s][:], dr["kT"][h, :, 0:NKEY]).then_inc(head_loaded[s], 16)
                sp.dma_start(vh[s][:], dr["v"][0:KT, :, h * P:(h + 1) * P]
                             .rearrange("t p c -> p t c")).then_inc(head_loaded[s], 16)

        @block.tensor
        def _(pe):
            pe.wait_ge(const_loaded, 48)

            def score(k):
                h, q, c, n, is_first, _, _ = pieces[k]
                s = h % HR
                if q == 0:
                    pe.wait_ge(head_loaded[s], 48 * (h // HR + 1))
                if k >= RING:
                    pe.wait_ge(softened, 3 * (k - RING) + 3)
                zz, qq = z[k % RING], qh[s][:, q * P:(q + 1) * P]
                rest = n - P if is_first else n
                if rest:
                    last = pe.matmul(zz[:, 0:rest], qq, kh[s][:, c:c + rest], start=True, stop=True)
                if is_first:
                    pe.matmul(zz[:, rest:n], qq, kh[s][:, c + rest:c + n], start=True, stop=False)
                    last = pe.matmul(zz[:, rest:n], ident[:], neg[:], start=False, stop=True)
                last.then_inc(scored, 1)

            def turn(k):
                n = pieces[k][3]
                pe.wait_ge(weighed, k + 1)
                if k >= 2:
                    pe.wait_ge(copied, k - 1)
                for j in range(0, n, P):
                    last = pe.transpose(aT_ps[k % 2][:, j:j + P], soft[k % RING][:, j:j + P], ident[:])
                last.then_inc(turned, 1)

            def gather(k):
                h, q, c, n, is_first, is_last, u = pieces[k]
                pe.wait_ge(copied, k + 1)
                if is_first and u >= 2:
                    pe.wait_ge(kept, u - 1)
                for j in range(0, n, P):
                    last = pe.matmul(o_ps[u % 2][:], vh[h % HR][:, (c + j) // P, :], aT[k % 2][:, j:j + P],
                                     start=is_first and j == 0, stop=is_last and j == n - P)
                last.then_inc(summed, 1)

            for k in range(3):
                score(k)
            for k in range(N):
                if k + 3 < N:
                    score(k + 3)
                turn(k)
                if k:
                    gather(k - 1)
            gather(N - 1)

        @block.vector
        def _(v):
            v.memset(one[:], 1.0).then_inc(one_set, 1)
            v.wait_ge(one_set, 1)
            v.wait_ge(const_loaded, 48)

            def cap(k):
                h, n = pieces[k][0], pieces[k][3]
                v.wait_ge(scored, k + 1)
                if k >= RING:
                    v.wait_ge(turned, k - RING + 1)
                v.tensor_scalar(soft[k % RING][:, 0:n], z[k % RING][:, 0:n], bias[:, h:h + 1], CAP,
                                ALU.add, ALU.min).then_inc(capped, 1)

            def weights(k):
                h, q, c, n, is_first, _, _ = pieces[k]
                zz, sf, total = z[k % RING][:, 0:n], soft[k % RING][:, 0:n], sums[k % 2][:, 0:n]
                b = bias[:, h:h + 1]
                v.wait_ge(logged, 2 * k + 2)
                v.scalar_tensor_tensor(out=sf, in0=zz, scalar=b, in1=sf, op0=ALU.add,
                                       op1=ALU.max).then_inc(softened, 1)
                if k + 2 < N:
                    cap(k + 2)
                v.wait_ge(softened, 3 * k + 1)
                v.tensor_tensor_scan(out=total[:, ::-1], data0=one[:].to_broadcast([P, n]), data1=sf[:, ::-1],
                                     initial=0.0 if is_first else sums[(k - 1) % 2][:, 0:1], op0=ALU.mult,
                                     op1=ALU.add).then_inc(softened, 1)
                bg.vector(v, "prompt", 2 * k, 2 * N)
                v.wait_ge(softened, 3 * k + 2)
                v.scalar_tensor_tensor(out=sf, in0=zz, scalar=b, in1=total, op0=ALU.add,
                                       op1=ALU.subtract).then_inc(softened, 1)

            cap(0)
            cap(1)
            for k in range(N):
                weights(k)
                bg.vector(v, "prompt", 2 * k + 1, 2 * N)

        @block.scalar
        def _(act):
            def soften(k):
                sf = soft[k % RING][:, 0:pieces[k][3]]
                act.wait_ge(capped, k + 1)
                act.activation(sf, sf, ACT.Exp).then_inc(logged, 1)
                act.wait_ge(logged, 2 * k + 1)
                act.activation(sf, sf, ACT.Ln, bias=1.0).then_inc(logged, 1)

            def weigh(k):
                sf = soft[k % RING][:, 0:pieces[k][3]]
                act.wait_ge(softened, 3 * k + 3)
                act.activation(sf, sf, ACT.Exp).then_inc(weighed, 1)

            def copy(k):
                n = pieces[k][3]
                act.wait_ge(turned, k + 1)
                if k >= 2:
                    act.wait_ge(summed, k - 1)
                act.activation(aT[k % 2][:, 0:n], aT_ps[k % 2][:, 0:n], ACT.Copy).then_inc(copied, 1)

            def keep(k):
                h, q, _, _, _, is_last, u = pieces[k]
                if not is_last:
                    return
                s = h % 2
                act.wait_ge(summed, k + 1)
                if q == 0:
                    o_stored.wait_free(act, s)
                act.activation(oT[s][:, q * P:(q + 1) * P], o_ps[u % 2][:], ACT.Copy).then_inc(kept, 1)
                if q == tiles - 1:
                    act.wait_ge(kept, u + 1)
                    o_stored.start(act, s, dr["sbT"][h, :, tile0 * P:(tile0 + tiles) * P], oT[s][:])

            soften(0)
            for k in range(N):
                if k + 1 < N:
                    soften(k + 1)
                bg.scalar(act, "prompt", 2 * k, 2 * N)
                weigh(k)
                if k >= 1:
                    copy(k - 1)
                if k >= 2:
                    keep(k - 2)
                bg.scalar(act, "prompt", 2 * k + 1, 2 * N)
            copy(N - 1)
            for k in range(N - 2, N):
                keep(k)
            o_stored.wait_all(act)


def layer_norm_steps(prefix):
    return [prefix + x for x in ("stats", "mean", "var", "rstd", "norm", "scaled", "out")]


def layer_norm(v, dve, acts, n, prefix, x, out, stats, mean, std, gain, offset, unwaited):
    v.bn_stats(stats[:, 0:6], x[:, 0:512])
    dve.done(v.bn_stats(stats[:, 6:12], x[:, 512:1024]), prefix + "stats")
    dve.wait(v, n, prefix + "stats")
    apart(v, unwaited)
    dve.done(v.bn_aggr(mean[:], stats[:]), prefix + "mean")
    dve.wait(v, n, prefix + "mean")
    if not isinstance(n, int) or n:
        acts.wait(v, n - 1, prefix + "root")
    dve.done(v.tensor_scalar(std[:, 0:1], mean[:, 1:2], EPS, None, ALU.add), prefix + "var")
    acts.wait(v, n, prefix + "root")
    dve.done(v.reciprocal(std[:, 1:2], std[:, 1:2]), prefix + "rstd")
    dve.wait(v, n, prefix + "rstd")
    dve.done(v.tensor_scalar(out, x, mean[:, 0:1], std[:, 1:2], ALU.subtract, ALU.mult), prefix + "norm")
    dve.wait(v, n, prefix + "norm")
    dve.done(v.tensor_tensor(out, out, gain[:], op=ALU.mult), prefix + "scaled")
    dve.wait(v, n, prefix + "scaled")
    dve.done(v.tensor_tensor(out, out, offset[:], op=ALU.add), prefix + "out")


def merge(nc, block, sem, gate, dr, bg, g, tile0, tiles):
    T = tiles * P
    t0 = tile0 * P
    cols = slice(t0, t0 + T)
    chunks = [(c, min(512, T - c)) for c in range(0, T, 512)]
    ph = Phase(nc, f"mg{g}")
    with ph.ctx:
        zT = ph.sb("zT", [P, KD, T])
        gated_sum(nc, block, sem, dr, bg, g, T, cols, chunks, zT)
        gate.close(block)
        mix_and_norm(nc, block, sem, dr, bg, g, tile0, tiles, zT)
        gate.close(block)
        route(nc, block, sem, dr, bg, g, tile0, tiles, chunks, zT)
        gate.close(block)


def gated_sum(nc, block, sem, dr, bg, g, T, cols, chunks, zT):
    NC = len(chunks)
    ph = Phase(nc, f"gs{g}")
    with ph.ctx:
        bgate = ph.sb("bgate", [P, 24])
        xT = ph.sb("xT", [P, KD, T])
        brT = ph.sb("brT", [P, 16, T])
        wbuf = [ph.sb(f"w{i}", [P, KD, GATE_W]) for i in range(3)]
        gates = [ph.sb(f"gate{i}", [P, 512]) for i in range(2)]
        term = ph.sb("term", [P, 512])
        gate_ps = [ph.ps(f"gp{i}", [P, 512]) for i in range(2)]
        branch_ps = [ph.ps(f"bp{i}", [P, 512]) for i in range(2)]
        bias_loaded = sem("bias_loaded")
        x_loaded, branches_loaded = sem("gx_loaded"), sem("branches_loaded")
        w_loaded = [sem(f"gw_loaded{i}") for i in range(3)]
        gate_ready, gate_done = sem("gate_ready"), sem("gate_done")
        branch_ready, branch_done = sem("branch_ready"), sem("branch_done")
        term_done = sem("term_done")
        pairs = [(qt, b) for qt in range(4) for b in range(3)]
        KB = {0: GG, 1: HEADS, 2: MH}
        KOFF = {0: 0, 1: GG, 2: GG + HEADS}
        jobs = [(p, mf, c) for p in range(len(pairs)) for mf in range(2) for c in range(NC)]
        per_pair = 2 * NC

        @block.sync
        def _(sp):
            sp.dma_start(bgate[:], dr["b_gate"]).then_inc(bias_loaded, 16)
            sp.dma_start(xT[:], dr["xT"][:, :, cols]).then_inc(x_loaded, 16)

            def load(u):
                p = u // 2
                qt, b = pairs[p]
                if u >= 3:
                    sp.wait_ge((gate_ready, branch_ready)[(u - 3) % 2], per_pair * ((u - 3) // 2 + 1))
                if u % 2 == 0:
                    sp.dma_start(wbuf[u % 3][:], dr["w_gate"][4 * b + qt]).then_inc(w_loaded[u % 3], 16)
                else:
                    sp.dma_start(wbuf[u % 3][:, 0:KB[b], :], dr[f"w_br{b}"][qt]).then_inc(w_loaded[u % 3], 16)

            load(0)
            load(1)
            sp.dma_start(brT[:, 0:GG, :], dr["gT"][:, :, cols].rearrange("b p n -> p b n")).then_inc(branches_loaded, 16)
            sp.dma_start(brT[:, GG:GG + HEADS, :], dr["sbT"][:, :, cols].rearrange("b p n -> p b n")).then_inc(branches_loaded, 16)
            sp.dma_start(brT[:, GG + HEADS:, :], dr["mT"][:, :, cols].rearrange("b p n -> p b n")).then_inc(branches_loaded, 16)
            for u in range(2, 2 * len(pairs)):
                load(u)

        @block.tensor
        def _(pe):
            pe.wait_ge(x_loaded, 16)
            for j, (p, mf, c) in enumerate(jobs):
                b = pairs[p][1]
                c0, n = chunks[c]
                ug, ub = 2 * p, 2 * p + 1
                if mf == 0 and c == 0:
                    pe.wait_ge(w_loaded[ug % 3], 16 * (ug // 3 + 1))
                if j >= 2:
                    pe.wait_ge(gate_done, j - 1)
                for k in range(KD):
                    last = pe.matmul(gate_ps[j % 2][:, 0:n], wbuf[ug % 3][:, k, mf * P:(mf + 1) * P],
                                     xT[:, k, c0:c0 + n], start=k == 0, stop=k == KD - 1)
                last.then_inc(gate_ready, 1)
                if mf == 0 and c == 0:
                    pe.wait_ge(w_loaded[ub % 3], 16 * (ub // 3 + 1))
                if j == 0:
                    pe.wait_ge(branches_loaded, 48)
                if j >= 2:
                    pe.wait_ge(branch_done, j - 1)
                for k in range(KB[b]):
                    last = pe.matmul(branch_ps[j % 2][:, 0:n], wbuf[ub % 3][:, k, mf * P:(mf + 1) * P],
                                     brT[:, KOFF[b] + k, c0:c0 + n], start=k == 0, stop=k == KB[b] - 1)
                last.then_inc(branch_ready, 1)

        @block.scalar
        def _(act):
            bg.scalar(act, "sum", 0, len(jobs) + 1)
            act.wait_ge(bias_loaded, 16)
            for j, (p, mf, c) in enumerate(jobs):
                qt, b = pairs[p]
                n = chunks[c][1]
                col = b * KD + qt * 2 + mf
                act.wait_ge(gate_ready, j + 1)
                if j >= 2:
                    act.wait_ge(branch_done, j - 1)
                act.activation(gates[j % 2][:, 0:n], gate_ps[j % 2][:, 0:n], ACT.Sigmoid,
                               bias=bgate[:, col:col + 1]).then_inc(gate_done, 1)
                bg.scalar(act, "sum", j + 1, len(jobs) + 1)

        @block.vector
        def _(v):
            bg.vector(v, "sum", 0, len(jobs) + 1)
            terms = 0
            for j, (p, mf, c) in enumerate(jobs):
                qt, b = pairs[p]
                c0, n = chunks[c]
                dst = zT[:, 2 * qt + mf, c0:c0 + n]
                v.wait_ge(gate_done, j + 1)
                v.wait_ge(branch_ready, j + 1)
                if b == 0:
                    v.tensor_tensor(dst, gates[j % 2][:, 0:n], branch_ps[j % 2][:, 0:n], op=ALU.mult)\
                        .then_inc(branch_done, 1)
                else:
                    terms += 1
                    v.wait_ge(branch_done, j)
                    v.tensor_tensor(term[:, 0:n], gates[j % 2][:, 0:n], branch_ps[j % 2][:, 0:n], op=ALU.mult)\
                        .then_inc(term_done, 1)
                    v.wait_ge(term_done, terms)
                    v.tensor_tensor(dst, dst, term[:, 0:n], op=ALU.add).then_inc(branch_done, 1)
                bg.vector(v, "sum", j + 1, len(jobs) + 1)


def mix_and_norm(nc, block, sem, dr, bg, g, tile0, tiles, zT):
    ph = Phase(nc, f"mx{g}")
    with ph.ctx:
        ident = ph.sb("ident", [P, P])
        lng = ph.sb("lng", [P, D])
        lnb = ph.sb("lnb", [P, D])
        w = ph.sb("w", [P, 2, KD, 512])
        x1 = ph.sb("x1", [P, tiles, D])
        stats = ph.sb("stats", [P, 12])
        mean = ph.sb("mean", [P, 2])
        std = ph.sb("std", [P, 2])
        mix_ps = [ph.ps(f"mp{i}", [P, 512]) for i in range(4)]
        turn_ps = [ph.ps(f"tp{i}", [P, 512]) for i in range(2)]
        const_loaded = sem("ln1_loaded")
        w_loaded = [sem(f"wo_loaded{i}") for i in range(2)]
        x_loaded = sem("x_loaded")
        mix_ready, mix_done = sem("mix_ready"), sem("mix_done")
        turned, turn_kept = sem("turned"), sem("turn_kept")
        x1_stored = sem("x1_stored")
        dve = Steps(sem("ln_dve"), layer_norm_steps(""))
        acts = Steps(sem("ln_act"), ["root"])
        places = 1 + 2 * tiles

        @block.sync
        def _(sp):
            for c in range(2):
                sp.dma_start(w[:, c], dr["w_out"][c]).then_inc(w_loaded[c], 16)
            sp.dma_start(x1[:], dr["x"][tile0:tile0 + tiles].rearrange("t p c -> p t c")).then_inc(x_loaded, 16)
            for dst, src in ((ident[:], "ident"), (lng[:], "ln1_g"), (lnb[:], "ln1_b")):
                sp.dma_start(dst, dr[src]).then_inc(const_loaded, 16)
            for n in range(tiles):
                dve.wait(sp, n, "out")
                sp.dma_start(dr["x1"][tile0 + n], x1[:, n, :]).then_inc(x1_stored, 16)
            sp.wait_ge(x1_stored, 16 * tiles)

        @block.tensor
        def _(pe):
            def turn(n):
                dve.wait(pe, n, "out")
                for hf in range(2):
                    if n:
                        pe.wait_ge(turn_kept, 2 * n + hf - 1)
                    for k in range(4):
                        kk = 4 * hf + k
                        last = pe.transpose(turn_ps[hf][:, k * P:(k + 1) * P], x1[:, n, kk * P:(kk + 1) * P], ident[:])
                    last.then_inc(turned, 1)

            for n in range(tiles):
                for c in range(2):
                    j = 2 * n + c
                    if n == 0:
                        pe.wait_ge(w_loaded[c], 16)
                    if j >= 4:
                        pe.wait_ge(mix_done, j - 3)
                    for k in range(KD):
                        last = pe.matmul(mix_ps[j % 4][:], zT[:, k, n * P:(n + 1) * P], w[:, c, k, :],
                                         start=k == 0, stop=k == KD - 1)
                    last.then_inc(mix_ready, 1)
                if n == 0:
                    pe.wait_ge(const_loaded, 48)
                else:
                    turn(n - 1)
            turn(tiles - 1)

        @block.scalar
        def _(act):
            acts.open(act)
            bg.scalar(act, "mix", 0, places)
            for n in range(tiles):
                bg.scalar(act, "mix", 2 * n + 1, places)
                dve.wait(act, n, "var")
                acts.done(act.activation(std[:, 1:2], std[:, 0:1], ACT.Sqrt), "root")
                bg.scalar(act, "mix", 2 * n + 2, places)
                for hf in range(2):
                    act.wait_ge(turned, 2 * n + hf + 1)
                    act.activation(zT[:, 4 * hf:4 * hf + 4, n * P:(n + 1) * P],
                                   turn_ps[hf][:].rearrange("p (k n) -> p k n", k=4), ACT.Copy).then_inc(turn_kept, 1)

        @block.vector
        def _(v):
            dve.open(v)
            bg.vector(v, "mix", 0, places)
            v.wait_ge(x_loaded, 16)
            v.wait_ge(const_loaded, 48)
            for n in range(tiles):
                for c in range(2):
                    j = 2 * n + c
                    v.wait_ge(mix_ready, j + 1)
                    dst = x1[:, n, c * 512:(c + 1) * 512]
                    v.scalar_tensor_tensor(out=dst, in0=dst, scalar=ALPHA, in1=mix_ps[j % 4][:], op0=ALU.mult,
                                           op1=ALU.add).then_inc(mix_done, 1)
                bg.vector(v, "mix", 2 * n + 1, places)
                v.wait_ge(mix_done, 2 * n + 2)
                layer_norm(v, dve, acts, n, "", x1[:, n, :], x1[:, n, :], stats, mean, std, lng, lnb, dr["unwaited"])
                bg.vector(v, "mix", 2 * n + 2, places)


def route(nc, block, sem, dr, bg, g, tile0, tiles, chunks, xT):
    T = tiles * P
    NC = len(chunks)
    ph = Phase(nc, f"rt{g}")
    with ph.ctx:
        keysT = ph.sb("keysT", [P, 2 * PH, NK])
        queries = ph.sb("queries", [P, 2 * PH, T])
        wbuf = [ph.sb(f"w{i}", [P, KD, GATE_W]) for i in range(3)]
        stage = [ph.sb(f"st{i}", [P, 2 * PH * NK]) for i in range(2)]
        bank = [ph.ps(f"b{i}", [P, 512]) for i in range(4)]
        score_ps = ph.ps("score", [P, 2 * PH * NK])
        keys_loaded = sem("keys_loaded")
        w_loaded = [sem(f"wq_loaded{i}") for i in range(3)]
        query_ready, query_kept = sem("query_ready"), sem("query_kept")
        scored, score_kept = sem("scored"), sem("score_kept")
        s_stored = Store([sem(f"s_stored{i}") for i in range(2)])
        per_unit = 2 * NC
        jobs = [(u, b, c) for u in range(8) for b in range(2) for c in range(NC)]
        places = 1 + len(jobs) + tiles

        @block.sync
        def _(sp):
            for u in range(8):
                if u >= 3:
                    sp.wait_ge(query_ready, per_unit * (u - 2))
                sp.dma_start(wbuf[u % 3][:], dr["w_q"][u]).then_inc(w_loaded[u % 3], 16)
                if u == 2:
                    sp.dma_start(keysT[:], dr["keysT"]).then_inc(keys_loaded, 16)

        @block.tensor
        def _(pe):
            for j, (u, b, c) in enumerate(jobs):
                c0, n = chunks[c]
                if b == 0 and c == 0:
                    pe.wait_ge(w_loaded[u % 3], 16 * (u // 3 + 1))
                if j >= 4:
                    pe.wait_ge(query_kept, j - 3)
                for k in range(KD):
                    last = pe.matmul(bank[j % 4][:, 0:n], wbuf[u % 3][:, k, b * P:(b + 1) * P],
                                     xT[:, k, c0:c0 + n], start=k == 0, stop=k == KD - 1)
                last.then_inc(query_ready, 1)
            pe.wait_ge(keys_loaded, 16)
            pe.wait_ge(query_kept, len(jobs))
            for n in range(tiles):
                for half in range(2):
                    if n:
                        pe.wait_ge(score_kept, 2 * n + half - 1)
                    for hp in range(half * PH, (half + 1) * PH):
                        last = pe.matmul(score_ps[:, hp * NK:(hp + 1) * NK], queries[:, hp, n * P:(n + 1) * P],
                                         keysT[:, hp, :], start=True, stop=True)
                    last.then_inc(scored, 1)

        @block.scalar
        def _(act):
            bg.scalar(act, "route", 0, places)
            for j, (u, b, c) in enumerate(jobs):
                c0, n = chunks[c]
                act.wait_ge(query_ready, j + 1)
                act.activation(queries[:, 2 * u + b, c0:c0 + n], bank[j % 4][:, 0:n], ACT.Copy).then_inc(query_kept, 1)
                bg.scalar(act, "route", j + 1, places)
            for n in range(tiles):
                s_stored.wait_free(act, n % 2)
                for half in range(2):
                    c = slice(half * PH * NK, (half + 1) * PH * NK)
                    act.wait_ge(scored, 2 * n + half + 1)
                    act.activation(stage[n % 2][:, c], score_ps[:, c], ACT.Copy).then_inc(score_kept, 1)
                act.wait_ge(score_kept, 2 * n + 2)
                s_stored.start(act, n % 2, dr["scores"][tile0 + n], stage[n % 2][:])
                bg.scalar(act, "route", 1 + len(jobs) + n, places)
            s_stored.wait_all(act)

        @block.vector
        def _(v):
            for i in range(places):
                bg.vector(v, "route", i, places)


def attend_sample(nc, block, sem, dr, bg):
    R = HEADS * NQ
    MR = MH * NQ
    CW = CHUNK_PAGES * P
    NCH = PAGES // CHUNK_PAGES
    ph = Phase(nc, "sa")
    with ph.ctx:
        ident = ph.sb("ident", [P, P])
        sel = ph.sb("sel", [R, HEADS, R])
        selm = ph.sb("selm", [MR, MH, MR])
        negn = ph.sb("negn", [R, NQ])
        bias = ph.sb("bias", [R, 1])
        one = ph.sb("one", [P, 1])
        table = ph.sb("table", [1, NSEQ * PAGES], I32)
        q = ph.sb("q", [P, HEADS, R])
        kn = ph.sb("kn", [P, HEADS, R])
        qm = ph.sb("qm", [P, MH, R])
        qpad = ph.sb("qpad", [P, HEADS * (R + NQ)])
        qmpad = ph.sb("qmpad", [P, MH * (MR + NQ)])
        mk = ph.sb("mk", [P, MH, NMEM])
        mv = ph.sb("mv", [P, 2, 512])
        kc = [ph.sb(f"kc{i}", [P, CHUNK_PAGES, HEADS * P]) for i in range(2)]
        vc = [ph.sb(f"vc{i}", [P, CHUNK_PAGES, HEADS * P]) for i in range(2)]
        soft = [ph.sb(f"soft{i}", [R, CW]) for i in range(2)]
        loga = [ph.sb(f"loga{i}", [R, CW]) for i in range(2)]
        first = [ph.sb(f"first{i}", [R, 1]) for i in range(2)]
        aT = [ph.sb(f"aT{i}", [P, CHUNK_PAGES * R]) for i in range(2)]
        osb = ph.sb("osb", [R, HEADS * P])
        vn = osb[0:NQ]
        so = ph.sb("so", [P, HEADS, R])
        smo = ph.sb("smo", [P, MH, R])
        probT = ph.sb("probT", [P, 2, MR])
        prob, om = soft[0][0:MR, 0:NMEM], soft[1][0:MR, 0:512]
        peak = ph.sb("peak", [MR, 1])
        npeak = ph.sb("npeak", [MR, 1])
        den = ph.sb("den", [MR, 1])
        rden = ph.sb("rden", [MR, 1])
        z = [ph.ps(f"z{i}", [R, CW]) for i in range(2)]
        aT_ps = [ph.ps(f"aTp{i}", [P, CHUNK_PAGES * R]) for i in range(2)]
        o_ps = ph.ps("o", [R, HEADS * P])
        fin_ps = ph.ps("fin", [P, 512])
        m_ps = ph.ps("m", [P, 512])
        const_loaded, table_loaded = sem("const_loaded"), sem("table_loaded")
        cleared = sem("cleared")
        mem_loaded = sem("mem_loaded")
        vn_loaded = sem("vn_loaded")
        k_loaded = [sem(f"k_loaded{i}") for i in range(2)]
        v_loaded = [sem(f"v_loaded{i}") for i in range(2)]
        o_stored = sem("o_stored")
        blocks = ["n"] + [str(c) for c in range(NCH)]
        per_seq = 1 + 2 * len(blocks)
        places = NSEQ * per_seq
        dve = Steps(sem("dve_steps"), ["pads", "peak", "npeak", "rden", "prob"] +
                    [f"{b}_{x}" for b in blocks for x in ("cap", "sp", "cum", "first", "log")])
        acts = Steps(sem("act_steps"), ["mexp", "mprobT", "mom", "mout"] +
                     [f"{b}_{x}" for b in blocks for x in ("exp", "ln", "a", "aT")] + ["osb", "out"])
        pes = Steps(sem("pe_steps"), ["mscore", "mprobT", "mom", "mout", "n_z"] +
                    [x for c in range(NCH) for x in (f"{c}_z", f"{blocks[c]}_aT", f"{blocks[c]}_o")] +
                    [f"{NCH - 1}_aT", f"{NCH - 1}_o", "out"])

        @block.sync
        def _(sp):
            c0 = PT * P
            sp.dma_start(table[:], dr["table"]).then_inc(table_loaded, 16)
            for dst, src in ((q[:], dr["qT"][:, :, c0:c0 + R].rearrange("h p n -> p h n")),
                             (qm[:], dr["qmT"][:, :, c0:c0 + R].rearrange("h p n -> p h n")),
                             (kn[:], dr["kT"][:, :, c0:c0 + R].rearrange("h p n -> p h n")),
                             (ident[:], dr["ident"]), (sel[:], dr["sel"]), (selm[:], dr["selm"]),
                             (negn[:], dr["neg_new"]), (bias[:], dr["sb_bias_rows"])):
                sp.dma_start(dst, src).then_inc(const_loaded, 16)
            sp.wait_ge(table_loaded, 16)
            with sp.Fori(0, NSEQ) as i:
                acts.wait(sp, i - 1, "mout")
                sp.dma_start(mk[:], dr["mem_k"][bass.ds(i, 1)].rearrange("a p h m -> p (a h) m")).then_inc(mem_loaded, 16)
                sp.dma_start(mv[:], dr["mem_v"][bass.ds(i, 1)].rearrange("a p m c -> p (a m) c")).then_inc(mem_loaded, 16)
                for c in range(NCH):
                    s = c % 2
                    before = (i, c - 2) if c >= 2 else (i - 1, c + NCH - 2)
                    pes.wait(sp, before[0], f"{before[1]}_z")
                    apart(sp, dr["unwaited"])
                    for k in range(CHUNK_PAGES):
                        page = PAGES - CHUNK_PAGES * (c + 1) + k
                        reg = sp.value_load(table[0:1, bass.ds(i * PAGES + page, 1)], min_val=0,
                                            max_val=dr["cache_k"].shape[0] - 1)
                        sp.dma_start(kc[s][:, k, :], dr["cache_k"][bass.ds(reg, 1)]
                                     .rearrange("a p c -> p (a c)")).then_inc(k_loaded[s], 16)
                    pes.wait(sp, before[0], f"{before[1]}_o")
                    apart(sp, dr["unwaited"])
                    for k in range(CHUNK_PAGES):
                        page = PAGES - CHUNK_PAGES * (c + 1) + k
                        reg = sp.value_load(table[0:1, bass.ds(i * PAGES + page, 1)], min_val=0,
                                            max_val=dr["cache_v"].shape[0] - 1)
                        sp.dma_start(vc[s][:, k, :], dr["cache_v"][bass.ds(reg, 1)]
                                     .rearrange("a p c -> p (a c)")).then_inc(v_loaded[s], 16)

        @block.tensor
        def _(pe):
            pe.wait_ge(const_loaded, 16 * 8)
            pes.open(pe)
            with pe.Fori(0, NSEQ) as i:
                dve.wait(pe, i, "pads")
                pe.wait_ge(mem_loaded, 32 * i + 32)
                for h in range(MH):
                    last = pe.matmul(m_ps[0:MR, 0:NMEM], qmpad[:, h * MR:(h + 1) * MR], mk[:, h, :],
                                     start=h == 0, stop=h == MH - 1)
                pes.done(last, "mscore")
                dve.wait(pe, i, "prob")
                apart(pe, dr["unwaited"])
                for m in range(2):
                    last = pe.transpose(m_ps[:, m * MR:(m + 1) * MR], prob[:, m * P:(m + 1) * P], ident[0:MR, 0:MR])
                pes.done(last, "mprobT")
                acts.wait(pe, i, "mprobT")
                for m in range(2):
                    last = pe.matmul(m_ps[0:MR, :], probT[:, m, :], mv[:, m, :], start=m == 0, stop=m == 1)
                pes.done(last, "mom")
                acts.wait(pe, i, "mom")
                for h in range(MH):
                    last = pe.matmul(m_ps[:, 0:MR], om[:, h * P:(h + 1) * P], selm[:, h, :],
                                     start=h == 0, stop=h == MH - 1)
                pes.done(last, "mout")

                for h in range(HEADS):
                    pe.matmul(fin_ps[0:R, 0:NQ], qpad[:, h * R:(h + 1) * R], kn[:, h, bass.ds(i * NQ, NQ)],
                              start=h == 0, stop=False)
                pes.done(pe.matmul(fin_ps[0:R, 0:NQ], ident[0:R, 0:R], negn[:], start=False, stop=True), "n_z")

                def turn_and_sum(b):
                    acts.wait(pe, i, f"{b}_a")
                    apart(pe, dr["unwaited"])
                    if b == "n":
                        last = pe.transpose(aT_ps[1][0:NQ, 0:R], loga[1][:, 0:NQ], ident[0:R, 0:R])
                        pes.done(last, "n_aT")
                        acts.wait(pe, i, "n_aT")
                        pe.wait_ge(vn_loaded, 16 * i + 16)
                        acts.wait(pe, i - 1, "osb")
                        for hf in range(2):
                            last = pe.matmul(o_ps[:, hf * 512:(hf + 1) * 512], aT[1][0:NQ, 0:R],
                                             vn[:, hf * 512:(hf + 1) * 512], start=True, stop=False)
                        pes.done(last, "n_o")
                        return
                    c = int(b)
                    s = c % 2
                    for k in range(CHUNK_PAGES):
                        last = pe.transpose(aT_ps[s][:, k * R:(k + 1) * R], loga[s][:, k * P:(k + 1) * P],
                                            ident[0:R, 0:R])
                    pes.done(last, f"{b}_aT")
                    acts.wait(pe, i, f"{b}_aT")
                    pe.wait_ge(v_loaded[s], 64 * (2 * i + c // 2) + 64)
                    for k in range(CHUNK_PAGES):
                        for hf in range(2):
                            last = pe.matmul(o_ps[:, hf * 512:(hf + 1) * 512], aT[s][:, k * R:(k + 1) * R],
                                             vc[s][:, k, hf * 512:(hf + 1) * 512], start=False,
                                             stop=c == NCH - 1 and k == CHUNK_PAGES - 1)
                    pes.done(last, f"{b}_o")

                for c in range(NCH):
                    s = c % 2
                    pe.wait_ge(k_loaded[s], 64 * (2 * i + c // 2) + 64)
                    if c >= 2:
                        dve.wait(pe, i, f"{c - 2}_log")
                    for h in range(HEADS):
                        last = pe.matmul(z[s][:], qpad[:, h * R:(h + 1) * R], kc[s][:, :, h * P:(h + 1) * P],
                                         start=h == 0, stop=h == HEADS - 1)
                    pes.done(last, f"{c}_z")
                    turn_and_sum(blocks[c])
                turn_and_sum(blocks[NCH])
                acts.wait(pe, i, "osb")
                for h in range(HEADS):
                    last = pe.matmul(fin_ps[:, 0:R], osb[:, h * P:(h + 1) * P], sel[:, h, :], start=h == 0,
                                     stop=h == HEADS - 1)
                pes.done(last, "out")

        @block.vector
        def _(v):
            v.memset(one[:], 1.0).then_inc(cleared, 1)
            v.memset(qpad[:], 0.0).then_inc(cleared, 1)
            v.memset(qmpad[:], 0.0).then_inc(cleared, 1)
            v.wait_ge(cleared, 3)
            v.wait_ge(const_loaded, 16 * 8)
            dve.open(v)
            for i in range(NSEQ):
                pes.wait(v, i - 1, "out")
                v.tensor_copy(qpad[:].rearrange("p (h c) -> p h c", c=R + NQ)[:, :, 0:NQ],
                              q[:, :, bass.ds(i * NQ, NQ)])
                dve.done(v.tensor_copy(qmpad[:].rearrange("p (h c) -> p h c", c=MR + NQ)[:, :, 0:NQ],
                                       qm[:, :, bass.ds(i * NQ, NQ)]), "pads")
                bg.vector(v, "sample", i * per_seq, places)
                pes.wait(v, i, "mscore")
                dve.done(v.reduce_max(peak[:], m_ps[0:MR, 0:NMEM], axis=AX), "peak")
                dve.wait(v, i, "peak")
                dve.done(v.tensor_scalar(npeak[:], peak[:], -MEM_SCALE, None, ALU.mult), "npeak")
                acts.wait(v, i, "mexp")
                dve.done(v.reciprocal(rden[:], den[:]), "rden")
                dve.wait(v, i, "rden")
                dve.done(v.tensor_scalar(prob[:], prob[:], rden[:], None, ALU.mult), "prob")
                for nth, b in enumerate(blocks):
                    at = i * per_seq + 1 + 2 * nth
                    s = 1 if b == "n" else int(b) % 2
                    w = NQ if b == "n" else CW
                    zz = fin_ps[0:R, 0:NQ] if b == "n" else z[s][:]
                    sf, lg = soft[s][:, 0:w], loga[s][:, 0:w]
                    prev = None if b == "n" else first[1 - s]
                    pes.wait(v, i, f"{b}_z")
                    dve.done(v.tensor_scalar(sf, zz, bias[:], CAP, ALU.add, ALU.min), f"{b}_cap")
                    bg.vector(v, "sample", at, places)
                    acts.wait(v, i, f"{b}_ln")
                    dve.done(v.scalar_tensor_tensor(out=sf, in0=zz, scalar=bias[:], in1=sf, op0=ALU.add,
                                                    op1=ALU.max), f"{b}_sp")
                    dve.wait(v, i, f"{b}_sp")
                    if b not in ("n", "0"):
                        pes.wait(v, i, "n_aT" if b == "1" else f"{int(b) - 2}_aT")
                    dve.done(v.tensor_tensor_scan(out=lg[:, ::-1], data0=one[0:R, :].to_broadcast([R, w]),
                                                  data1=sf[:, ::-1], initial=0.0 if prev is None else prev[:],
                                                  op0=ALU.mult, op1=ALU.add), f"{b}_cum")
                    dve.wait(v, i, f"{b}_cum")
                    dve.done(v.tensor_copy(first[s][:], lg[:, 0:1]), f"{b}_first")
                    dve.wait(v, i, f"{b}_first")
                    dve.done(v.scalar_tensor_tensor(out=lg, in0=zz, scalar=bias[:], in1=lg, op0=ALU.add,
                                                    op1=ALU.subtract), f"{b}_log")
                    bg.vector(v, "sample", at + 1, places)

        @block.scalar
        def _(act):
            act.wait_ge(cleared, 3)
            act.wait_ge(const_loaded, 16 * 8)
            acts.open(act)

            def load_vn(i):
                act.dma_start(vn, dr["v"][PT, i * NQ:(i + 1) * NQ, :]).then_inc(vn_loaded, 16)

            load_vn(0)
            for i in range(NSEQ):
                bg.scalar(act, "sample", i * per_seq, places)
                dve.wait(act, i, "npeak")
                acts.done(act.activation(prob[:], m_ps[0:MR, 0:NMEM], ACT.Exp, bias=npeak[:], scale=MEM_SCALE,
                                         accum_out=den[:]), "mexp")
                pes.wait(act, i, "mprobT")
                acts.done(act.activation(probT[:].rearrange("p m r -> p (m r)"), m_ps[:, 0:2 * MR], ACT.Copy), "mprobT")
                pes.wait(act, i, "mom")
                acts.done(act.activation(om[:], m_ps[0:MR, :], ACT.Copy), "mom")
                pes.wait(act, i, "mout")
                acts.done(act.activation(smo[:, :, bass.ds(i * NQ, NQ)],
                                         m_ps[:, 0:MR].rearrange("p (h q) -> p h q", h=MH), ACT.Copy), "mout")
                for nth, b in enumerate(blocks):
                    at = i * per_seq + 1 + 2 * nth
                    s = 1 if b == "n" else int(b) % 2
                    w = NQ if b == "n" else CW
                    sf, lg = soft[s][:, 0:w], loga[s][:, 0:w]
                    dve.wait(act, i, f"{b}_cap")
                    acts.done(act.activation(sf, sf, ACT.Exp), f"{b}_exp")
                    acts.wait(act, i, f"{b}_exp")
                    acts.done(act.activation(sf, sf, ACT.Ln, bias=1.0), f"{b}_ln")
                    bg.scalar(act, "sample", at, places)
                    dve.wait(act, i, f"{b}_log")
                    acts.done(act.activation(lg, lg, ACT.Exp), f"{b}_a")
                    pes.wait(act, i, f"{b}_aT")
                    if b == "n":
                        acts.done(act.activation(aT[1][0:NQ, 0:R], aT_ps[1][0:NQ, 0:R], ACT.Copy), "n_aT")
                    else:
                        acts.done(act.activation(aT[s][:], aT_ps[s][:], ACT.Copy), f"{b}_aT")
                    bg.scalar(act, "sample", at + 1, places)
                pes.wait(act, i, f"{NCH - 1}_o")
                acts.done(act.activation(osb[:], o_ps[:], ACT.Copy), "osb")
                pes.wait(act, i, "out")
                acts.done(act.activation(so[:, :, bass.ds(i * NQ, NQ)],
                                         fin_ps[:, 0:R].rearrange("p (h q) -> p h q", h=HEADS), ACT.Copy), "out")
                if i < NSEQ - 1:
                    load_vn(i + 1)
            acts.wait(act, NSEQ - 1, "out")
            for c0 in (PT * P, PT * P + NEW):
                act.dma_start(dr["sbT"][:, :, c0:c0 + NEW].rearrange("h p n -> p h n"), so[:]).then_inc(o_stored, 16)
                act.dma_start(dr["mT"][:, :, c0:c0 + NEW].rearrange("h p n -> p h n"), smo[:]).then_inc(o_stored, 16)
            act.wait_ge(o_stored, 64)


class TopK:

    def __init__(self, peer, v, tile):
        self.peer, self.v, self.tile, self.n = peer, v, tile, 0

    def wait_round_before(self):
        if self.n or not isinstance(self.tile, int) or self.tile:
            self.v.wait_ge(self.peer.picked, self.peer.KSTEP * self.tile + self.n)
            apart(self.v, self.peer.dr["unwaited"])

    def end_round(self, ins):
        ins.then_inc(self.peer.picked, 1)
        self.n += 1

    def keys(self, h):
        v, peer = self.v, self.peer
        score = [peer.score[:, 2 * h + p, :] for p in range(2)]
        for lo in (0, 8):
            best = [peer.best[:, h, p, lo:lo + 8] for p in range(2)]
            besti = [peer.besti[:, h, p, lo:lo + 8] for p in range(2)]
            self.wait_round_before()
            if h == 0 and lo == 0:
                v.wait_ge(peer.score_loaded, 16 * self.tile + 16)
                apart(v, peer.dr["unwaited"])
            v.max(best[0], score[0])
            self.end_round(v.max(best[1], score[1]))
            yield
            self.wait_round_before()
            v.max_index(besti[0], best[0], score[0])
            self.end_round(v.max_index(besti[1], best[1], score[1]))
            yield
            if lo == 0:
                self.wait_round_before()
                v.match_replace(score[0], best[0], score[0], NEG)
                self.end_round(v.match_replace(score[1], best[1], score[1], NEG))
                yield

    def sums(self):
        peer = self.peer
        wide = [P, PH, TOPK, TOPK]
        self.wait_round_before()
        self.end_round(self.v.tensor_tensor(
            peer.cand, peer.best[:, :, 0, :].unsqueeze(3).to_broadcast(wide),
            peer.best[:, :, 1, :].unsqueeze(2).to_broadcast(wide), op=ALU.add))
        yield

    def pairs(self, h0):
        v, peer = self.v, self.peer
        cand = [peer.cand[:, h0 + i].rearrange("p a b -> p (a b)") for i in range(2)]
        for lo in (0, 8):
            top = [peer.top[:, h0 + i, lo:lo + 8] for i in range(2)]
            topi = [peer.topi[:, h0 + i, lo:lo + 8] for i in range(2)]
            self.wait_round_before()
            v.max(top[0], cand[0])
            self.end_round(v.max(top[1], cand[1]))
            yield
            self.wait_round_before()
            v.max_index(topi[0], top[0], cand[0])
            self.end_round(v.max_index(topi[1], top[1], cand[1]))
            yield
            if lo == 0:
                self.wait_round_before()
                v.match_replace(cand[0], top[0], cand[0], NEG)
                self.end_round(v.match_replace(cand[1], top[1], cand[1], NEG))
                yield

    def lookup(self, p):
        v, peer = self.v, self.peer
        wide = [P, PH, TOPK, TOPK]
        if p == 0:
            self.wait_round_before()
            v.tensor_scalar(peer.half[0][:], peer.topi[:], 4, None, ALU.logical_shift_right)
            v.tensor_scalar(peer.half[1][:], peer.topi[:], 15, None, ALU.bitwise_and)
            self.end_round(v.tensor_copy(peer.bestf[:], peer.besti[:]))
            yield
            self.wait_round_before()
            v.tensor_copy(peer.halff[0][:], peer.half[0][:])
            self.end_round(v.tensor_copy(peer.halff[1][:], peer.half[1][:]))
            yield
        self.wait_round_before()
        self.end_round(v.tensor_tensor(
            peer.cand, peer.halff[p][:].unsqueeze(3).to_broadcast(wide),
            peer.iota[:].unsqueeze(1).unsqueeze(1).to_broadcast(wide), op=ALU.is_equal))
        yield
        self.wait_round_before()
        self.end_round(v.tensor_tensor(
            peer.cand, peer.cand, peer.bestf[:, :, p, :].unsqueeze(2).to_broadcast(wide), op=ALU.mult))
        yield
        self.wait_round_before()
        self.end_round(v.reduce_sum(peer.part[p][:], peer.cand, axis=AX))
        yield

    def experts(self):
        v, peer = self.v, self.peer
        self.wait_round_before()
        if not isinstance(self.tile, int) or self.tile:
            v.wait_ge(peer.indexed, self.tile)
        self.end_round(v.scalar_tensor_tensor(
            out=peer.index_next[:].rearrange("p (h k) -> p h k", h=PH), in0=peer.part[0][:], scalar=float(NK),
            in1=peer.part[1][:], op0=ALU.mult, op1=ALU.add))
        yield

    def parts(self, parts):
        for what, *which in parts:
            if what == "keys":
                yield from self.keys(*which)
            elif what == "sums":
                yield from self.sums()
            elif what == "pairs":
                yield from self.pairs(*which)
            elif what == "lookup":
                yield from self.lookup(*which)
            else:
                yield from self.experts()


PARTS = [("keys", h) for h in range(PH)] + [("sums",)] + [("pairs", h) for h in range(0, PH, 2)] + \
    [("lookup", 0), ("lookup", 1), ("experts",), ("share",), ("total",)]
LATE = 3 * UNITS // 4
ROUNDS = {("sums",): 1, ("lookup", 0): 5, ("lookup", 1): 3, ("experts",): 1}
ROUNDS.update({part: 5 for part in PARTS if part[0] in ("keys", "pairs")})


def spread(first):
    at = {}
    for i, part in enumerate(PARTS):
        at.setdefault(first + i * (UNITS - 1 - first) // len(PARTS), []).append(part)
    return at


EARLY_PARTS, LATE_PARTS = spread(1), spread(LATE)


class Peer:

    KSTEP = sum(ROUNDS.values())
    SH = 4
    BLOCK = 4
    TKN = PH * TOPK
    HALVES = ((slice(0, NEW), slice(0, TKN // 2)), (slice(NEW, P), slice(TKN // 2, TKN)))

    def __init__(self, sem, dr, ph, n_tiles, late):
        self.dr, self.n_tiles, self.late = dr, n_tiles, late
        self.lng = ph.sb("lng", [P, D])
        self.lnb = ph.sb("lnb", [P, D])
        self.iota = ph.sb("iota", [P, TOPK])
        self.score = ph.sb("score", [P, 2 * PH, NK])
        assert 2 * PH * NK == PH * TOPK * TOPK
        self.cand = self.score[:].rearrange("p a n -> p (a n)").rearrange("p (h a b) -> p h a b", h=PH, a=TOPK)
        self.best = ph.sb("best", [P, PH, 2, TOPK])
        self.besti = ph.sb("besti", [P, PH, 2, TOPK], U32)
        self.bestf = ph.sb("bestf", [P, PH, 2, TOPK])
        self.top = ph.sb("top", [P, PH, TOPK])
        self.topi = ph.sb("topi", [P, PH, TOPK], U32)
        self.half = [ph.sb(f"half{i}", [P, PH, TOPK], U32) for i in range(2)]
        self.halff = [ph.sb(f"halff{i}", [P, PH, TOPK]) for i in range(2)]
        self.part = [ph.sb(f"part{i}", [P, PH, TOPK]) for i in range(2)]
        self.index_next = ph.sb("index_next", [P, self.TKN], U32)
        self.index = ph.sb("index", [P, self.TKN], U32)
        self.staged = [ph.sb(f"staged{i}", [P, ROWS], U32) for i in range(self.BLOCK)]
        self.share_next = ph.sb("share_next", [P, PH, TOPK])
        self.share = ph.sb("share", [P, self.TKN])
        self.total = ph.sb("total", [P, PH])
        self.x1 = ph.sb("x1", [P, D])
        self.y = ph.sb("y", [P, D])
        self.out = ph.sb("out", [P, D])
        self.hid = ph.sb("hid", [P, self.TKN])
        self.coef = ph.sb("coef", [P, self.TKN])
        self.urow = [ph.sb(f"urow{i}", [P, D]) for i in range(2 * ROWS)]
        self.vrow = [ph.sb(f"vrow{i}", [P, D]) for i in range(2 * ROWS)]
        self.stats = ph.sb("stats", [P, 12])
        self.mean = ph.sb("mean", [P, 2])
        self.std = ph.sb("std", [P, 2])
        self.tile_ready = sem("tile_ready")
        self.const_loaded = sem("const_loaded")
        self.score_loaded, self.x1_loaded = sem("score_loaded"), sem("x1_loaded")
        self.u_loaded = [sem(f"u_loaded{i}") for i in range(2 * ROWS)]
        self.v_loaded = [sem(f"v_loaded{i}") for i in range(2 * ROWS)]
        self.dotted = sem("dotted")
        self.added = sem("added")
        self.gelued = sem("gelued")
        self.weighted = sem("weighted")
        self.picked = sem("picked")
        self.exped = sem("exped")
        self.y_set = sem("y_set")
        self.shared = sem("shared")
        self.indexed = sem("indexed")
        self.staging = sem("staging")
        self.y_stored = sem("y_stored")
        self.halved = sem("halved")
        self.brought = sem("brought")
        self.folded = sem("folded")
        self.out_free = sem("out_free")
        self.dve = Steps(sem("ln_dve"), layer_norm_steps(""))
        self.acts = Steps(sem("ln_act"), ["root"])
        self.pick, self.rounds, self.rounds_left = None, None, 0
        self.v_at = self.a_at = -len(PARTS)

    def units_of(self, n):
        return UNITS // 2 if isinstance(n, int) and n == self.n_tiles - 1 else UNITS

    def gather(self, block):
        dr, last = self.dr, self.n_tiles - 1

        def load_score(pool, n):
            src = dr["scores"][n] if isinstance(n, int) else \
                dr["scores"][bass.ds(n, 1)].rearrange("a p n -> p (a n)")
            pool.wait_ge(self.tile_ready, n + 1)
            apart(pool, dr["unwaited"])
            pool.dma_start(self.score[:].rearrange("p a n -> p (a n)"), src).then_inc(self.score_loaded, 16)

        def fetch(pool, rows, k, loaded, table, slot):
            b = slot % 2 * ROWS + k
            pool.indirect_dma_start(
                out=rows[b][:], out_offset=None, in_=dr[table],
                in_offset=bass.IndirectOffsetOnAxis(ap=self.staged[slot][:, k:k + 1], axis=0)
            ).then_inc(loaded[b], 16)

        def fetch_v(pool, m, k, slot):
            pool.wait_ge(self.added, ROWS * m + k + 1)
            apart(pool, dr["unwaited"])
            fetch(pool, self.vrow, k, self.v_loaded, "peer_v", slot)

        def units(pool, n, i, first=False):
            for s in range(self.BLOCK):
                m = n * UNITS + i * self.BLOCK + s
                pool.tensor_copy(self.staged[s][:], self.index[:, bass.ds((i * self.BLOCK + s) * ROWS, ROWS)])\
                    .then_inc(self.staging, 1)
                pool.wait_ge(self.staging, m + 1)
                for k in range(ROWS):
                    pool.wait_ge(self.dotted, ROWS * m + k + 1)
                    apart(pool, dr["unwaited"])
                    fetch(pool, self.urow, k, self.u_loaded, "peer_u", s)
                    if s or not first:
                        fetch_v(pool, m, k, (s - 1) % self.BLOCK)

        def tile(pool, n, late=False):
            following = not isinstance(n, int) or n < last
            blocks, half = self.units_of(n) // self.BLOCK, LATE // self.BLOCK
            pool.wait_ge(self.picked, self.KSTEP * n + self.KSTEP)
            apart(pool, dr["unwaited"])
            if not following:
                pool.wait_ge(self.halved, 1)
            pool.tensor_copy(self.index[:], self.index_next[:]).then_inc(self.indexed, 1)
            pool.wait_ge(self.indexed, n + 1)
            apart(pool, dr["unwaited"])
            if following and not late:
                load_score(pool, n + 1)
            start = 0
            if isinstance(n, int) and n == 0:
                units(pool, 0, 0, first=True)
                start = 1
            if late:
                with pool.Fori(start, half) as i:
                    units(pool, n, i)
                load_score(pool, n + 1)
                start = half
            with pool.Fori(start, blocks) as i:
                units(pool, n, i)

        @block.gpsimd
        def _(pool):
            for dst, src in ((self.lng[:], "ln2_g"), (self.lnb[:], "ln2_b"), (self.iota[:], "iota")):
                pool.dma_start(dst, dr[src]).then_inc(self.const_loaded, 16)
            load_score(pool, 0)
            n = 0
            for stop in sorted({0, last, *self.late}):
                if stop - n > 1:
                    with pool.Fori(n, stop) as i:
                        tile(pool, i)
                elif stop - n == 1:
                    tile(pool, n)
                tile(pool, stop, late=stop in self.late)
                n = stop + 1
            for k in range(ROWS):
                fetch_v(pool, last * UNITS + self.units_of(last), k, self.BLOCK - 1)

    def scalar_open(self, act, part):
        if part == 0:
            self.acts.open(act)
        elif PARTS[part][0] == "share":
            self.exp_shares(act, 0)
        elif PARTS[part][0] == "total":
            self.load_x1(act, 0)
            self.set_y(act, 0)

    def exp_shares(self, act, n):
        act.wait_ge(self.shared, self.SH * n + 2)
        act.activation(self.share_next[:], self.share_next[:], ACT.Exp).then_inc(self.exped, 1)

    def load_x1(self, act, n):
        src = self.dr["x1"][n] if isinstance(n, int) else self.dr["x1"][bass.ds(n, 1)].rearrange("a p n -> p (a n)")
        act.wait_ge(self.dotted, ROWS * UNITS * n + 2 * ROWS)
        act.dma_start(self.x1[:], src).then_inc(self.x1_loaded, 16)

    def set_y(self, act, n):
        act.wait_ge(self.x1_loaded, 16 * n + 16)
        self.dve.wait(act, n - 1, "norm")
        if self.units_of(n) == UNITS:
            act.activation(self.y[:], self.x1[:], ACT.Copy, scale=ALPHA).then_inc(self.y_set, 1)
        else:
            for (r, _), scale in zip(self.HALVES, (ALPHA, 0.0)):
                act.activation(self.y[r], self.x1[r], ACT.Copy, scale=scale).then_inc(self.y_set, 1)

    def scalar_unit(self, act, n, j, before, following):
        m = n * UNITS + j
        act.wait_ge(self.dotted, ROWS * m + 3 * ROWS)
        c = slice(ROWS * j, ROWS * (j + 1))
        act.activation(self.coef[:, c], self.hid[:, c], ACT.Gelu_apprx_tanh).then_inc(self.gelued, 1)
        if j == 0 and before:
            self.finish_tile(act, n - 1)
            self.store_tile(act, n - 1, n)
        if j == 2 and before:
            act.wait_ge(self.y_stored, 16 * n)
            act.sem_inc(self.out_free, 1)
        if following and ("share",) in following.get(j, []):
            self.exp_shares(act, n + 1)
        if j == UNITS - 1 and following:
            self.load_x1(act, n + 1)

    def finish_tile(self, act, n):
        self.dve.wait(act, n, "var")
        self.acts.done(act.activation(self.std[:, 1:2], self.std[:, 0:1], ACT.Sqrt), "root")

    def store_tile(self, act, n, next_tile):
        if next_tile is not None:
            self.set_y(act, next_tile)
        self.dve.wait(act, n, "out")
        dst = self.dr["y"][n] if isinstance(n, int) else self.dr["y"][bass.ds(n, 1)].rearrange("a p n -> p (a n)")
        act.dma_start(dst, self.out[:]).then_inc(self.y_stored, 16)

    def scalar_close(self, act):
        last = self.n_tiles - 1
        act.wait_ge(self.added, ROWS * UNITS * last + ROWS * (self.units_of(last) + 3))
        act.dma_start(self.out[0:NEW, :], self.y[NEW:P, :]).then_inc(self.brought, 16)
        self.finish_tile(act, self.n_tiles - 1)
        self.store_tile(act, self.n_tiles - 1, None)
        act.wait_ge(self.y_stored, 16 * self.n_tiles)

    def vector_open(self, v, part):
        if part == 0:
            v.wait_ge(self.const_loaded, 48)
            v.sem_inc(self.dotted, 2 * ROWS)
            v.sem_inc(self.added, 3 * ROWS)
            v.sem_inc(self.shared, 1)
            v.sem_inc(self.weighted, 1)
            v.sem_inc(self.out_free, 1)
            self.dve.open(v)
        if part == 0:
            self.pick = TopK(self, v, 0)
        if PARTS[part] in ROUNDS:
            for _ in self.pick.parts([PARTS[part]]):
                pass
        else:
            self.next_shares(v, 0, PARTS[part])
        if part == len(PARTS) - 1:
            self.softmax_take(v, 0)

    def next_shares(self, v, n, part):
        if part[0] == "share":
            assert self.pick.n == self.KSTEP
            self.softmax_start(v, n)
        else:
            self.softmax_end(v, n)

    def next_rounds(self, steps_left):
        for _ in range(-(-self.rounds_left // steps_left)):
            next(self.rounds)
            self.rounds_left -= 1

    def softmax_start(self, v, n):
        v.wait_ge(self.picked, self.KSTEP * n + self.KSTEP)
        v.wait_ge(self.shared, self.SH * n + 1)
        v.tensor_tensor(self.share_next[:], self.top[:], self.top[:, :, 0:1].to_broadcast([P, PH, TOPK]),
                        op=ALU.subtract).then_inc(self.shared, 1)

    def softmax_end(self, v, n):
        v.wait_ge(self.exped, n + 1)
        v.reduce_sum(self.total[:], self.share_next[:], axis=AX).then_inc(self.shared, 1)
        v.wait_ge(self.shared, self.SH * n + 3)
        v.reciprocal(self.total[:], self.total[:]).then_inc(self.shared, 1)

    def softmax_take(self, v, n):
        v.wait_ge(self.shared, self.SH * n + 4)
        v.wait_ge(self.weighted, UNITS * n + 1)
        if self.units_of(n) == UNITS:
            v.tensor_tensor(self.share[:].rearrange("p (h k) -> p h k", h=PH), self.share_next[:],
                            self.total[:].unsqueeze(2).to_broadcast([P, PH, TOPK]), op=ALU.mult).then_inc(self.shared, 1)
            v.wait_ge(self.shared, self.SH * n + 5)
            return
        for (r, _), h in zip(self.HALVES, (0, PH // 2)):
            v.tensor_tensor(self.share[r, 0:self.TKN // 2].rearrange("p (h k) -> p h k", k=TOPK),
                            self.share_next[r, h:h + PH // 2, :],
                            self.total[r, h:h + PH // 2].unsqueeze(2).to_broadcast([NEW, PH // 2, TOPK]),
                            op=ALU.mult).then_inc(self.shared, 1)
        v.wait_ge(self.shared, self.SH * n + 6)

    def dot(self, v, n, j, k):
        b = j % 2 * ROWS + k
        v.wait_ge(self.u_loaded[b], 16 * (UNITS // 2) * n + 16 * (j // 2 + 1))
        if j == 0 and k == 0:
            v.wait_ge(self.x1_loaded, 16 * n + 16)
        col = ROWS * j + k
        v.scalar_tensor_tensor(out=self.urow[b][:], in0=self.urow[b][:], scalar=1.0, in1=self.x1[:], op0=ALU.mult,
                               op1=ALU.mult, accum_out=self.hid[:, col:col + 1]).then_inc(self.dotted, 1)

    def weigh(self, v, n, j):
        v.wait_ge(self.gelued, UNITS * n + j + 1)
        c = slice(ROWS * j, ROWS * (j + 1))
        v.tensor_tensor(self.coef[:, c], self.coef[:, c], self.share[:, c], op=ALU.mult).then_inc(self.weighted, 1)

    def add(self, v, n, j, k):
        b = j % 2 * ROWS + k
        v.wait_ge(self.v_loaded[b], 16 * (UNITS // 2) * n + 16 * (j // 2 + 1))
        if j == 0 and k == 0:
            v.wait_ge(self.y_set, n + 1 if self.units_of(n) == UNITS else n + 2)
        if k == 0:
            v.wait_ge(self.weighted, UNITS * n + j + 2)
        v.wait_ge(self.added, ROWS * UNITS * n + ROWS * (j + 3) + k)
        col = ROWS * j + k
        v.scalar_tensor_tensor(out=self.y[:], in0=self.vrow[b][:], scalar=self.coef[:, col:col + 1], in1=self.y[:],
                               op0=ALU.mult, op1=ALU.add).then_inc(self.added, 1)

    def norm(self, v, n):
        v.wait_ge(self.added, ROWS * UNITS * n + ROWS * (self.units_of(n) + 3))
        if self.units_of(n) == UNITS:
            v.wait_ge(self.out_free, n + 1)
        else:
            v.wait_ge(self.brought, 16)
            v.tensor_tensor(self.y[0:NEW], self.y[0:NEW], self.out[0:NEW], op=ALU.add).then_inc(self.folded, 1)
            v.wait_ge(self.folded, 1)
        layer_norm(v, self.dve, self.acts, n, "", self.y[:], self.out[:], self.stats, self.mean, self.std,
                   self.lng, self.lnb, self.dr["unwaited"])

    def vector_step(self, v, n, j, k, before, following):
        pn, pj = (n, j - 1) if j else (n - 1, UNITS - 1)
        adding = j or before
        parts = (following or {}).get(j, [])
        if adding and k == 0:
            self.weigh(v, pn, pj)
        if k == 0:
            if following and j == 0:
                self.pick = TopK(self, v, n + 1)
            picks = [part for part in parts if part in ROUNDS]
            self.rounds = self.pick.parts(picks)
            self.rounds_left = sum(ROUNDS[part] for part in picks)
        self.dot(v, n, j, k)
        self.next_rounds(2 * (ROWS - k))
        if adding:
            self.add(v, pn, pj, k)
        self.next_rounds(2 * (ROWS - k) - 1)
        if k < ROWS - 1:
            return
        if j == 0 and before:
            self.softmax_take(v, n)
            self.norm(v, n - 1)
        for part in parts:
            if part not in ROUNDS:
                self.next_shares(v, n + 1, part)

    def vector_close(self, v):
        n = self.n_tiles - 1
        self.weigh(v, n, self.units_of(n) - 1)
        for k in range(ROWS):
            self.add(v, n, self.units_of(n) - 1, k)
        self.norm(v, n)

    def parts(self, n):
        if n == self.n_tiles - 1:
            return None
        return LATE_PARTS if n in self.late else EARLY_PARTS

    def vector(self, v, steps, limit):
        for at in range(self.v_at, max(self.v_at, min(self.v_at + steps, limit))):
            n, row = divmod(at, UNITS * ROWS)
            if at < 0:
                self.vector_open(v, at + len(PARTS))
            else:
                self.vector_step(v, n, row // ROWS, row % ROWS, n > 0, self.parts(n))
            self.v_at = at + 1

    def scalar(self, act, steps, limit):
        for at in range(self.a_at, max(self.a_at, min(self.a_at + steps, limit))):
            n, row = divmod(at, UNITS * ROWS)
            if at < 0:
                self.scalar_open(act, at + len(PARTS))
            elif row % ROWS == ROWS - 1:
                self.scalar_unit(act, n, row // ROWS, n > 0, self.parts(n))
            self.a_at = at + 1

    def rest(self, block):
        per_tile = UNITS * ROWS
        last = self.n_tiles - 1

        @block.scalar
        def _(act):
            n0 = -(-self.a_at // per_tile)
            assert max(self.late) < n0 < last
            self.scalar(act, per_tile, n0 * per_tile)
            with act.Fori(n0, last) as n:
                for j in range(UNITS):
                    self.scalar_unit(act, n, j, True, EARLY_PARTS)
            for j in range(self.units_of(last)):
                self.scalar_unit(act, last, j, True, None)
            self.scalar_close(act)

        @block.vector
        def _(v):
            n0 = -(-self.v_at // per_tile)
            self.vector(v, per_tile, n0 * per_tile)
            with v.Fori(n0, last) as n:
                for j in range(UNITS):
                    for k in range(ROWS):
                        self.vector_step(v, n, j, k, True, EARLY_PARTS)
            rows, second = self.HALVES[1]
            v.wait_ge(self.picked, self.KSTEP * self.n_tiles)
            v.tensor_copy(self.index_next[rows, 0:self.TKN // 2], self.index_next[rows, second]).then_inc(self.halved, 1)
            for j in range(self.units_of(last)):
                for k in range(ROWS):
                    self.vector_step(v, last, j, k, True, None)
            self.vector_close(v)


GROUPS = (
    dict(tiles=2, shares=None),
    dict(tiles=3, shares=dict(project=69, local=27, prompt=42, sum=56, mix=18, route=31)),
    dict(tiles=4, shares=dict(project=83, local=32, prompt=44, sample=82, sum=82, mix=25, route=48)),
)
assert sum(g["tiles"] for g in GROUPS) == TT


def build(nc, dr):
    with nc.semaphore("unwaited") as unwaited:
        dr["unwaited"] = unwaited

        def scratch(name, *shape):
            dr[name] = nc.dram_tensor(f"scratch_{name}", shape, F32, kind="Internal").ap()

        scratch("uT", GG, P, TPAD)
        scratch("qmT", MH, P, TPAD)
        scratch("qT", HEADS, P, TPAD)
        scratch("gv", TT, P, 512)
        scratch("gT", GG, P, TPAD)
        scratch("mT", MH, P, TPAD)
        scratch("sbT", HEADS, P, TPAD)
        scratch("x1", TT, P, D)
        scratch("scores", TT, P, 2 * PH * NK)

        def sem_of(own, stage, made):
            def sem(label):
                made.append(own.enter_context(nc.semaphore(f"{stage}_{label}")))
                return made[-1]
            return sem

        def front(block, made, gate, own, bg, g, tile0, tiles):
            def sem(stage):
                return sem_of(own, f"g{g}_{stage}", made)

            prompt_tiles = min(tiles, PT - tile0)
            project(nc, block, sem("project"), dr, bg, g, tile0, tiles)
            gate.close(block)
            local_branches(nc, block, sem("local"), dr, bg, g, tile0, tiles)
            gate.close(block)
            attend_prompt(nc, block, sem("prompt"), dr, bg, g, tile0, prompt_tiles)
            gate.close(block)
            if prompt_tiles < tiles:
                attend_sample(nc, block, sem("sample"), dr, bg)
                gate.close(block)
            merge(nc, block, sem("merge"), gate, dr, bg, g, tile0, tiles)

        ph, lasting = Phase(nc, "peer"), []
        with ph.ctx, ExitStack() as own:
            starts = [sum(x["tiles"] for x in GROUPS[:g]) for g in range(len(GROUPS) + 1)]
            with nc.Block() as block:
                peer = Peer(sem_of(own, "peer", lasting), dr, ph, TT, late=[s - 1 for s in starts[1:-1]])
                peer.gather(block)
                gate = Gate(sem_of(own, "gate", lasting)("passed"))
                for g, group in enumerate(GROUPS):
                    bg = NoBackground() if g == 0 else \
                        Background(peer, group["shares"], ((starts[g] - 1) * UNITS + LATE) * ROWS)
                    with ExitStack() as front_own:
                        made = []
                        front(block, made, gate, front_own, bg, g, starts[g], group["tiles"])

                        @block.sync
                        def _(sp):
                            sp.sem_inc(peer.tile_ready, group["tiles"])
                            for s in made:
                                sp.sem_clear(s)

                        gate.close(block)
                peer.rest(block)


def kernel(**inputs):
    import concourse.bacc as bacc
    from concourse.bass_utils import run_bass_kernel_spmd

    a = {k: np.asarray(v) for k, v in inputs.items()}

    def pad_tokens():
        x = np.zeros((TPAD, D), np.float32)
        x[0:SEQ] = a["x_prompt"][0]
        x[SEQ:SEQ + NEW] = x[SEQ + NEW:] = a["x_sample"].reshape(NEW, D)
        return x

    def feature_major(x):
        return x.T.reshape(-1, P, x.shape[0]).transpose(1, 0, 2)

    def units(w, width=UW):
        return w.reshape(w.shape[0] // P, P, w.shape[1] // width, width).transpose(2, 1, 0, 3)

    def rows(x, n=P):
        return np.broadcast_to(x, (n, x.size))

    x = pad_tokens()
    w = a["w_in"][0]
    u, gv, q, k, v, qm, gates = np.split(w, np.cumsum([512, 512, 1024, 1024, 1024, 512]), axis=1)
    spatial = a["w_spatial"][0].transpose(2, 0, 1)
    spatial_new = np.zeros((P, GG, P), np.float32)
    bias_new = np.zeros((GG, P), np.float32)
    for s in range(P // NQ):
        at = slice(s * NQ, (s + 1) * NQ)
        spatial_new[at, :, at] = spatial[0:NQ, :, 0:NQ]
        bias_new[:, at] = a["b_spatial"][0][:, 0:NQ]
    sel = np.zeros((HEADS * NQ, HEADS, HEADS * NQ), np.float32)
    for r in range(HEADS * NQ):
        sel[r, r // NQ, r] = 1.0
    n_phys = a["cache_sb_k"].shape[1]
    at_query = np.arange(HEADS * NQ) % NQ
    ins = {
        "x": x.reshape(TT, P, D),
        "xT": feature_major(x),
        "memT": feature_major(a["mem_prompt"][0]),
        "w_in": units(np.concatenate([u, qm, q, k, gv, v], axis=1)),
        "w_gate": units(gates, GATE_W),
        "w_mem": units(a["w_mem_kv"][0]),
        "w_br0": units(a["w_br_gmlp"][0], GATE_W),
        "w_br1": units(a["w_br_sb"][0], GATE_W),
        "w_br2": units(a["w_br_mem"][0], GATE_W),
        "w_out": units(a["w_out"][0]),
        "w_q": units(a["peer_wq"][0], GATE_W),
        "b_gate": a["b_gate"][0].reshape(24, P).T,
        "gln_g": rows(a["gmlp_ln_g"][0]),
        "gln_b": rows(a["gmlp_ln_b"][0]),
        "w_spatial": np.stack([spatial, spatial_new], axis=1),
        "b_spatial": np.stack([a["b_spatial"][0], bias_new])[None],
        "sb_bias": rows(a["sb_bias"][0]),
        "sb_bias_rows": np.repeat(a["sb_bias"][0], NQ)[:, None],
        "ln1_g": rows(a["ln1_g"][0]),
        "ln1_b": rows(a["ln1_b"][0]),
        "ln2_g": rows(a["ln2_g"][0]),
        "ln2_b": rows(a["ln2_b"][0]),
        "keysT": a["peer_subkeys"][0].reshape(2 * PH, NK, P).transpose(2, 0, 1),
        "peer_u": a["peer_u"][0],
        "peer_v": a["peer_v"][0],
        "cache_k": a["cache_sb_k"][0].transpose(0, 3, 2, 1).reshape(n_phys, P, HEADS * P),
        "cache_v": a["cache_sb_v"][0].reshape(n_phys, P, HEADS * P),
        "mem_k": a["cache_mem_k"][0].transpose(0, 3, 2, 1),
        "mem_v": a["cache_mem_v"][0].reshape(NSEQ, 2, P, 512).transpose(0, 2, 1, 3),
        "table": a["page_table"].reshape(1, -1).astype(np.int32),
        "ident": np.eye(P, dtype=np.float32),
        "ones": np.ones((1, P), np.float32),
        "tril": np.triu(np.ones((P, P), np.float32)),
        "neg": np.where(np.arange(P)[None] >= np.arange(P)[:, None], NEG, 0.0).astype(np.float32),
        "neg_new": np.where(np.arange(NQ)[None] >= at_query[:, None], NEG, 0.0).astype(np.float32),
        "sel": sel,
        "selm": sel[0:MH * NQ, 0:MH, 0:MH * NQ],
        "iota": rows(np.arange(TOPK, dtype=np.float32)),
    }
    outs = {
        "kT": (HEADS, P, TPAD), "v": (TT, P, HEADS * P), "mkT": (MH, P, NMEM), "mv": (2, P, 512),
        "gv_sample": (NEW, 512), "y": (TT, P, D),
    }
    nc = bacc.Bacc("TRN2", target_bir_lowering=False, num_devices=1)
    arrays, dr = {}, {}
    for name, value in ins.items():
        arrays[f"in_{name}"] = np.ascontiguousarray(value)
        dr[name] = nc.dram_tensor(f"in_{name}", value.shape, mybir.dt.from_np(value.dtype), kind="ExternalInput").ap()
    for name, shape in outs.items():
        dr[name] = nc.dram_tensor(f"out_{name}", shape, F32, kind="ExternalOutput").ap()
    build(nc, dr)
    res = run_bass_kernel_spmd(nc, [arrays], core_ids=[0]).results[0]
    got = {name: np.asarray(res[f"out_{name}"]) for name in outs}
    y = got["y"].reshape(TPAD, D)
    k = got["kT"].reshape(HEADS * P, TPAD).T
    v = got["v"].reshape(TPAD, HEADS * P)
    new = slice(SEQ, SEQ + NEW)
    return (y[0:SEQ].reshape(1, SEQ, D), y[new].reshape(NSEQ, NQ, D),
            k[0:SEQ].reshape(1, 1, SEQ, HEADS, P), v[0:SEQ].reshape(1, 1, SEQ, HEADS, P),
            got["mkT"].reshape(MH * P, NMEM).T.reshape(1, 1, NMEM, MH, P), got["mv"].reshape(1, 1, NMEM, MH, P),
            k[new].reshape(1, NSEQ, NQ, HEADS, P), v[new].reshape(1, NSEQ, NQ, HEADS, P),
            got["gv_sample"].reshape(1, NSEQ, NQ, GG, P))
```
